# Optimizing a Trainium2 kernel written in Bass

```python
import math
import jax
import jax.numpy as jnp
from jax import lax
import numpy as np

D_MODEL = 1024
BATCH = 1
SEQ = 512
DEPTH = 1

EPS = 1e-6
NEG_INF = -1e30
DN_HEADS = 4
DN_DK = 128
DN_DV = 128
DN_KEY_W = DN_HEADS * DN_DK
DN_VAL_W = DN_HEADS * DN_DV
DN_CONV = 4
DN_CHUNK = 64
N_DIR = 2
DA_GROUPS = ((128, 1), (512, 4), (2048, 16))
DA_HEADS = 4
DA_HD = 128
DA_W = len(DA_GROUPS) * DA_HEADS * DA_HD
RP_BUCKETS = 32
RP_MAX_DIST = 1024
PEER_HEADS = 8
PEER_NKEYS = 128
PEER_QDIM = 256
PEER_TOPK = 16
PEER_EXPERTS = PEER_NKEYS * PEER_NKEYS
PEER_TOKEN_BLOCK = 128

IN_WIDTHS = (DN_KEY_W, DN_KEY_W, DN_VAL_W, DN_VAL_W, N_DIR * DN_HEADS, N_DIR * DN_HEADS,
             DA_W, DA_W, DA_W, D_MODEL, D_MODEL)


def rmsnorm(x, g):
    xf = x.astype(jnp.float32)
    y = xf * lax.rsqrt(jnp.mean(xf * xf, axis=-1, keepdims=True) + EPS)
    return (y * g.astype(jnp.float32)).astype(x.dtype)

def l2norm(x):
    return x * lax.rsqrt(jnp.sum(x * x, axis=-1, keepdims=True) + EPS)

def split_columns(t, widths):
    out, start = [], 0
    for w in widths:
        out.append(t[..., start:start + w])
        start += w
    return out

def centred_depthwise_conv(x, w):
    k, c = w.shape
    left = k // 2
    return lax.conv_general_dilated(x, w[:, None, :], window_strides=(1,), padding=[(left, k - 1 - left)],
                                    dimension_numbers=('NWC', 'WIO', 'NWC'), feature_group_count=c)

def gated_delta_rule(q, k, v, g, beta):
    r, s, dk = q.shape
    dv = v.shape[-1]
    c = DN_CHUNK
    n = s // c
    q = (q * (dk ** -0.5)).reshape(r, n, c, dk)
    k = k.reshape(r, n, c, dk)
    v = v.reshape(r, n, c, dv)
    beta = beta.reshape(r, n, c)
    gcum = jnp.cumsum(g.reshape(r, n, c), axis=-1)
    diff = gcum[..., :, None] - gcum[..., None, :]
    lower = jnp.tril(jnp.ones((c, c), dtype=bool))
    strict = jnp.tril(jnp.ones((c, c), dtype=bool), -1)
    decay = jnp.where(lower, jnp.exp(jnp.where(lower, diff, 0.0)), 0.0)
    kb = k * beta[..., None]
    lmat = jnp.where(strict, jnp.einsum('rnid,rnjd->rnij', kb, k) * decay, 0.0)
    amat = jnp.eye(c, dtype=jnp.float32) + lmat
    rhs = jnp.concatenate([v * beta[..., None], kb * jnp.exp(gcum)[..., None]], axis=-1)
    sol = lax.linalg.triangular_solve(amat, rhs, left_side=True, lower=True, unit_diagonal=True)
    u, w = sol[..., :dv], sol[..., dv:]
    intra = jnp.einsum('rnid,rnjd->rnij', q, k) * decay
    q_dec = q * jnp.exp(gcum)[..., None]
    k_dec = k * jnp.exp(gcum[..., -1:] - gcum)[..., None]
    g_last = jnp.exp(gcum[..., -1])

    def step(state, inp):
        u_i, w_i, intra_i, qd_i, kd_i, gl_i = inp
        v_new = u_i - jnp.einsum('rcd,rde->rce', w_i, state)
        out = jnp.einsum('rcd,rde->rce', qd_i, state) + jnp.einsum('rij,rje->rie', intra_i, v_new)
        state = state * gl_i[:, None, None] + jnp.einsum('rcd,rce->rde', kd_i, v_new)
        return state, out

    xs = tuple(jnp.moveaxis(a, 1, 0) for a in (u, w, intra, q_dec, k_dec, g_last))
    _, out = lax.scan(step, jnp.zeros((r, dk, dv), jnp.float32), xs)
    return jnp.moveaxis(out, 0, 1).reshape(r, s, dv)

def deltanet_branch(q, k, v, z, a, b, conv_w, a_log, dt_bias, out_norm):
    bsz, s, _ = q.shape
    f32 = jnp.float32
    qkv = jax.nn.silu(centred_depthwise_conv(jnp.concatenate([q, k, v], axis=-1), conv_w))
    q, k, v = split_columns(qkv, (DN_KEY_W, DN_KEY_W, DN_VAL_W))

    def heads(t, d):
        return t.reshape(bsz, s, DN_HEADS, d).transpose(0, 2, 1, 3).astype(f32)

    def per_dir(t):
        return t.reshape(bsz, s, N_DIR, DN_HEADS).transpose(2, 0, 3, 1).astype(f32)

    q, k, v = l2norm(heads(q, DN_DK)), l2norm(heads(k, DN_DK)), heads(v, DN_DV)
    g = -jnp.exp(a_log.astype(f32))[:, None, :, None] * jax.nn.softplus(per_dir(a) + dt_bias.astype(f32)[:, None, :, None])
    beta = jax.nn.sigmoid(per_dir(b))
    qs = jnp.stack([q, jnp.flip(q, 2)])
    ks = jnp.stack([k, jnp.flip(k, 2)])
    vs = jnp.stack([v, jnp.flip(v, 2)])
    gs = jnp.stack([g[0], jnp.flip(g[1], -1)])
    bs = jnp.stack([beta[0], jnp.flip(beta[1], -1)])
    rows = N_DIR * bsz * DN_HEADS
    o = gated_delta_rule(qs.reshape(rows, s, DN_DK), ks.reshape(rows, s, DN_DK), vs.reshape(rows, s, DN_DV),
                         gs.reshape(rows, s), bs.reshape(rows, s)).reshape(N_DIR, bsz, DN_HEADS, s, DN_DV)
    o = (o[0] + jnp.flip(o[1], 2)).transpose(0, 2, 1, 3)
    o = rmsnorm(o, out_norm) * jax.nn.silu(z.reshape(bsz, s, DN_HEADS, DN_DV).astype(f32))
    return o.reshape(bsz, s, DN_VAL_W)

def t5_bucket(rel):
    half = RP_BUCKETS // 2
    max_exact = half // 2
    n = np.abs(rel)
    large = max_exact + (np.log(np.maximum(n, 1) / max_exact) / math.log(RP_MAX_DIST / max_exact)
                         * (half - max_exact)).astype(np.int64)
    large = np.minimum(large, half - 1)
    return np.where(rel > 0, half, 0) + np.where(n < max_exact, n, large)

def dilated_group_attention(q, k, v, bias_table, window, dil):
    bsz, h, s, hd = q.shape
    side = window // (2 * dil)
    length = s // dil
    nb = -(-length // side)
    padded = nb * side

    def residue_blocks(t):
        t = t.reshape(bsz, h, length, dil, hd).transpose(0, 1, 3, 2, 4)
        t = jnp.pad(t, ((0, 0), (0, 0), (0, 0), (0, padded - length), (0, 0)))
        return t.reshape(bsz, h, dil, nb, side, hd)

    def with_neighbours(t):
        tp = jnp.pad(t, ((0, 0), (0, 0), (0, 0), (1, 1), (0, 0), (0, 0)))
        return jnp.concatenate([tp[:, :, :, :-2], tp[:, :, :, 1:-1], tp[:, :, :, 2:]], axis=4)

    qb = residue_blocks(q)
    kn = with_neighbours(residue_blocks(k))
    vn = with_neighbours(residue_blocks(v)).astype(jnp.float32)
    rel = np.arange(3 * side)[None, :] - side - np.arange(side)[:, None]
    key_idx = np.arange(nb)[:, None, None] * side + np.arange(3 * side)[None, None, :] - side
    valid = (np.abs(rel) <= side)[None] & (key_idx >= 0) & (key_idx < length)
    bias = bias_table.astype(jnp.float32)[:, t5_bucket(rel * dil)]
    scores = jnp.einsum('bhrnqd,bhrnkd->bhrnqk', qb, kn, preferred_element_type=jnp.float32) * (hd ** -0.5)
    scores = jnp.where(valid, scores + bias[None, :, None, None], NEG_INF)
    m = jnp.max(scores, axis=-1, keepdims=True)
    p = jnp.exp(scores - m)
    l = jnp.sum(p, axis=-1)
    o = jnp.einsum('bhrnqk,bhrnkd->bhrnqd', p, vn) / l[..., None]
    lse = m[..., 0] + jnp.log(l)
    o = o.reshape(bsz, h, dil, padded, hd)[:, :, :, :length].transpose(0, 1, 3, 2, 4).reshape(bsz, h, s, hd)
    lse = lse.reshape(bsz, h, dil, padded)[..., :length].transpose(0, 1, 3, 2).reshape(bsz, h, s)
    return o, lse

def dilated_attention_branch(q, k, v, rel_bias):
    bsz, s, _ = q.shape

    def groups(t):
        return t.reshape(bsz, s, len(DA_GROUPS), DA_HEADS, DA_HD).transpose(2, 0, 3, 1, 4)

    qg, kg, vg = groups(q), groups(k), groups(v)
    outs, lses = [], []
    for gi, (window, dil) in enumerate(DA_GROUPS):
        table = rel_bias[:, gi * DA_HEADS:(gi + 1) * DA_HEADS].T
        o, lse = dilated_group_attention(qg[gi], kg[gi], vg[gi], table, window, dil)
        outs.append(o)
        lses.append(lse)
    wts = jax.nn.softmax(jnp.stack(lses), axis=0)
    o = jnp.einsum('gbhs,gbhsd->bhsd', wts, jnp.stack(outs))
    return o.transpose(0, 2, 1, 3).reshape(bsz, s, DA_HEADS * DA_HD)

def peer_ffn(xn, w_q, sub_keys, expert_u, expert_v):
    bsz, s, d = xn.shape
    t = bsz * s
    x2 = xn.reshape(t, d)
    qh = (x2 @ w_q).reshape(t, PEER_HEADS, 2, PEER_QDIM // 2)
    scores = jnp.einsum('thcd,hckd->thck', qh, sub_keys, preferred_element_type=jnp.float32)
    sv, si = lax.top_k(scores, PEER_TOPK)
    cand = sv[..., 0, :, None] + sv[..., 1, None, :]
    cv, ci = lax.top_k(cand.reshape(t, PEER_HEADS, PEER_TOPK * PEER_TOPK), PEER_TOPK)
    i1 = jnp.take_along_axis(si[..., 0, :], ci // PEER_TOPK, axis=-1)
    i2 = jnp.take_along_axis(si[..., 1, :], ci % PEER_TOPK, axis=-1)
    experts = (i1 * PEER_NKEYS + i2).reshape(t, PEER_HEADS * PEER_TOPK)
    gates = jax.nn.softmax(cv, axis=-1).reshape(t, PEER_HEADS * PEER_TOPK)

    def token_block(args):
        xb, eb, gb = args
        act = jax.nn.gelu(jnp.einsum('tkd,td->tk', expert_u[eb], xb, preferred_element_type=jnp.float32))
        return jnp.einsum('tk,tkd->td', act * gb, expert_v[eb].astype(jnp.float32)).astype(xb.dtype)

    nblk = t // PEER_TOKEN_BLOCK
    out = lax.map(token_block, (x2.reshape(nblk, PEER_TOKEN_BLOCK, d),
                                experts.reshape(nblk, PEER_TOKEN_BLOCK, -1),
                                gates.reshape(nblk, PEER_TOKEN_BLOCK, -1)))
    return out.reshape(bsz, s, d)

def first_inputs(seed: int = 0) -> dict:
    key = jax.random.key(seed)
    ks = jax.random.split(key, 18)
    f32 = jnp.float32

    def normal(k, shape, scale):
        return jax.random.normal(k, shape, f32) * scale

    dt = jnp.exp(jax.random.uniform(ks[5], (DEPTH, N_DIR, DN_HEADS), f32, math.log(1e-3), math.log(1e-1)))
    return {
        'x': normal(ks[0], (BATCH, SEQ, D_MODEL), 1.0),
        'norm_mix': 1.0 + normal(ks[1], (DEPTH, D_MODEL), 0.02),
        'w_in': normal(ks[2], (DEPTH, D_MODEL, sum(IN_WIDTHS)), D_MODEL ** -0.5),
        'dn_conv': normal(ks[3], (DEPTH, DN_CONV, 2 * DN_KEY_W + DN_VAL_W), DN_CONV ** -0.5),
        'dn_a_log': jnp.log(jax.random.uniform(ks[4], (DEPTH, N_DIR, DN_HEADS), f32, 1.0, 16.0)),
        'dn_dt_bias': dt + jnp.log(-jnp.expm1(-dt)),
        'dn_out_norm': 1.0 + normal(ks[6], (DEPTH, DN_DV), 0.02),
        'rel_bias': normal(ks[7], (RP_BUCKETS, len(DA_GROUPS) * DA_HEADS), 0.2),
        'w_branch_dn': normal(ks[8], (DEPTH, DN_VAL_W, D_MODEL), DN_VAL_W ** -0.5),
        'w_branch_da': normal(ks[9], (DEPTH, DA_HEADS * DA_HD, D_MODEL), (DA_HEADS * DA_HD) ** -0.5),
        'w_out': normal(ks[10], (DEPTH, D_MODEL, D_MODEL), D_MODEL ** -0.5),
        'norm_ffn': 1.0 + normal(ks[11], (DEPTH, D_MODEL), 0.02),
        'peer_wq': normal(ks[12], (DEPTH, D_MODEL, PEER_HEADS * PEER_QDIM), D_MODEL ** -0.5),
        'peer_sub_keys': normal(ks[13], (DEPTH, PEER_HEADS, 2, PEER_NKEYS, PEER_QDIM // 2), (PEER_QDIM // 2) ** -0.5),
        'peer_u': normal(ks[14], (DEPTH, PEER_EXPERTS, D_MODEL), D_MODEL ** -0.5),
        'peer_v': normal(ks[15], (DEPTH, PEER_EXPERTS, D_MODEL), PEER_HEADS ** -0.5),
        'norm_final': 1.0 + normal(ks[16], (D_MODEL,), 0.02),
    }

def first_block(x, norm_mix, w_in, dn_conv, dn_a_log, dn_dt_bias, dn_out_norm, rel_bias, w_branch_dn,
              w_branch_da, w_out, norm_ffn, peer_wq, peer_sub_keys, peer_u, peer_v, norm_final):
    h = x
    for layer in range(DEPTH):
        xn = rmsnorm(h, norm_mix[layer])
        (dq, dk, dv, dz, da, db, aq, ak, av, gate_dn, gate_da) = split_columns(xn @ w_in[layer], IN_WIDTHS)
        o_dn = deltanet_branch(dq, dk, dv, dz, da, db, dn_conv[layer], dn_a_log[layer], dn_dt_bias[layer],
                               dn_out_norm[layer]).astype(h.dtype)
        o_da = dilated_attention_branch(aq, ak, av, rel_bias).astype(h.dtype)
        merged = (jax.nn.sigmoid(gate_dn) * (o_dn @ w_branch_dn[layer])
                  + jax.nn.sigmoid(gate_da) * (o_da @ w_branch_da[layer]))
        h = h + merged @ w_out[layer]
        h = h + peer_ffn(rmsnorm(h, norm_ffn[layer]), peer_wq[layer], peer_sub_keys[layer],
                         peer_u[layer], peer_v[layer])
    return rmsnorm(h, norm_final)


DEPTH_2 = 2

GRID_W = 64
CTX_LEN = 256
HEAD_DIM = 64
GLA_HEADS = 4
NA_HEADS = 6
SWA_HEADS = 6
SWA_KV_HEADS = 2
GLA_W = GLA_HEADS * HEAD_DIM
NA_W = NA_HEADS * HEAD_DIM
SWA_W = SWA_HEADS * HEAD_DIM
SWA_KV_W = SWA_KV_HEADS * HEAD_DIM
MIX_WIDTH = GLA_W + NA_W + SWA_W
GLA_RANK = 16
GLA_TAU = 16.0
GLA_CHUNK = 64
NA_KH = 8
NA_KW = 16
NA_QW = 16
NA_CB = NA_KW + NA_QW
SWA_WINDOW = 128
SWA_BLOCK = 128
ROPE_THETA = 10000.0
NORM_EPS = 1e-6
D_FF = -(-8 * D_MODEL // (3 * 256)) * 256
IN_SPLITS = (GLA_W, GLA_W, GLA_W, GLA_W, GLA_RANK, GLA_RANK, NA_W, NA_W, NA_W, SWA_W, SWA_KV_W, SWA_KV_W)
IN_WIDTH = sum(IN_SPLITS)


def rms_norm(x, g):
    xf = x.astype(jnp.float32)
    y = xf * lax.rsqrt(jnp.mean(xf * xf, axis=-1, keepdims=True) + NORM_EPS)
    return (y * g.astype(jnp.float32)).astype(x.dtype)

def split_cols(p):
    bounds = [int(b) for b in np.cumsum(IN_SPLITS)[:-1]]
    return jnp.split(p, bounds, axis=-1)

def split_heads(a, n_heads):
    return a.reshape(a.shape[:-1] + (n_heads, HEAD_DIM))

def axial_rope(n_tokens):
    t = jnp.arange(n_tokens, dtype=jnp.int32)
    row = (t // GRID_W).astype(jnp.float32)
    col = (t % GRID_W).astype(jnp.float32)
    n_freq = HEAD_DIM // 4
    inv_freq = ROPE_THETA ** (-jnp.arange(n_freq, dtype=jnp.float32) / n_freq)
    ang = jnp.concatenate([row[:, None] * inv_freq, col[:, None] * inv_freq], axis=-1)
    return jnp.cos(ang), jnp.sin(ang)

def apply_rope(a, cos, sin):
    half = HEAD_DIM // 2
    af = a.astype(jnp.float32)
    a1, a2 = af[..., :half], af[..., half:]
    cs = cos[None, :, None, :]
    sn = sin[None, :, None, :]
    return jnp.concatenate([a1 * cs - a2 * sn, a1 * sn + a2 * cs], axis=-1).astype(a.dtype)

def gla_heads(a):
    B, T, _ = a.shape
    return a.reshape(B, T, GLA_HEADS, HEAD_DIM).transpose(0, 2, 1, 3)

def gla_log_decay(z_low, w2, b2):
    z = (z_low @ w2 + b2).astype(jnp.float32)
    return gla_heads(jax.nn.log_sigmoid(z) / GLA_TAU)

def gla_chunked(q, k, v, log_a, s0):
    B, H, T, dk = q.shape
    dv = v.shape[-1]
    n = T // GLA_CHUNK

    def chunks(a):
        return a.astype(jnp.float32).reshape(B, H, n, GLA_CHUNK, a.shape[-1])

    qc, kc, vc, la = chunks(q), chunks(k), chunks(v), chunks(log_a)
    b = jnp.cumsum(la, axis=3)
    b_last = b[:, :, :, -1:, :]
    q_in = qc * jnp.exp(b)
    k_in = kc * jnp.exp(-b)
    k_end = kc * jnp.exp(b_last - b)
    lower = jnp.tril(jnp.ones((GLA_CHUNK, GLA_CHUNK), dtype=bool))
    a_intra = jnp.where(lower, jnp.einsum('bhncd,bhnsd->bhncs', q_in, k_in), 0.0)
    o_intra = jnp.einsum('bhncs,bhnse->bhnce', a_intra, vc)
    chunk_state = jnp.einsum('bhnsd,bhnse->bhnde', k_end, vc)
    chunk_decay = jnp.exp(b_last[:, :, :, 0, :])

    def step(state, inp):
        dec, cs = inp
        return dec[..., None] * state + cs, state

    s_final, s_enter = lax.scan(step, s0, (jnp.moveaxis(chunk_decay, 2, 0), jnp.moveaxis(chunk_state, 2, 0)))
    o_inter = jnp.einsum('bhncd,nbhde->bhnce', q_in, s_enter)
    o = (o_intra + o_inter).reshape(B, H, T, dv).astype(v.dtype)
    return o, s_final

def gla_final_state(k, v, log_a):
    A = jnp.cumsum(log_a.astype(jnp.float32), axis=2)
    w = jnp.exp(A[:, :, -1:, :] - A)
    return jnp.einsum('bhtd,bhte->bhde', k.astype(jnp.float32) * w, v.astype(jnp.float32))

def gla_output(o, g, norm_g):
    B, H, T, dv = o.shape
    o = rms_norm(o.transpose(0, 2, 1, 3), norm_g.reshape(H, dv))
    return o.reshape(B, T, H * dv) * jax.nn.silu(g)

def gla_mixer(parts, parts_c, wa2_f, ba_f, wa2_b, ba_b, norm_g, need_ctx_out):
    q, k, v, g, za_f, za_b = parts
    qc, kc, vc, gc, zac_f, zac_b = parts_c
    scale = HEAD_DIM ** -0.5

    def flip(a):
        return jnp.flip(a, axis=2)

    K_c, V_c = gla_heads(kc), gla_heads(vc)
    la_cf = gla_log_decay(zac_f, wa2_f, ba_f)
    la_cb = gla_log_decay(zac_b, wa2_b, ba_b)
    if need_ctx_out:
        Q_c = gla_heads(qc) * scale
        zeros = jnp.zeros(K_c.shape[:2] + (HEAD_DIM, HEAD_DIM), jnp.float32)
        oc_f, s_f = gla_chunked(Q_c, K_c, V_c, la_cf, zeros)
        oc_b, s_b = gla_chunked(flip(Q_c), flip(K_c), flip(V_c), flip(la_cb), zeros)
        yc = gla_output(oc_f + flip(oc_b), gc, norm_g)
    else:
        s_f = gla_final_state(K_c, V_c, la_cf)
        s_b = gla_final_state(flip(K_c), flip(V_c), flip(la_cb))
        yc = None
    Q, K, V = gla_heads(q) * scale, gla_heads(k), gla_heads(v)
    o_f, _ = gla_chunked(Q, K, V, gla_log_decay(za_f, wa2_f, ba_f), s_f)
    o_b, _ = gla_chunked(flip(Q), flip(K), flip(V), flip(gla_log_decay(za_b, wa2_b, ba_b)), s_b)
    y = gla_output(o_f + flip(o_b), g, norm_g)
    return y, yc

def context_attention(qc, kc, vc, sink):
    B, L, Hq, dh = qc.shape
    Hkv = kc.shape[2]
    G = Hq // Hkv
    s = jnp.einsum('bqhgd,bkhd->bhgqk', qc.reshape(B, L, Hkv, G, dh), kc).astype(jnp.float32) * dh ** -0.5
    if sink is None:
        p = jax.nn.softmax(s, axis=-1)
    else:
        s_sink = jnp.broadcast_to(sink.astype(jnp.float32).reshape(1, Hkv, G, 1, 1), s.shape[:-1] + (1,))
        p = jax.nn.softmax(jnp.concatenate([s, s_sink], axis=-1), axis=-1)[..., :-1]
    o = jnp.einsum('bhgqk,bkhd->bqhgd', p.astype(vc.dtype), vc)
    return o.reshape(B, L, Hq * dh)

def neighborhood_attention(q, k, v, kc, vc, rpb):
    B, T, H, dh = q.shape
    rows = T // GRID_W
    kh = min(NA_KH, rows)
    ncb = GRID_W // NA_QW
    r = np.arange(rows)
    row_idx = np.clip(r - kh // 2, 0, rows - kh)[:, None] + np.arange(kh)[None, :]
    q_cols = np.arange(GRID_W).reshape(ncb, NA_QW)
    win_start = np.clip(q_cols - NA_KW // 2, 0, GRID_W - NA_KW)
    col_idx = np.clip(np.arange(ncb) * NA_QW - NA_KW // 2, 0, GRID_W - NA_CB)[:, None] + np.arange(NA_CB)[None, :]
    key_col = col_idx[:, None, :]
    valid = (key_col >= win_start[:, :, None]) & (key_col < win_start[:, :, None] + NA_KW)
    dr = row_idx - r[:, None] + NA_KH - 1
    dc = np.clip(key_col - q_cols[:, :, None] + NA_KW - 1, 0, 2 * NA_KW - 2)
    bias = rpb.astype(jnp.float32)[:, dr[:, None, None, :, None], dc[None, :, :, None, :]]
    bias = jnp.where(valid[None, None, :, :, None, :], bias, -jnp.inf)

    q_blk = q.reshape(B, rows, ncb, NA_QW, H, dh)
    k_grid = k.reshape(B, rows, GRID_W, H, dh)
    v_grid = v.reshape(B, rows, GRID_W, H, dh)
    ri = row_idx[:, None, :, None]
    ci = col_idx[None, :, None, :]
    k_blk = k_grid[:, ri, ci]
    v_blk = v_grid[:, ri, ci]
    scale = dh ** -0.5
    s_loc = jnp.einsum('brnqhd,brnkchd->bhrnqkc', q_blk, k_blk).astype(jnp.float32) * scale + bias
    n_loc = kh * NA_CB
    s_loc = s_loc.reshape(s_loc.shape[:5] + (n_loc,))
    s_ctx = jnp.einsum('brnqhd,blhd->bhrnql', q_blk, kc).astype(jnp.float32) * scale
    p = jax.nn.softmax(jnp.concatenate([s_loc, s_ctx], axis=-1), axis=-1)
    p_loc = p[..., :n_loc].reshape(p.shape[:5] + (kh, NA_CB)).astype(v.dtype)
    p_ctx = p[..., n_loc:].astype(vc.dtype)
    o = (jnp.einsum('bhrnqkc,brnkchd->brnqhd', p_loc, v_blk)
         + jnp.einsum('bhrnql,blhd->brnqhd', p_ctx, vc))
    return o.reshape(B, T, H * dh)

def sliding_window_attention(q, k, v, kc, vc, sink):
    B, T, Hq, dh = q.shape
    Hkv = k.shape[2]
    G = Hq // Hkv
    bs = SWA_BLOCK
    nb = T // bs
    qb = q.reshape(B, nb, bs, Hkv, G, dh)
    pad = ((0, 0), (bs, bs), (0, 0), (0, 0))
    kp, vp = jnp.pad(k, pad), jnp.pad(v, pad)
    idx = np.arange(nb)[:, None] * bs + np.arange(3 * bs)[None, :]
    kb, vb = kp[:, idx], vp[:, idx]
    kpos = idx - bs
    qpos = np.arange(T).reshape(nb, bs)
    valid = ((np.abs(qpos[:, :, None] - kpos[:, None, :]) <= SWA_WINDOW)
             & (kpos[:, None, :] >= 0) & (kpos[:, None, :] < T))
    scale = dh ** -0.5
    s_loc = jnp.einsum('bnqhgd,bnkhd->bhgnqk', qb, kb).astype(jnp.float32) * scale
    s_loc = jnp.where(valid, s_loc, -jnp.inf)
    s_ctx = jnp.einsum('bnqhgd,blhd->bhgnql', qb, kc).astype(jnp.float32) * scale
    s_sink = jnp.broadcast_to(sink.astype(jnp.float32).reshape(1, Hkv, G, 1, 1, 1), s_loc.shape[:-1] + (1,))
    p = jax.nn.softmax(jnp.concatenate([s_loc, s_ctx, s_sink], axis=-1), axis=-1)
    n_loc = 3 * bs
    L = kc.shape[1]
    p_loc = p[..., :n_loc].astype(v.dtype)
    p_ctx = p[..., n_loc:n_loc + L].astype(vc.dtype)
    o = (jnp.einsum('bhgnqk,bnkhd->bnqhgd', p_loc, vb)
         + jnp.einsum('bhgnql,blhd->bnqhgd', p_ctx, vc))
    return o.reshape(B, T, Hq * dh)

def token_mixers(h, hc, w_in, w_out, wa2_f, ba_f, wa2_b, ba_b, gla_norm, na_rpb, swa_sink, cos, sin, need_ctx_out):
    p = split_cols(h @ w_in)
    pc = split_cols(hc @ w_in)
    y_gla, yc_gla = gla_mixer(p[0:6], pc[0:6], wa2_f, ba_f, wa2_b, ba_b, gla_norm, need_ctx_out)
    nq, nk, nv = (split_heads(a, NA_HEADS) for a in p[6:9])
    nkc, nvc = split_heads(pc[7], NA_HEADS), split_heads(pc[8], NA_HEADS)
    y_na = neighborhood_attention(nq, nk, nv, nkc, nvc, na_rpb)
    sq = apply_rope(split_heads(p[9], SWA_HEADS), cos, sin)
    sk = apply_rope(split_heads(p[10], SWA_KV_HEADS), cos, sin)
    sv = split_heads(p[11], SWA_KV_HEADS)
    skc, svc = split_heads(pc[10], SWA_KV_HEADS), split_heads(pc[11], SWA_KV_HEADS)
    y_swa = sliding_window_attention(sq, sk, sv, skc, svc, swa_sink)
    y = jnp.concatenate([y_gla, y_na, y_swa], axis=-1) @ w_out
    if not need_ctx_out:
        return y, None
    yc_na = context_attention(split_heads(pc[6], NA_HEADS), nkc, nvc, None)
    yc_swa = context_attention(split_heads(pc[9], SWA_HEADS), skc, svc, swa_sink)
    yc = jnp.concatenate([yc_gla, yc_na, yc_swa], axis=-1) @ w_out
    return y, yc

def swiglu(h, w_gate, w_up, w_down):
    return (jax.nn.silu(h @ w_gate) * (h @ w_up)) @ w_down

def second_inputs(seed: int = 0) -> dict:
    key = jax.random.key(seed)
    ks = jax.random.split(key, 24)
    f32 = jnp.float32
    D = D_MODEL

    def nrm(k, shape, s):
        return jax.random.normal(k, shape, f32) * s

    return {
        'x': nrm(ks[0], (BATCH, SEQ, D), 1.0),
        'c': nrm(ks[1], (BATCH, D), 1.0),
        'ctx': nrm(ks[2], (BATCH, CTX_LEN, D), 1.0),
        'c_ctx': nrm(ks[3], (D,), 1.0),
        'w_mod': nrm(ks[4], (DEPTH_2, D, 6 * D), 0.5 * D ** -0.5),
        'b_mod': nrm(ks[5], (DEPTH_2, 6 * D), 0.02),
        'norm_mix': 1.0 + nrm(ks[6], (DEPTH_2, D), 0.05),
        'norm_ffn': 1.0 + nrm(ks[7], (DEPTH_2, D), 0.05),
        'w_in': nrm(ks[8], (DEPTH_2, D, IN_WIDTH), D ** -0.5),
        'gla_wa2_f': nrm(ks[9], (DEPTH_2, GLA_RANK, GLA_W), GLA_RANK ** -0.5),
        'gla_ba_f': nrm(ks[10], (DEPTH_2, GLA_W), 0.5),
        'gla_wa2_b': nrm(ks[11], (DEPTH_2, GLA_RANK, GLA_W), GLA_RANK ** -0.5),
        'gla_ba_b': nrm(ks[12], (DEPTH_2, GLA_W), 0.5),
        'gla_norm': 1.0 + nrm(ks[13], (DEPTH_2, GLA_W), 0.05),
        'na_rpb': nrm(ks[14], (DEPTH_2, NA_HEADS, 2 * NA_KH - 1, 2 * NA_KW - 1), 0.1),
        'swa_sink': nrm(ks[15], (DEPTH_2, SWA_HEADS), 0.5),
        'w_out': nrm(ks[16], (DEPTH_2, MIX_WIDTH, D), MIX_WIDTH ** -0.5),
        'w_gate': nrm(ks[17], (DEPTH_2, D, D_FF), D ** -0.5),
        'w_up': nrm(ks[18], (DEPTH_2, D, D_FF), D ** -0.5),
        'w_down': nrm(ks[19], (DEPTH_2, D_FF, D), D_FF ** -0.5),
        'final_norm': 1.0 + nrm(ks[20], (D,), 0.05),
    }

def second_block(x, c, ctx, c_ctx, w_mod, b_mod, norm_mix, norm_ffn, w_in, gla_wa2_f, gla_ba_f, gla_wa2_b, gla_ba_b,
              gla_norm, na_rpb, swa_sink, w_out, w_gate, w_up, w_down, final_norm):
    T = x.shape[1]
    cos, sin = axial_rope(T)
    s_lat = jax.nn.silu(c)
    s_ctx = jax.nn.silu(c_ctx)
    xc = ctx
    for i in range(DEPTH_2):
        need_ctx_out = i < DEPTH_2 - 1
        mod = (s_lat @ w_mod[i] + b_mod[i])[:, None, :]
        mod_c = s_ctx @ w_mod[i] + b_mod[i]
        sh1, sc1, g1, sh2, sc2, g2 = jnp.split(mod, 6, axis=-1)
        sh1c, sc1c, g1c, sh2c, sc2c, g2c = jnp.split(mod_c, 6, axis=-1)
        h = rms_norm(x, norm_mix[i]) * (1.0 + sc1) + sh1
        hc = rms_norm(xc, norm_mix[i]) * (1.0 + sc1c) + sh1c
        y, yc = token_mixers(h, hc, w_in[i], w_out[i], gla_wa2_f[i], gla_ba_f[i], gla_wa2_b[i], gla_ba_b[i],
                             gla_norm[i], na_rpb[i], swa_sink[i], cos, sin, need_ctx_out)
        x = x + g1 * y
        h = rms_norm(x, norm_ffn[i]) * (1.0 + sc2) + sh2
        x = x + g2 * swiglu(h, w_gate[i], w_up[i], w_down[i])
        if need_ctx_out:
            xc = xc + g1c * yc
            hc = rms_norm(xc, norm_ffn[i]) * (1.0 + sc2c) + sh2c
            xc = xc + g2c * swiglu(hc, w_gate[i], w_up[i], w_down[i])
    return rms_norm(x, final_norm)


def setup_inputs(seed=0):
    out = dict(first_inputs(seed))
    for name, value in second_inputs(seed + 1).items():
        if name != "x":
            out[name + "_2"] = value
    return out


def reference(
    x, norm_mix, w_in, dn_conv, dn_a_log, dn_dt_bias, dn_out_norm, rel_bias, w_branch_dn,
    w_branch_da, w_out, norm_ffn, peer_wq, peer_sub_keys, peer_u, peer_v, norm_final, c_2,
    ctx_2, c_ctx_2, w_mod_2, b_mod_2, norm_mix_2, norm_ffn_2, w_in_2, gla_wa2_f_2, gla_ba_f_2,
    gla_wa2_b_2, gla_ba_b_2, gla_norm_2, na_rpb_2, swa_sink_2, w_out_2, w_gate_2, w_up_2,
    w_down_2, final_norm_2,
):
    x = first_block(
        x, norm_mix, w_in, dn_conv, dn_a_log, dn_dt_bias, dn_out_norm, rel_bias, w_branch_dn,
        w_branch_da, w_out, norm_ffn, peer_wq, peer_sub_keys, peer_u, peer_v, norm_final,
    )
    return second_block(
        x, c_2, ctx_2, c_ctx_2, w_mod_2, b_mod_2, norm_mix_2, norm_ffn_2, w_in_2, gla_wa2_f_2,
        gla_ba_f_2, gla_wa2_b_2, gla_ba_b_2, gla_norm_2, na_rpb_2, swa_sink_2, w_out_2,
        w_gate_2, w_up_2, w_down_2, final_norm_2,
    )


_drawn_inputs = setup_inputs


def setup_inputs(seed=0):
    import zlib

    import numpy as np

    out = dict(_drawn_inputs(seed))
    spreads = {}
    factors = {'dn_out_norm': 3.353,
     'rel_bias': 2.728,
     'norm_final': 2.684,
     'norm_mix_2': 3.917,
     'norm_ffn_2': 2.669,
     'gla_wa2_f_2': 2.932,
     'gla_wa2_b_2': 2.67,
     'gla_norm_2': 7.765,
     'na_rpb_2': 8.0,
     'swa_sink_2': 8.0}
    for name, (base, spread) in spreads.items():
        noise = np.random.default_rng([zlib.crc32(name.encode()), seed]).standard_normal(out[name].shape)
        drawn = base * np.exp(spread * noise) if base else spread * noise
        out[name] = jnp.asarray(drawn.astype(out[name].dtype))
    for name, factor in factors.items():
        out[name] = (out[name] * factor).astype(out[name].dtype)
    return out
```

```python
import numpy as np
import concourse.bass as bass
from concourse import mybir

F32 = mybir.dt.float32
F32R = mybir.dt.float32r
U8 = mybir.dt.uint8
U32 = mybir.dt.uint32
ALU = mybir.AluOpType
ACT = mybir.ActivationFunctionType
AX = mybir.AxisListType

T = 512
D = 1024
KC = 8
EPS = 1e-6
NEG = -1e30

IDENT, UF, UB, MASKF, MASKB = 0, 128, 256, 384, 512
G_MIX, G_FFN, G_FIN = 640, 648, 656
CONVW = 664
DTB, ALOG, ONORM = 712, 720, 728
IOTA = 736
BMOD, N2MIX, N2FFN, N2FIN = 864, 960, 976, 992
CVEC, GBA, GNORM, SINK = 1000, 1016, 1024, 1028
NCONST = 1040
COS, SIN, PERM, RSTF, RSTB, ONESBD, BMASK = 0, 512, 1024, 1152, 1664, 2176, 2304
NC2 = 2432
HALF = 11
LEVELS = (1, 2, 4, 8, 16, 32, 64)


class Op:
    __slots__ = ("eng", "fn", "after", "asked", "sem", "count")

    def __init__(self, eng, fn, after):
        self.eng, self.fn, self.after = eng, fn, after
        self.asked, self.sem, self.count = False, None, 0


def flat(x):
    if x is None:
        return []
    if isinstance(x, Op):
        return [x]
    out = []
    for y in x:
        out += flat(y)
    return out


class Plan:

    def __init__(self, nc):
        self.nc = nc
        self.queues = {e: [] for e in ("tensor", "vector", "scalar", "gpsimd", "sync")}
        self.dmas = []
        self.dma_counts = {}

    def op(self, eng, fn, after=()):
        o = Op(eng, fn, flat(after))
        for a in o.after:
            a.asked = True
        self.queues[eng].append(o)
        return o

    def dma(self, eng, out, in_, sem, after=()):
        o = self.op(eng, lambda e: e.dma_start(out, in_), after)
        n = self.dma_counts.get(sem, 0) + 16
        self.dma_counts[sem] = n
        o.sem, o.count = sem, n
        self.dmas.append(o)
        return o

    def emit(self, sem_of):
        for eng, queue in self.queues.items():
            n = 0
            for o in queue:
                if o.sem is None and o.asked:
                    n += 1
                    o.sem, o.count = eng, n
        with self.nc.Block() as block:
            for eng, queue in self.queues.items():
                getter = {"tensor": block.tensor, "vector": block.vector, "scalar": block.scalar,
                          "gpsimd": block.gpsimd, "sync": block.sync}[eng]
                getter(self.body(eng, queue, sem_of))

    def body(self, eng, queue, sem_of):
        def run(e):
            seen = {}
            for o in queue:
                need = {}
                for a in o.after:
                    need[a.sem] = max(need.get(a.sem, 0), a.count)
                for sem, count in need.items():
                    if seen.get(sem, 0) < count:
                        e.wait_ge(sem_of(sem), count)
                        seen[sem] = count
                ins = o.fn(e)
                if o.sem is not None:
                    ins.then_inc(sem_of(o.sem), 16 if o.sem != eng else 1)
            if eng == "sync":
                for sem, count in self.dma_counts.items():
                    if seen.get(sem, 0) < count:
                        e.wait_ge(sem_of(sem), count)
        return run


class Cell:

    def __init__(self, ap):
        self.ap, self.ready, self.free, self.held = ap, [], [], False

    def done(self, *readers):
        self.free, self.held = flat(readers), False


class Ring:
    def __init__(self, cells):
        self.cells, self.n = cells, 0

    def next(self):
        for _ in self.cells:
            c = self.cells[self.n % len(self.cells)]
            self.n += 1
            if not c.held:
                c.held = True
                return c
        raise AssertionError("every cell is in use")


def program(nc, io, until=None):
    P = Plan(nc)
    sems = {}

    def sem_of(name):
        if name not in sems:
            sems[name] = nc.alloc_semaphore("s_" + name)
        return sems[name]

    BASE = 16512

    def sb(name, kb, shape, dt=F32):
        return nc.alloc_sbuf_tensor_at(name, [128] + list(shape), dt, offset=BASE + int(kb * 1024))

    psum = nc.alloc_psum_tensor("ps", [128, 8, 512], F32)
    bank = [Cell(psum[:, i, :]) for i in range(8)]

    def mm(out, lhsT, rhs, start=True, stop=True, after=(), at=None):
        if at is None:
            return P.op("tensor", lambda e: e.matmul(out, lhsT, rhs, start=start, stop=stop), after)
        return P.op("tensor", lambda e: e.matmul(out, lhsT, rhs, start=start, stop=stop, tile_position=at), after)

    def tr(out, in_, idn, after=()):
        return P.op("tensor", lambda e: e.transpose(out, in_, idn), after)

    def act(out, in_, func, after=(), bias=0.0, scale=1.0, accum=None):
        if accum is None:
            return P.op("scalar", lambda e: e.activation(out, in_, func, bias=bias, scale=scale), after)
        return P.op("scalar", lambda e: e.activation(out, in_, func, bias=bias, scale=scale, accum_out=accum), after)

    def tt(out, a, b, op, after=(), eng="vector"):
        return P.op(eng, lambda e: e.tensor_tensor(out, a, b, op), after)

    def ts(out, a, s1, op0, after=(), s2=None, op1=None, eng="vector"):
        if op1 is None:
            return P.op(eng, lambda e: e.tensor_scalar(out, a, s1, None, op0), after)
        return P.op(eng, lambda e: e.tensor_scalar(out, a, s1, s2, op0, op1), after)

    def stt(out, a, s, b, op0, op1, after=()):
        return P.op("vector", lambda e: e.scalar_tensor_tensor(out, a, s, b, op0, op1), after)

    def copy(out, in_, after=(), eng="vector"):
        return P.op(eng, lambda e: e.tensor_copy(out, in_), after)

    def memset(ap, v, after=(), eng="gpsimd"):
        return P.op(eng, lambda e: e.memset(ap, v), after)

    def cpred(out, mask, data, after=()):
        return P.op("vector", lambda e: e.copy_predicated(out, mask, data), after)

    def heads(ap):
        return ap.rearrange("p (h f) -> p h f", h=4)

    def along(col, n=128):
        return col.unsqueeze(2).broadcast_to([128, col.shape[1], n])

    def over(mat, n=4):
        return mat.unsqueeze(1).broadcast_to([128, n, mat.shape[1]])

    cst = sb("cst", 0, [NCONST])
    lvl = sb("lvl", 5, [2, len(LEVELS), 128], U8)
    tri = sb("tri", 6.75, [2, 128], U8)
    ones = sb("ones", 7, [128])
    mod = sb("mod", 7.5, [2, 2, 48])
    amod = sb("amod", 8.25, [2, 2, 2, 8])
    mask_in = sb("mask_in", 137, [2048])
    ld_c = P.dma("sync", cst[:], io["consts"], "cst")
    ld_m = P.dma("sync", mask_in[:], io["masks"], "masks")
    ld_c = [ld_c, copy(lvl[:].rearrange("p d l f -> p (d l f)"), mask_in[:, 0:1792], [ld_m]),
            copy(tri[:].rearrange("p d f -> p (d f)"), mask_in[:, 1792:2048], [ld_m])]
    w_ones = memset(ones[:], 1.0)
    ident = cst[:, IDENT:IDENT + 128]

    def cv(off, n=1):
        return cst[:, off:off + n]

    NRAW, NW, LOOK = 4, 3, 2
    raw = [Cell(sb(f"raw{i}", 9 + 4 * i, [1024])) for i in range(NRAW)]
    whi = [Cell(sb(f"whi{i}", 25 + 4 * i, [1024], F32R)) for i in range(NW)]
    wlo = [Cell(sb(f"wlo{i}", 37 + 4 * i, [1024], F32R)) for i in range(NW)]
    hhi_t, hlo_t = sb("hhi", 49, [KC, T], F32R), sb("hlo", 65, [KC, T], F32R)
    hhi = [Cell(hhi_t[:, c, :]) for c in range(KC)]
    hlo = [Cell(hlo_t[:, c, :]) for c in range(KC)]

    spine = []
    u_dn, u_da, u_z, u_merge, u_out, u_wq, u_peer = [], [], [], [], [], [], []

    class Unit:

        def __init__(self, slab, groups, evac, ring=None, split=True):
            self.slab, self.groups, self.evac, self.ring, self.split = slab, groups, evac, ring, split

    state = {"loaded": 0, "split": 0, "unit": 0}
    spine_banks = Ring(bank[0:2])
    spent = set()
    open_banks = {}

    def load_to(n):
        while state["loaded"] < min(n, len(spine)):
            i = state["loaded"]
            if i >= NRAW and i - NRAW not in spent:
                return
            c = raw[i % NRAW]
            c.ready = [P.dma("sync", c.ap[:], spine[i].slab, f"raw{i % NRAW}", c.free)]
            state["loaded"] += 1

    def raw_done(i, readers):
        raw[i % NRAW].free = readers
        spent.add(i)
        load_to(i + 1 + NRAW)

    def split_to(n):
        while state["split"] < min(n, len(spine)):
            i = state["split"]
            state["split"] += 1
            if not spine[i].split:
                continue
            load_to(i + 1)
            r, hi, lo = raw[i % NRAW], whi[i % NW], wlo[i % NW]
            a = act(hi.ap[:], r.ap[:], ACT.Copy, [r.ready, hi.free])
            b = tt(lo.ap[:], r.ap[:], hi.ap[:].bitcast(F32), ALU.subtract, [r.ready, a, lo.free])
            hi.ready, lo.ready, hi.free, lo.free = [a], [b], [], []
            raw_done(i, [b])

    def run_unit():
        i = state["unit"]
        state["unit"] += 1
        u = spine[i]
        split_to(i + 1)
        if not u.split:
            load_to(i + 1)
            last = u.evac(raw[i % NRAW])
            raw_done(i, [last])
            split_to(i + 1 + LOOK)
            return
        hi, lo = whi[i % NW], wlo[i % NW]
        groups = u.groups()
        j, full = 0, False
        for key, pairs, opens, closes in groups:
            if opens:
                open_banks[key] = (u.ring or spine_banks).next()
            bk = open_banks[key]
            o = bk.ap[:, 0:pairs[0][0].ap.shape[-1]]
            for n, (xh, xl) in enumerate(pairs):
                w = hi.ap[:, 128 * j:128 * j + 128]
                mm(o, w, xh.ap, opens and n == 0, False, [hi.ready, xh.ready, bk.free if opens else []])
                mm(o, w, xl.ap, False, False, [xl.ready])
                j += 1
                if j % 4 == 0:
                    if j == 8:
                        split_to(i + 1 + LOOK)
                        full = True
                    yield
        if not full:
            split_to(i + 1 + LOOK)
        j, banks, lasts = 0, [], []
        for key, pairs, opens, closes in groups:
            bk = open_banks[key]
            o = bk.ap[:, 0:pairs[0][0].ap.shape[-1]]
            for n, (xh, xl) in enumerate(pairs):
                last = mm(o, lo.ap[:, 128 * j:128 * j + 128], xh.ap, False, closes and n == len(pairs) - 1,
                          [lo.ready])
                j += 1
            for xh, xl in pairs:
                xh.free, xl.free = [last], [last]
            if closes:
                banks.append(bk)
                lasts.append(last)
                del open_banks[key]
        hi.free, lo.free = [last], [last]
        if banks:
            u.evac(banks, lasts)
        yield

    def whole(*lists):
        return [(n, list(x), True, True) for n, x in enumerate(lists)]

    def run_spine(n, sides, rate=1):
        for _ in range(n):
            for _ in run_unit():
                for s in list(sides):
                    for _ in range(rate):
                        try:
                            next(s)
                        except StopIteration:
                            sides.remove(s)
                            break

    def drain(s):
        for _ in s:
            pass

    def split_chunk(h32, c, after):
        a = act(hhi[c].ap, h32, ACT.Copy, [after, hhi[c].free])
        b = tt(hlo[c].ap, h32, hhi[c].ap.bitcast(F32), ALU.subtract, [after, a, hlo[c].free])
        hhi[c].ready, hlo[c].ready = [a], [b]
        hhi[c].free, hlo[c].free = [], []
        return [a, b]

    WK = 81
    xT0 = sb("xT0", WK + 40, [KC, T])
    xc0 = [Cell(xT0[:, c, :]) for c in range(KC)]
    for c in range(KC):
        xc0[c].ready = [P.dma("sync", xc0[c].ap, io["xT"][:, c, :], f"x{c}")]
    sq = Ring([Cell(sb(f"sq{i}", WK + 74 + 2 * i, [T])) for i in range(2)])
    h32 = Ring([Cell(sb(f"h32{i}", WK + 78 + 2 * i, [T])) for i in range(2)])
    rst = sb("rst", WK + 82, [T])

    def first_norm():
        b = bank[2]
        last = None
        for c in range(KC):
            s = sq.next()
            a = act(s.ap[:], xc0[c].ap, ACT.Square, [xc0[c].ready, s.free])
            last = mm(b.ap, ones[:], s.ap[:], c == 0, c == KC - 1, [w_ones, a, b.free])
            s.done(last)
        l = act(rst[:], b.ap, ACT.Ln, [last, ld_c], bias=EPS, scale=1.0 / D)
        b.done(l)
        r = act(rst[:], rst[:], ACT.Exp, [l], scale=-0.5)
        for c in range(KC):
            h = h32.next()
            w = stt(h.ap[:], xc0[c].ap, cv(G_MIX + c), rst[:], ALU.mult, ALU.mult, [r, ld_c, h.free])
            h.done(split_chunk(h.ap[:], c, [w]))
            xc0[c].free = [w]

    qT, kT = sb("qT", WK, [4, T]), sb("kT", WK + 8, [4, T])
    ktok, vtok = sb("ktok", WK + 16, [4, 4, 128]), sb("vtok", WK + 24, [4, 4, 128])
    oacc = sb("oacc", WK + 32, [4, 4, 128])
    vT = sb("vT", WK + 56, [4, T])
    cbuf = Ring([Cell(sb(f"cbuf{i}", WK + 40 + 2.25 * i, [516])) for i in range(2)])
    cacc = Ring([Cell(sb(f"cacc{i}", WK + 45 + 2 * i, [T])) for i in range(2)])
    abT = sb("abT", WK + 68, [T])
    qkv = {"k": [Cell(kT[:, h, :]) for h in range(4)], "q": [Cell(qT[:, h, :]) for h in range(4)],
           "v": [Cell(vT[:, h, :]) for h in range(4)]}
    abc = Cell(abT[:])
    convpad = []

    def start_conv(after):
        for c in cbuf.cells:
            convpad.append(memset(c.ap[:, 0:2], 0.0, after))
            convpad.append(memset(c.ap[:, 514:516], 0.0, after))

    def conv_evac(kind, h):
        col = CONVW + 4 * ({"q": 0, "k": 4, "v": 8}[kind] + h)
        dst = qkv[kind][h]

        def evac(bks, done):
            cb, ca = cbuf.next(), cacc.next()
            a = act(cb.ap[:, 2:514], bks[0].ap, ACT.Copy, [done, cb.free])
            bks[0].done(a)
            o = ts(ca.ap[:], cb.ap[:, 0:T], cv(col), ALU.mult, [a, convpad, ld_c, ca.free])
            for j in range(1, 4):
                o = stt(ca.ap[:], cb.ap[:, j:j + T], cv(col + j), ca.ap[:], ALU.mult, ALU.add, [o])
            cb.done(o)
            s = act(dst.ap, ca.ap[:], ACT.Silu, [o, dst.free])
            ca.done(s)
            dst.ready, dst.free = [s], []
        return evac

    def ab_evac(bks, done):
        a = act(abT[:], bks[0].ap, ACT.Copy, [done])
        bks[0].done(a)
        abc.ready = [a]

    def h_rhs():
        return whole(zip(hhi, hlo))

    for kind in "kqv":
        for h in range(4):
            u_dn.append(Unit(io["w_in"][{"q": 0, "k": 4, "v": 8}[kind] + h], h_rhs, conv_evac(kind, h)))
    u_dn.append(Unit(io["w_in"][16], h_rhs, ab_evac))

    dnbs = [Ring(bank[2:4]), Ring(bank[4:6])]
    dnb = Ring(bank[2:6])
    small = sb("dnsmall", WK + 72, [448])

    def sm(i, n=32):
        return small[:, i:i + n]
    ab_tok, x_, ax_, g_, beta, gc, eg, nbeta, nbeg = (
        sm(0, 64), sm(64), sm(96), sm(128), sm(160), sm(192), sm(224), sm(256), sm(288))
    gl, kdf = [sm(320, 4), sm(324, 4)], [sm(328, 4), sm(332, 4)]
    nea = sm(336, 8)
    CH = WK + 40
    slot = [[sb(f"ch{d}_{i}", CH + 16 * d + 2 * i, [T]) for i in range(8)] for d in range(2)]
    o_ready = [[] for _ in range(4)]
    S_ready = [[], []]

    def dn_prepare():
        sq2 = Ring([Cell(sb(f"sqb{i}", WK + 49 + 2 * i, [T])) for i in range(2)])
        rs2 = Ring([Cell(sb(f"rsb{i}", WK + 64 + 2 * i, [T])) for i in range(2)])
        for kind, scale in (("k", 1.0), ("q", 128.0 ** -0.5)):
            for h in range(4):
                c = qkv[kind][h]
                s, r, b = sq2.next(), rs2.next(), dnb.next()
                a = act(s.ap[:], c.ap, ACT.Square, [c.ready, s.free])
                m = mm(b.ap, ones[:], s.ap[:], after=[a, b.free, w_ones])
                s.done(m)
                l = act(r.ap[:], b.ap, ACT.Ln, [m, r.free], bias=EPS)
                b.done(l)
                x = act(r.ap[:], r.ap[:], ACT.Exp, [l], scale=-0.5)
                w = stt(c.ap, c.ap, scale, r.ap[:], ALU.mult, ALU.mult, [x])
                r.done(w)
                c.ready = [w]
                yield
        tok = {}
        for kind, dst in (("k", ktok), ("v", vtok)):
            tok[kind] = []
            for n in range(4):
                b = dnb.next()
                for h in range(4):
                    m = tr(b.ap[:, 128 * h:128 * h + 128], qkv[kind][h].ap[:, 128 * n:128 * n + 128], ident,
                           [qkv[kind][h].ready, b.free, ld_c])
                w = act(dst[:, n], heads(b.ap), ACT.Copy, [m])
                b.done(w)
                tok[kind].append(w)
                yield
        b = dnb.next()
        for n in range(4):
            m = tr(b.ap[:, 16 * n:16 * n + 16], abT[0:16, 128 * n:128 * n + 128], ident[0:16, 0:16],
                   [abc.ready, b.free])
        w = copy(ab_tok, b.ap[:, 0:64], [m])
        b.done(w)
        ab = ab_tok.rearrange("p (n k d h) -> p k d n h", n=4, k=2, d=2)

        def dnh(ap):
            return ap.rearrange("p (d n h) -> p d n h", d=2, n=4)
        xs = []
        for d in range(2):
            dtb = cv(DTB + 4 * d, 4).unsqueeze(1).broadcast_to([128, 4, 4])
            xs.append(tt(dnh(x_)[:, d], ab[:, 0, d], dtb, ALU.add, [w, ld_c]))
            xs.append(copy(dnh(beta)[:, d], ab[:, 1, d], [w]))
        a1 = act(ax_, x_, ACT.Abs, xs)
        a2 = act(ax_, ax_, ACT.Exp, [a1], scale=-1.0)
        a3 = act(ax_, ax_, ACT.Ln, [a2], bias=1.0)
        s1 = stt(x_, x_, 0.0, ax_, ALU.max, ALU.add, [a3])
        a4 = act(nea, cv(ALOG, 8), ACT.Exp, [ld_c])
        gs = []
        for d in range(2):
            al = nea[:, 4 * d:4 * d + 4].unsqueeze(1).broadcast_to([128, 4, 4])
            gs.append(stt(dnh(g_)[:, d], dnh(x_)[:, d], -1.0, al, ALU.mult, ALU.mult, [s1, a4]))
        a5 = act(beta, beta, ACT.Exp, xs, scale=-1.0)
        b1 = ts(beta, beta, 1.0, ALU.add, [a5])
        b2 = P.op("vector", lambda e: e.reciprocal(beta, beta), [b1])
        yield
        b = dnb.next()
        m = mm(b.ap[:, 0:16], cv(UF, 128), g_[:, 0:16], after=[gs, b.free])
        m = mm(b.ap[:, 16:32], cv(UB, 128), g_[:, 16:32])
        w = copy(gc, b.ap[:, 0:32], [m])
        e1 = act(eg, gc, ACT.Exp, [w])
        b.done(w)
        n1 = ts(nbeta, beta, -1.0, ALU.mult, [b2])
        n2 = tt(nbeg, nbeta, eg, ALU.mult, [n1, e1])
        yield
        tok["small"] = [n2, n1, w, e1, b2, gs, tok["k"], tok["v"]]
        return tok

    def chain(d, tok):
        B0, B1, B2, B3, B4, B5, B6, S = slot[d]
        U = cv(UF if d == 0 else UB, 128)
        MASK = cv(MASKF if d == 0 else MASKB, 128)
        last = 127 if d == 0 else 0
        free = [[] for _ in range(8)]
        dnb = dnbs[d]
        for step in range(4):
            n = step if d == 0 else 3 - step
            col = 16 * d + 4 * n
            ncol = slice(col, col + 4)
            hs = [slice(128 * h, 128 * h + 128) for h in range(4)]
            tc = slice(128 * n, 128 * n + 128)
            small_ready = tok["small"]
            gu = tt(heads(B5[:]), over(U), along(g_[:, ncol]), ALU.mult, [small_ready, free[5]], eng="gpsimd")
            b = dnb.next()
            m = mm(b.ap, ones[:], B5[:], after=[gu, b.free])
            yield
            dd = tt(heads(B0[:]), along(gc[:, ncol]), heads(b.ap), ALU.subtract, [m, free[0]])
            if step < 3:
                kd = tt(kdf[d], heads(b.ap)[:, :, last], gc[:, ncol], ALU.subtract, [m])
                kd2 = act(kdf[d], kdf[d], ACT.Exp, [kd])
                glast = act(gl[d], heads(b.ap)[:, :, last], ACT.Exp, [free[7]])
            eB = act(B6[:], b.ap, ACT.Exp, [dd, kd, free[6]])
            b.done(eB)
            dm = tt(heads(B0[:]), heads(B0[:]), over(MASK), ALU.add, [dd])
            dec = act(B0[:], B0[:], ACT.Exp, [dm])
            qd = tt(heads(B6[:]), qT[:, :, tc], heads(B6[:]), ALU.mult, [eB], eng="gpsimd")
            bk, bq = dnb.next(), dnb.next()
            for h in range(4):
                mk = mm(bk.ap[:, hs[h]], kT[:, h, tc], kT[:, h, tc], after=[bk.free])
            for h in range(4):
                mq = mm(bq.ap[:, hs[h]], qT[:, h, tc], kT[:, h, tc], after=[bq.free])
            yield
            k1 = tt(heads(B1[:]), heads(bk.ap), along(nbeta[:, ncol]), ALU.mult, [mk, free[1]])
            nl = tt(B1[:], B1[:], B0[:], ALU.mult, [k1, dec])
            bk.done(k1)
            it = tt(B0[:], bq.ap, B0[:], ALU.mult, [mq, dec, nl])
            bq.done(it)
            vb = tt(heads(B3[:]), vtok[:, n], along(beta[:, ncol]), ALU.mult, [tok["v"], free[3]], eng="gpsimd")
            yield
            bn, bi = dnb.next(), dnb.next()
            for h in range(4):
                mn = tr(bn.ap[:, hs[h]], B1[:, hs[h]], ident, [nl, bn.free])
            for h in range(4):
                mi = tr(bi.ap[:, hs[h]], B0[:, hs[h]], ident, [it, bi.free])
            nlt = act(B2[:], bn.ap, ACT.Copy, [mn, free[2]])
            bn.done(nlt)
            itT = act(B0[:], bi.ap, ACT.Copy, [mi])
            bi.done(itT)
            x0 = copy(heads(B4[:]), over(ident), [free[4]], eng="gpsimd")
            y0 = copy(heads(B5[:]), over(ident), [m], eng="gpsimd")
            xr = cpred(heads(B4[:]), over(lvl[:, d, 0]), heads(B1[:]), [x0, nl, ld_c])
            yr = cpred(heads(B5[:]), over(lvl[:, 1 - d, 0]), heads(B2[:]), [y0, nlt])
            yield
            for i in range(1, 7):
                bt = dnb.next()
                for h in range(4):
                    mt = mm(bt.ap[:, hs[h]], B2[:, hs[h]], B4[:, hs[h]], after=[xr, nlt, bt.free])
                ev = act(B1[:], bt.ap, ACT.Copy, [mt, xr])
                bt.done(ev)
                yield
                by = dnb.next()
                for h in range(4):
                    my = mm(by.ap[:, hs[h]], B1[:, hs[h]], B5[:, hs[h]], after=[ev, yr, by.free])
                if i < 6:
                    bx = dnb.next()
                    for h in range(4):
                        mx = mm(bx.ap[:, hs[h]], B5[:, hs[h]], B1[:, hs[h]], after=[bx.free])
                    xr = cpred(heads(B4[:]), over(lvl[:, d, i]), heads(bx.ap), [mx])
                    bx.done(xr)
                yr = cpred(heads(B5[:]), over(lvl[:, 1 - d, i]), heads(by.ap), [my, mx])
                by.done(yr)
                yield
            kb = tt(heads(B1[:]), ktok[:, n], along(nbeg[:, ncol]), ALU.mult, [tok["k"], my], eng="gpsimd")
            if step < 3:
                kdc = tt(heads(B2[:]), ktok[:, n], along(kdf[d]), ALU.mult, [kd2, mt], eng="gpsimd")
            yield
            first = step == 0
            if not first:
                bw = dnb.next()
                for h in range(4):
                    mw = mm(bw.ap[:, hs[h]], B1[:, hs[h]], B5[:, hs[h]], after=[kb, yr, bw.free])
                wT = act(B4[:], bw.ap, ACT.Copy, [mw, mt])
                bw.done(wT)
                yield
            bv = dnb.next()
            for h in range(4):
                mv = mm(bv.ap[:, hs[h]], B5[:, hs[h]], B3[:, hs[h]], True, first, [vb, yr, bv.free])
                if not first:
                    mv = mm(bv.ap[:, hs[h]], B4[:, hs[h]], S[:, hs[h]], False, True, [wT, S_ready[d]])
            vn = act(B3[:], bv.ap, ACT.Copy, [mv])
            bv.done(vn)
            yield
            bo = dnb.next()
            for h in range(4):
                if not first:
                    mm(bo.ap[:, hs[h]], B6[:, hs[h]], S[:, hs[h]], True, False, [qd, bo.free, S_ready[d]])
                mo = mm(bo.ap[:, hs[h]], B0[:, hs[h]], B3[:, hs[h]], first, True, [itT, vn, bo.free])
            if step < 3:
                bs = dnb.next()
                for h in range(4):
                    ms = mm(bs.ap[:, hs[h]], B2[:, hs[h]], B3[:, hs[h]], after=[kdc, bs.free])
            if not o_ready[n]:
                ow = copy(oacc[:, n], heads(bo.ap), [mo])
            else:
                ow = tt(oacc[:, n], oacc[:, n], heads(bo.ap), ALU.add, [mo, o_ready[n]])
            o_ready[n] = [ow]
            bo.done(ow)
            end = mo
            if step < 3:
                if first:
                    sw = copy(S[:], bs.ap, [ms])
                else:
                    s1 = tt(heads(S[:]), heads(S[:]), along(gl[d]), ALU.mult, [glast, mo])
                    sw = tt(S[:], S[:], bs.ap, ALU.add, [s1, ms])
                bs.done(sw)
                S_ready[d] = [sw]
                end = ms
            free = [[end]] * 7 + [S_ready[d]]
            yield

    def delta():
        tok = yield from dn_prepare()
        a, b = chain(0, tok), chain(1, tok)
        live = [a, b]
        while live:
            for c in list(live):
                try:
                    next(c)
                except StopIteration:
                    live.remove(c)
            yield

    DA = WK + 74
    dq = [sb(f"dq{i}", DA + 12 * i, [3, T]) for i in range(2)]
    dk = [sb(f"dk{i}", DA + 6 + 12 * i, [3, T]) for i in range(2)]
    dqc = [[Cell(dq[i][:, g, :]) for g in range(3)] for i in range(2)]
    dkc = [[Cell(dk[i][:, g, :]) for g in range(3)] for i in range(2)]
    dv = sb("dv", DA + 24, [3, 4, 128])
    dvT = Ring([Cell(sb(f"dvT{i}", DA + 30 + 2 * i, [T])) for i in range(2)])
    dS = sb("dS", DA + 34, [768])
    dPT = sb("dPT", DA + 37, [6, 128])
    dB = Cell(sb("dB", DA + 40, [768]))
    oda = sb("oda", DA + 43, [4, T])
    dO = sb("dO", DA + 51, [128])
    dst_ = sb("dstat", DA + 51.5, [16])
    v_pending = {}
    dab = [bank[6], bank[7]]
    da_done = []

    def by_residue(ap):
        return ap.rearrange("p (l r) -> p r l", r=4)

    def da_evac(kind, h, g):
        def evac(bks, done):
            ps = by_residue(bks[0].ap)
            if kind == "v":
                c = dvT.next()
                a = act(c.ap[:].rearrange("p (r l) -> p r l", r=4), ps, ACT.Copy, [done, c.free])
                v_pending[h, g] = (c, a)
            else:
                c = (dqc if kind == "q" else dkc)[h % 2][g]
                o = c.ap.rearrange("p (r l) -> p r l", r=4)
                if kind == "q":
                    a = act(o, ps, ACT.Copy, [done, c.free], scale=128.0 ** -0.5)
                else:
                    a = copy(o, ps, [done, c.free])
                c.ready, c.free = [a], []
            bks[0].done(a)
        return evac

    for h in range(4):
        for kind, base in (("q", 17), ("k", 29), ("v", 41)):
            for g in range(3):
                u_da.append(Unit(io["w_in"][base + 4 * g + h], h_rhs, da_evac(kind, h, g)))

    def dilated():
        A, B = dab
        s_free, pv, out_done = [], [], []
        for h in range(4):
            vt = []
            for g in range(3):
                while (h, g) not in v_pending:
                    yield
                c, a = v_pending[h, g]
                b = (A, B)[g % 2]
                for r in range(4):
                    m = tr(b.ap[:, 128 * r:128 * r + 128], c.ap[:, 128 * r:128 * r + 128], ident, [a, b.free])
                w = act(dv[:, g], heads(b.ap), ACT.Copy, [m, pv])
                c.done(m)
                b.free = [w]
                vt.append(w)
                yield
            q, k = dq[h % 2], dk[h % 2]
            qk_ready = [c.ready for c in dqc[h % 2] + dkc[h % 2]]
            for r in range(4):
                ld = P.dma("gpsimd", dB.ap[:], io["da_bias"][h, r], "dabias", dB.free)
                t = slice(128 * r, 128 * r + 128)
                mm(A.ap, q[:, 0, t], k[:, 0, :], after=[qk_ready, A.free])
                mm(B.ap[:, 0:128], q[:, 1, t], k[:, 1, t], after=[B.free])
                m = mm(B.ap[:, 128:256], q[:, 2, t], k[:, 2, t])
                yield
                s2 = psum[:, 6:8, :].rearrange("p a b -> p (a b)")[:, 0:768]
                mx = P.op("vector", lambda e, s2=s2: e.tensor_tensor_reduce(
                    dS[:], s2, dB.ap[:], 1.0, -3e38, ALU.add, ALU.max, dst_[:, 0:1]), [m, ld, s_free])
                A.free, B.free, dB.free = [mx], [mx], [mx]
                nm = ts(dst_[:, 1:2], dst_[:, 0:1], -1.0, ALU.mult, [mx])
                ex = act(dS[:], dS[:], ACT.Exp, [nm], bias=dst_[:, 1:2], accum=dst_[:, 2:3])
                rc = P.op("vector", lambda e: e.reciprocal(dst_[:, 3:4], dst_[:, 2:3]), [ex])
                yield
                for i in range(6):
                    b = A if i < 4 else B
                    m = tr(b.ap[:, 128 * (i % 4):128 * (i % 4) + 128], dS[:, 128 * i:128 * i + 128], ident,
                           [ex, b.free])
                    if i == 3:
                        p1 = act(dPT[:, 0:4], heads(A.ap), ACT.Copy, [m, pv])
                s_free = [m]
                p2 = copy(dPT[:, 4:6], B.ap[:, 0:256].rearrange("p (a b) -> p a b", a=2), [m, pv])
                A.free, B.free = [p1], [p2]
                yield
                for i in range(6):
                    g, rr = (0, i) if i < 4 else (i - 3, r)
                    m = mm(A.ap[:, 0:128], dPT[:, i], dv[:, g, rr], i == 0, i == 5, [p1, p2, vt, A.free])
                pv = [m]
                o1 = act(dO[:], A.ap[:, 0:128], ACT.Copy, [m, rc, out_done], scale=dst_[:, 3:4])
                A.free = [o1]
                yield
                m = tr(B.ap[:, 0:128], dO[:], ident, [o1, B.free])
                w = copy(oda[:, h].rearrange("p (l r) -> p r l", r=4)[:, r], B.ap[:, 0:128], [m])
                out_done = [m]
                B.free = [w]
                da_done.append(w)
            for c in dqc[h % 2] + dkc[h % 2]:
                c.free = pv
            yield

    zs = sb("zs", DA, [4, T])
    zt = sb("zt", DA + 8, [T])
    zsc = [Cell(zs[:, h, :]) for h in range(4)]
    zfree = []

    def z_evac(h):
        def evac(bks, done):
            ps = bks[0].ap
            a = act(zt[:], ps, ACT.Exp, [done, zfree, [c.free for c in dqc[0] + dkc[0]]], scale=-1.0)
            b = act(zt[:], zt[:], ACT.Ln, [a], bias=1.0)
            c = act(zt[:], zt[:], ACT.Exp, [b], scale=-1.0)
            w = tt(zsc[h].ap, ps, zt[:], ALU.mult, [c])
            bks[0].done(w)
            zfree[:] = [w]
            zsc[h].ready = [w]
        return evac

    for h in range(4):
        u_z.append(Unit(io["w_in"][12 + h], h_rhs, z_evac(h)))

    odn_hi, odn_lo = sb("odn_hi", WK + 16, [4, T], F32R), sb("odn_lo", WK + 24, [4, T], F32R)
    oda_hi, oda_lo = sb("oda_hi", WK + 40, [4, T], F32R), sb("oda_lo", WK + 48, [4, T], F32R)
    odn_c = [(Cell(odn_hi[:, h]), Cell(odn_lo[:, h])) for h in range(4)]
    oda_c = [(Cell(oda_hi[:, h]), Cell(oda_lo[:, h])) for h in range(4)]
    osq, of = sb("osq", WK + 64, [T]), sb("of", WK + 66, [T])
    orr = sb("orr", WK + 68, [8])

    def finish_mixers(chain_end):
        of_free, osq_free = [], []
        for n in range(4):
            a = tt(heads(osq[:]), oacc[:, n], oacc[:, n], ALU.mult, [o_ready[n], chain_end, osq_free])
            b = P.op("vector", lambda e: e.tensor_reduce(orr[:, 0:4], heads(osq[:]), AX.X, ALU.add), [a])
            c = act(orr[:, 4:8], orr[:, 0:4], ACT.Ln, [b, osq_free], bias=EPS, scale=1.0 / 128)
            d_ = act(orr[:, 4:8], orr[:, 4:8], ACT.Exp, [c], scale=-0.5)
            e_ = tt(heads(osq[:]), oacc[:, n], along(orr[:, 4:8]), ALU.mult, [d_])
            bk = dnb.next()
            for h in range(4):
                m = tr(bk.ap[:, 128 * h:128 * h + 128], osq[:, 128 * h:128 * h + 128], ident, [e_, bk.free])
            osq_free = [m]
            f = stt(heads(of[:]), heads(bk.ap), cv(ONORM), zs[:, :, 128 * n:128 * n + 128], ALU.mult, ALU.mult,
                    [m, of_free, [z.ready for z in zsc]])
            bk.done(f)
            hi = act(odn_hi[:, :, 128 * n:128 * n + 128], heads(of[:]), ACT.Copy, [f])
            lo = tt(odn_lo[:, :, 128 * n:128 * n + 128], heads(of[:]),
                    odn_hi[:, :, 128 * n:128 * n + 128].bitcast(F32), ALU.subtract, [hi])
            of_free = [lo]
            for h in range(4):
                odn_c[h][0].ready.append(hi)
                odn_c[h][1].ready.append(lo)
            yield
        for h in range(4):
            hi = act(oda_hi[:, h], oda[:, h], ACT.Copy, [da_done, chain_end])
            lo = tt(oda_lo[:, h], oda[:, h], oda_hi[:, h].bitcast(F32), ALU.subtract, [hi])
            oda_c[h][0].ready, oda_c[h][1].ready = [hi], [lo]
            yield

    gates = Ring([Cell(sb(f"gate{i}", WK + 86 + 2 * i, [T])) for i in range(6)])
    gate_of = {}
    mg_hi, mg_lo = sb("mg_hi", WK + 56, [KC, T], F32R), None
    mg_lo = sb("mg_lo", WK + 98, [KC, T], F32R)
    mgc = [(Cell(mg_hi[:, c]), Cell(mg_lo[:, c])) for c in range(KC)]

    def gate_evac(which, o):
        def evac(bks, done):
            c = gates.next()
            a = act(c.ap[:], bks[0].ap, ACT.Sigmoid, [done, c.free, da_done])
            bks[0].done(a)
            gate_of[which, o] = (c, a)
        return evac

    xres = sb("xres", WK, [KC, T])
    xr = [Cell(xres[:, c, :]) for c in range(KC)]

    def merge_evac(o):
        def evac(bks, done):
            (c1, r1), (c2, r2) = gate_of["dn", o], gate_of["da", o]
            a = tt(c1.ap[:], bks[0].ap, c1.ap[:], ALU.mult, [done, r1])
            b = tt(c2.ap[:], bks[1].ap, c2.ap[:], ALU.mult, [done, r2])
            bks[0].done(a)
            bks[1].done(b)
            s = tt(c1.ap[:], c1.ap[:], c2.ap[:], ALU.add, [a, b])
            hi = act(mgc[o][0].ap, c1.ap[:], ACT.Copy, [s])
            lo = tt(mgc[o][1].ap, c1.ap[:], mgc[o][0].ap.bitcast(F32), ALU.subtract, [hi])
            c1.done(lo)
            c2.done(s)
            mgc[o][0].ready, mgc[o][1].ready = [hi], [lo]
        return evac

    late_banks = Ring(bank[2:6])
    GL = 2
    for o in range(KC + GL):
        if o < KC:
            u_merge.append(Unit(io["w_in"][53 + o], h_rhs, gate_evac("dn", o)))
            u_merge.append(Unit(io["w_in"][61 + o], h_rhs, gate_evac("da", o)))
        if o >= GL:
            u_merge.append(Unit(io["w_br"][o - GL], lambda: whole(odn_c, oda_c), merge_evac(o - GL), late_banks))

    class Norm:

        def __init__(self, name, kb, n, cells, ring):
            z = n / 256
            self.n, self.x, self.ring = n, cells, ring
            self.sq = Ring([Cell(sb(f"{name}sq{i}", kb + z * i, [n])) for i in range(2)])
            self.acc, self.r = sb(f"{name}acc", kb + 2 * z, [n]), sb(f"{name}r", kb + 3 * z, [n])
            self.hn = Ring([Cell(sb(f"{name}hn", kb + 4 * z, [n]))])
            self.summed, self.used = [], []

        def add(self, c, ready, after=()):
            s = self.sq.next()
            a = act(s.ap[:], self.x[c].ap, ACT.Square, [ready, s.free, after])
            if c == 0:
                g = copy(self.acc[:], s.ap[:], [a, self.summed, after], eng="gpsimd")
            elif c < KC - 1:
                g = tt(self.acc[:], self.acc[:], s.ap[:], ALU.add, [a, self.summed], eng="gpsimd")
            else:
                self.bank = self.ring.next()
                o = self.bank.ap[:, 0:self.n]
                mm(o, ones[:], self.acc[:], True, False, [self.summed, self.bank.free])
                g = mm(o, ones[:], s.ap[:], False, True, [a])
            s.done(g)
            self.summed = [g]

        def rs(self):
            l = act(self.r[:], self.bank.ap[:, 0:self.n], ACT.Ln, [self.summed, self.used], bias=EPS, scale=1.0 / D)
            self.bank.done(l)
            self.bank = None
            self.ready = [act(self.r[:], self.r[:], ACT.Exp, [l], scale=-0.5)]
            return self.ready

        def apply(self, scale, pairs, shift=None):
            rs = self.rs() if self.bank else self.ready
            for c in range(KC):
                h = self.hn.next()
                hi, lo = pairs[c]
                w = stt(h.ap[:], self.x[c].ap, scale(c), self.r[:], ALU.mult, ALU.mult, [rs, self.x[c].ready, h.free])
                if shift is None:
                    a = act(hi.ap, h.ap[:], ACT.Copy, [w, hi.free])
                    b = tt(lo.ap, h.ap[:], hi.ap.bitcast(F32), ALU.subtract, [a, lo.free])
                else:
                    a = act(hi.ap, h.ap[:], ACT.Identity, [w, hi.free], bias=shift(c))
                    b = stt(lo.ap, h.ap[:], shift(c), hi.ap.bitcast(F32), ALU.add, ALU.subtract, [a, lo.free])
                hi.ready, lo.ready = [a], [b]
                h.done(b)
            self.used = [w]

    norm = Norm("n", WK + 116, T, xr, late_banks)

    def wout_evac(o):
        def evac(bks, done):
            w = tt(xr[o].ap, xr[o].ap, bks[0].ap, ALU.add, [done, xr[o].ready])
            bks[0].done(w)
            xr[o].ready = [w]
            norm.add(o, [w], da_done)
        return evac

    for o in range(KC):
        u_out.append(Unit(io["w_out"][o], lambda: whole(mgc), wout_evac(o), late_banks))

    TK = WK + 16
    pq = sb("pq", TK, [16, T])
    pqc = [Cell(pq[:, i, :]) for i in range(16)]
    pkeys = sb("pkeys", TK + 32, [16, 128])
    cand, eqv, eqg = sb("cand", TK + 40, [2048]), sb("eqv", TK + 48, [2048]), sb("eqg", TK + 56, [2048])
    rest = sb("rest", TK + 64, [16, 128])
    sv = sb("sv", TK + 72, [16, 16])
    siu = sb("siu", TK + 73, [16, 16], U32)
    sif = sb("sif", TK + 74, [16, 16])
    cvl = sb("cvl", TK + 75, [8, 16])
    ciu = sb("ciu", TK + 75.5, [8, 16], U32)
    au, bu = sb("au", TK + 76, [128], U32), sb("bu", TK + 76.5, [128], U32)
    af, bf = sb("af", TK + 77, [128]), sb("bf", TK + 77.5, [128])
    i1f, i2f, gtf = sb("i1f", TK + 78, [128]), sb("i2f", TK + 78.5, [128]), sb("gtf", TK + 79, [128])
    ksm = sb("ksm", TK + 79.5, [32])
    i1T, i2T, gT = sb("i1T", TK + 80, [T]), sb("i2T", TK + 82, [T]), sb("gT", TK + 84, [T])

    key_idle = []

    def wq_evac(i):
        def evac(bks, done):
            a = act(pq[:, i, :], bks[0].ap, ACT.Copy, [done, pqc[i].free, key_idle])
            bks[0].done(a)
            pqc[i].ready = [a]
        return evac

    for i in range(16):
        u_wq.append(Unit(io["peer_wq"][i], h_rhs, wq_evac(i), spine_banks))

    keyb = bank[2:6]
    key_tok = {"T": []}

    def top_keys():
        ld = P.dma("sync", pkeys[:], io["peer_keys"], "pkeys", pqc[0].ready)
        NEGF = -3.0e38
        free = {"sel": [], "cand": [], "i": []}
        for n in range(4):
            t = slice(128 * n, 128 * n + 128)
            m = [None] * 16
            for i in range(16):
                m[i] = mm(keyb[i // 4].ap[:, 128 * (i % 4):128 * (i % 4) + 128], pq[:, i, t], pkeys[:, i, :],
                          after=[pqc[i].ready, ld, keyb[i // 4].free])
            yield
            src = [keyb[i // 4].ap[:, 128 * (i % 4):128 * (i % 4) + 128] for i in range(16)]
            m1, r1, m2, x1, x2 = [], [], [], [], []
            for i in range(16):
                m1.append(P.op("vector", lambda e, i=i: e.max(sv[:, i, 0:8], src[i]), [m[4 * (i // 4) + 3], free["sel"]]))
                if i % 4 == 3:
                    yield
            for i in range(16):
                r1.append(P.op("vector", lambda e, i=i: e.match_replace(
                    rest[:, i, :], sv[:, i, 0:8], src[i], NEGF), [m1[i]]))
                x1.append(P.op("vector", lambda e, i=i: e.max_index(siu[:, i, 0:8], sv[:, i, 0:8], src[i]), [m1[i]]))
                if i % 4 == 3:
                    keyb[i // 4].free = [r1[i], x1[i]]
                    yield
            for i in range(16):
                m2.append(P.op("vector", lambda e, i=i: e.max(sv[:, i, 8:16], rest[:, i, :]), [r1[i]]))
                if i % 4 == 3:
                    yield
            for i in range(16):
                x2.append(P.op("vector", lambda e, i=i: e.max_index(siu[:, i, 8:16], sv[:, i, 8:16], rest[:, i, :]),
                               [m2[i]]))
                if i % 4 == 3:
                    yield
            s4 = sv[:].rearrange("p (h c) k -> p h c k", c=2)
            s5 = sif[:].rearrange("p (h c) k -> p h c k", c=2)
            c4 = cand[:].rearrange("p (h a b) -> p h a b", h=8, a=16)
            fi = copy(sif[:], siu[:], [x1, x2])
            w = tt(c4, s4[:, :, 0, :].unsqueeze(3).broadcast_to([128, 8, 16, 16]),
                   s4[:, :, 1, :].unsqueeze(2).broadcast_to([128, 8, 16, 16]), ALU.add, [m1, m2, free["cand"]])
            yield
            ch = [cand[:, 256 * h:256 * h + 256] for h in range(8)]
            rh = [eqv[:, 256 * h:256 * h + 256] for h in range(8)]
            m1, r1, x1, m2, x2 = [], [], [], [], []
            for h in range(8):
                m1.append(P.op("vector", lambda e, h=h: e.max(cvl[:, h, 0:8], ch[h]), [w, free["i"]]))
            yield
            for h in range(8):
                r1.append(P.op("vector", lambda e, h=h: e.match_replace(rh[h], cvl[:, h, 0:8], ch[h], NEGF), [m1[h]]))
                x1.append(P.op("vector", lambda e, h=h: e.max_index(ciu[:, h, 0:8], cvl[:, h, 0:8], ch[h]), [m1[h]]))
                if h % 2:
                    yield
            for h in range(8):
                m2.append(P.op("vector", lambda e, h=h: e.max(cvl[:, h, 8:16], rh[h]), [r1[h]]))
            yield
            for h in range(8):
                x2.append(P.op("vector", lambda e, h=h: e.max_index(ciu[:, h, 8:16], cvl[:, h, 8:16], rh[h]), [m2[h]]))
                if h % 4 == 3:
                    yield
            cf = ciu[:].rearrange("p h k -> p (h k)")
            a1 = ts(au[:], cf, 4, ALU.logical_shift_right, [x1, x2])
            b1 = ts(bu[:], cf, 15, ALU.bitwise_and, [x1, x2])
            a2 = copy(af[:], au[:], [a1])
            b2 = copy(bf[:], bu[:], [b1])
            i16 = cst[:, IOTA:IOTA + 16].unsqueeze(1).broadcast_to([128, 128, 16])
            e3, g3 = eqv[:].rearrange("p (q j) -> p q j", j=16), eqg[:].rearrange("p (q j) -> p q j", j=16)

            def table(c):
                return s5[:, :, c, :].unsqueeze(2).broadcast_to([128, 8, 16, 16])
            p1 = tt(g3, along(bf[:], 16), i16, ALU.is_equal, [b2, ld_c, free["cand"]])
            p2 = tt(eqg[:].rearrange("p (h k j) -> p h k j", h=8, j=16),
                    eqg[:].rearrange("p (h k j) -> p h k j", h=8, j=16), table(1), ALU.mult, [p1, fi], eng="gpsimd")
            yield
            v1 = tt(e3, along(af[:], 16), i16, ALU.is_equal, [a2, x2, m2])
            v2 = tt(eqv[:].rearrange("p (h k j) -> p h k j", h=8, j=16),
                    eqv[:].rearrange("p (h k j) -> p h k j", h=8, j=16), table(0), ALU.mult, [v1, fi])
            v3 = P.op("vector", lambda e: e.tensor_reduce(i1f[:], e3, AX.X, ALU.add), [v2, free["i"]])
            yield
            d0 = tt(gtf[:].rearrange("p (h k) -> p h k", h=8), cvl[:], cvl[:, :, 0:1].broadcast_to([128, 8, 16]),
                    ALU.subtract, [m1, m2, free["i"]])
            d1 = act(gtf[:], gtf[:], ACT.Exp, [d0])
            d2 = P.op("vector", lambda e: e.tensor_reduce(ksm[:, 0:8], gtf[:].rearrange("p (h k) -> p h k", h=8),
                                                          AX.X, ALU.add), [d1])
            d3 = P.op("vector", lambda e: e.reciprocal(ksm[:, 8:16], ksm[:, 0:8]), [d2])
            d4 = tt(gtf[:].rearrange("p (h k) -> p h k", h=8), gtf[:].rearrange("p (h k) -> p h k", h=8),
                    ksm[:, 8:16].unsqueeze(2).broadcast_to([128, 8, 16]), ALU.mult, [d3])
            p3 = P.op("vector", lambda e: e.tensor_reduce(i2f[:], g3, AX.X, ALU.add), [p2, free["i"]])
            yield
            b = bank[6]
            q = [tr(b.ap[:, 0:128], i1f[:], ident, [v3, b.free]), tr(b.ap[:, 128:256], i2f[:], ident, [p3]),
                 tr(b.ap[:, 256:384], gtf[:], ident, [d4])]
            k = [copy(i1T[:, t], b.ap[:, 0:128], q), copy(i2T[:, t], b.ap[:, 128:256]), copy(gT[:, t], b.ap[:, 256:384])]
            b.free = k
            key_tok["T"].append(k)
            free = {"sel": [fi, w, v2, p2], "cand": [x1, p3], "i": [q, d0]}
            yield

    NG = 32
    gate_dram = nc.dram_tensor("gate_dram", [NG, 128, 128, 16], F32, kind="Internal").ap()
    ea = Ring([Cell(sb(f"ea{i}", TK + 8 * i, [16, 128])) for i in range(2)])
    eb = Ring([Cell(sb(f"eb{i}", TK + 16 + 8 * i, [16, 128])) for i in range(2)])
    stage = Ring([Cell(sb(f"stage{i}", TK + 32 + 8 * i, [128, 16])) for i in range(2)])
    gb = Ring(bank[2:6])
    g_written = []

    def dense_gates():
        io_b = cst[:, IOTA:IOTA + 128].unsqueeze(1).broadcast_to([128, 16, 128])
        for g in range(NG):
            t = slice(16 * g, 16 * g + 16)
            A, B, S = ea.next(), eb.next(), stage.next()
            k = key_tok["T"]
            a1 = tt(A.ap[:], io_b, along(i1T[:, t]), ALU.is_equal, [k, A.free])
            a2 = tt(A.ap[:], A.ap[:], along(gT[:, t]), ALU.mult, [a1], eng="gpsimd")
            b1 = tt(B.ap[:], io_b, along(i2T[:, t]), ALU.is_equal, [k, B.free])
            yield
            ws = []
            for u in range(4):
                b = gb.next()
                for v in range(4):
                    m = mm(b.ap[:, 128 * v:128 * v + 128], A.ap[:, 4 * u + v, :], B.ap[:, 4 * u + v, :],
                           after=[a2, b1, b.free])
                w = act(S.ap[:, :, 4 * u:4 * u + 4], b.ap.rearrange("p (v j) -> p j v", v=4), ACT.Copy, [m, S.free])
                b.done(w)
                ws.append(w)
                if u == 1:
                    yield
            A.done(m)
            B.done(m)
            d = P.dma("sync", gate_dram[g].rearrange("p j t -> p (j t)"), S.ap[:].rearrange("p j t -> p (j t)"),
                      f"stage{g % 2}", ws)
            S.done(d)
            g_written.append(d)
            yield

    GJ = 8
    gin = [Cell(sb(f"gin{i}", TK + 16 * i, [NG, GJ, 16])) for i in range(2)]
    ag_hi = [sb(f"ag_hi{i}", TK + 32 + 16 * i, [GJ, T], F32R) for i in range(2)]
    ag_lo = [sb(f"ag_lo{i}", TK + 64 + 16 * i, [GJ, T], F32R) for i in range(2)]
    agc = [[(Cell(ag_hi[i][:, j]), Cell(ag_lo[i][:, j])) for j in range(GJ)] for i in range(2)]
    uact = Ring([Cell(sb(f"uact{i}", TK + 96 + 2 * i, [T])) for i in range(2)])

    def load_gates(g):
        c = gin[g % 2]
        c.ready = [P.dma("sync", c.ap[:].rearrange("p n j t -> p n (j t)"),
                         gate_dram[:, :, GJ * g:GJ * g + GJ, :].rearrange("n p j t -> p n (j t)"),
                         f"gin{g % 2}", [g_written, c.free])]
        c.free = []

    def u_evac(j):
        g, jj = divmod(j, GJ)

        def evac(bks, done):
            c, gc_ = uact.next(), gin[g % 2]
            hi, lo = agc[g % 2][jj]
            a = act(c.ap[:], bks[0].ap, ACT.Gelu_apprx_tanh, [done, c.free])
            bks[0].done(a)
            t3 = c.ap[:].rearrange("p (n t) -> p n t", t=16)
            w = tt(t3, t3, gc_.ap[:, :, jj, :], ALU.mult, [a, gc_.ready])
            gc_.free = gc_.free + [w]
            h = act(hi.ap, c.ap[:], ACT.Copy, [w, hi.free])
            l = tt(lo.ap, c.ap[:], hi.ap.bitcast(F32), ALU.subtract, [h, lo.free])
            c.done(l)
            hi.ready, lo.ready = [h], [l]
        return evac

    def v_evac(g, dt):
        def evac(bks, done):
            w = tt(xr[dt].ap, xr[dt].ap, bks[0].ap, ALU.add, [done, xr[dt].ready])
            bks[0].done(w)
            xr[dt].ready = [w]
            if g == 128 // GJ - 1:
                norm.add(dt, [w])
        return evac

    NGR = 128 // GJ
    u_units = [[Unit(io["peer_u"][GJ * g + j], h_rhs, u_evac(GJ * g + j), spine_banks) for j in range(GJ)]
               for g in range(NGR)]
    v_units = [[Unit(io["peer_v"][8 * g + d], lambda g=g: whole(agc[g % 2]), v_evac(g, d), late_banks) for d in range(8)]
               for g in range(NGR)]
    u_peer += u_units[0]
    for g in range(NGR):
        for j in range(8):
            if g + 1 < NGR:
                u_peer.append(u_units[g + 1][j])
            u_peer.append(v_units[g][j])

    M0 = 97
    s32 = sb("s32", M0 + 80, [KC, 32])
    msb = Ring([Cell(sb(f"msb{i}", M0 + 81 + i, [256])) for i in range(2)])
    mod_ready = [[], []]
    s32_ready = []
    mod_bank = {}

    def start_mod():
        a = memset(s32[:], 0.0, [n.free for p in odn_c + oda_c + mgc for n in p])
        sv_ = s32[:].rearrange("p k v -> p v k")[:, 0:2, :]
        s32_ready.append(act(sv_, cv(CVEC, 16).rearrange("p (v k) -> p v k", v=2), ACT.Silu, [a, ld_c]))

    def mod_unit(l, q, k):
        def run(rawc):
            if k == 0:
                mod_bank[0] = late_banks.next()
            bk = mod_bank[0]
            for j in range(4):
                m = mm(bk.ap[32 * j:32 * j + 32, 0:256], s32[:, k, :], rawc.ap[:, 256 * j:256 * j + 256],
                       k == 0, k == KC - 1, [rawc.ready, s32_ready, bk.free], (0, 32 * j))
            if k == KC - 1:
                c = msb.next()
                w = act(c.ap[:], bk.ap[:, 0:256], ACT.Copy, [m, c.free])
                bk.done(w)
                b2 = late_banks.next()
                for x in range(2):
                    t = tr(b2.ap[:, 128 * x:128 * x + 128], c.ap[:, 128 * x:128 * x + 128], ident, [w, b2.free])
                c.done(t)
                for x in range(2):
                    src = b2.ap[:, 128 * x:128 * x + 128].rearrange("p (j v) -> p j v", j=4)[:, :, 0:2]
                    c0 = 8 * q + x
                    dst = mod[:, l].rearrange("p v c -> p c v")[:, c0:c0 + 7:2, :]
                    bias = cst[:, BMOD + 48 * l + c0:BMOD + 48 * l + c0 + 7:2].unsqueeze(2).broadcast_to([128, 4, 2])
                    w = tt(dst, src, bias, ALU.add, [t, ld_c])
                    mod_ready[l].append(w)
                b2.done(w)
                if q == 5:
                    for v in range(2):
                        for x, (nrm, sc) in enumerate(((N2MIX, 8), (N2FFN, 32))):
                            mod_ready[l].append(stt(amod[:, l, v, x], mod[:, l, v, sc:sc + 8], 1.0,
                                                    cv(nrm + 8 * l, 8), ALU.add, ALU.mult, [mod_ready[l], ld_c]))
            return m
        return run

    mod_units = [Unit(io["w_mod"][(l * 6 + q) * 8 + k], None, mod_unit(l, q, k), None, False)
                 for l in range(2) for q in range(6) for k in range(8)]

    def modv(l, v, chunk):
        return mod[:, l, v, chunk:chunk + 1]

    c2 = sb("c2", M0, [NC2])
    wa2 = sb("wa2", M0 + 9.5, [2, 256])
    c2_ready, wa2_cell = [], Cell(wa2[:])
    res_dram = nc.dram_tensor("ctx_res", [2, 128, 2560], F32, kind="Internal").ap()
    res_written = [None, None]

    class Mixer:
        pass

    def silu_chain(out, ps, tmp, after):
        a = act(tmp, ps, ACT.Exp, after, scale=-1.0)
        b = act(tmp, tmp, ACT.Ln, [a], bias=1.0)
        c = act(tmp, tmp, ACT.Exp, [b], scale=-1.0)
        return tt(out, ps, tmp, ALU.mult, [c])

    def make_mixer(l, v, N, base, hin, full, idle):
        m = Mixer()
        m.l, m.v, m.N, m.full, m.hin = l, v, N, full, hin
        NT, z = N // 128, N / 512
        nm = f"{'cl'[v == 0]}{l}"
        lat = v == 0
        lay = (dict(gq=0, gk=4, gvT=8, gvtok=12, gg=16, za=20, C=22, qin=26, kin=30, ktok=34, Sen=38, aT=46, tmp=50,
                    S0=54, nq=56, nk=62, nvT=68, sq=74, sk=80, svT=82, svtok=84, rope=86, pipe=12, nvtok=0, swm=33,
                    res=38) if lat else
               dict(gq=0, gk=2, gvT=4, gvtok=6, gg=8, za=10, C=11, qin=13, kin=15, ktok=17, Sen=19, aT=23, tmp=27,
                    S0=29, nq=30, nvT=33, sq=36, svT=39, pipe=0, res=40))

        def buf(key, shape, dt=F32, off=0.0, name=None):
            return sb(f"{nm}_{name or key}", base + lay[key] + off, shape, dt)
        res = buf("res", [2560])
        r_nk = res[:, 0:768].rearrange("p (i t) -> p i t", i=3)
        r_nv = res[:, 768:1536].rearrange("p (n f) -> p n f", n=2)
        r_sk = res[:, 1536:1792]
        r_sv = res[:, 1792:2048].rearrange("p (n f) -> p n f", n=2)
        r_S = res[:, 2048:2560].rearrange("p (d i f) -> p d i f", d=2, i=2)
        gq, gk, gvT, gvtok, gg = [buf(k, [2, N]) for k in ("gq", "gk", "gvT", "gvtok", "gg")]
        za, C, qin, kin, ktok, tmp = buf("za", [N]), *[buf(k, [2, N]) for k in ("C", "qin", "kin", "ktok", "tmp")]
        NCH = N // 64
        Sen = buf("Sen", [NCH, 2, 128])
        aT = [buf("aT", [4, 128], F32, 2 * i, f"aT{i}") for i in range(2)]
        dec = sb(f"{nm}_dec", 8.5 if lat else 8.75, [2, NCH])
        S0 = buf("S0", [2, 2, 128] if lat else [2, 128])
        nq, nvT, sq_, svT = buf("nq", [3, N]), buf("nvT", [3, N]), buf("sq", [3, N]), buf("svT", [N])
        nk = buf("nk", [3, N]) if lat else r_nk
        sk = buf("sk", [N]) if lat else r_sk
        ready = {}

        def plain(dst, key, scale=None, perm=False):
            def evac(bks, done):
                ps, o = bks[0].ap[:, 0:N], dst
                if perm:
                    if perm == "query":
                        ps = ps.rearrange("p (r b c) -> p b r c", r=8, b=4)
                        o = dst.rearrange("p (b r c) -> p b r c", b=4, r=8)
                    else:
                        ps = ps.rearrange("p (x r w) -> p x w r", x=2, r=4)
                        o = dst.rearrange("p (x w r) -> p x w r", x=2, r=4)
                    if scale is not None:
                        w = ts(o, ps, scale, ALU.mult, [done, idle])
                    else:
                        w = copy(o, ps, [done, idle])
                elif scale is not None:
                    w = act(o, ps, ACT.Copy, [done, idle], scale=scale)
                else:
                    w = act(o, ps, ACT.Copy, [done, idle])
                bks[0].done(w)
                ready[key] = [w]
            return evac

        def silu_evac(dst, i):
            def evac(bks, done):
                w = silu_chain(dst, bks[0].ap[:, 0:N], tmp[:, 0], [done, idle, ready.get("gg", [])])
                bks[0].done(w)
                ready["gg"] = ready.get("gg", []) + [w]
            return evac

        proj = []
        for i in range(2):
            proj.append((4 + i, plain(gvT[:, i], f"gv{i}")))
        proj.append((8, plain(za[:], "za")))
        for i in range(2):
            proj.append((2 + i, plain(gk[:, i], f"gk{i}")))
        if full:
            for i in range(2):
                proj.append((i, plain(gq[:, i], f"gq{i}", 0.125)))
            for i in range(2):
                proj.append((6 + i, silu_evac(gg[:, i], i)))
        for i in range(3):
            if full:
                proj.append((9 + i, plain(nq[:, i], f"nq{i}", 0.125, lat and "query")))
            proj.append((12 + i, plain(nk[:, i], f"nk{i}", None, lat and "key")))
            proj.append((15 + i, plain(nvT[:, i], f"nv{i}", None, lat and "key")))
        if full:
            for i in range(3):
                proj.append((18 + i, plain(sq_[:, i], f"sq{i}", 0.125)))
        proj.append((21, plain(sk[:] if lat else sk, "sk")))
        proj.append((22, plain(svT[:], "sv")))
        m.units = [Unit(io["w_in2"][l * 23 + t], lambda: whole(hin), ev) for t, ev in proj]
        m.proj_done = False
        ob = bank[2:4]
        g4 = Ring(bank[4:8])
        hs = [slice(0, 64), slice(64, 128)]

        def wait_for(*keys):
            while not all(k in ready for k in keys):
                yield
            return [ready[k] for k in keys]

        def gla():
            w_wa = P.dma("sync", wa2[:], io["wa2"][l], "wa2", [wa2_cell.free, c2_ready])
            if lat:
                s_init = P.dma("sync", S0[:].rearrange("p d i f -> p (d i f)"), res_dram[l][:, 2048:2560], "S0",
                               [idle, res_written[l]])
            else:
                s_init = memset(S0[:], 0.0, [idle])
            vt = []
            for i in range(2):
                rd = yield from wait_for(f"gv{i}")
                b = g4.next()
                for n in range(NT):
                    t = tr(b.ap[:, 128 * n:128 * n + 128], gvT[:, i, 128 * n:128 * n + 128], ident, [rd, b.free])
                w = copy(gvtok[:, i], b.ap[:, 0:N], [t, idle])
                b.done(w)
                vt.append(w)
                yield
            r_za = yield from wait_for("za")
            o_first = [full, full]
            q_done, k_done, kt_done, sen_done, at_done, wa_done = [], [], [], [], [], []
            tmp_done = []
            for d in range(2):
                zb = []
                for i in range(2):
                    b = g4.next()
                    t = mm(b.ap[:, 0:N], wa2[:, d, 128 * i:128 * i + 128], za[:], after=[w_wa, r_za, b.free])
                    w = ts(tmp[:, i], b.ap[:, 0:N], cv(GBA + 4 * l + 2 * d + i), ALU.add,
                           [t, ld_c, tmp_done, ready.get("gg", [])], -1.0, ALU.mult)
                    b.done(w)
                    zb.append(w)
                wa_done.append(t)
                yield
                a = act(C[:], tmp[:], ACT.Abs, [zb, idle, q_done, k_done])
                a = act(C[:], C[:], ACT.Exp, [a], scale=-1.0)
                a = act(C[:], C[:], ACT.Ln, [a], bias=1.0)
                w = stt(tmp[:], tmp[:], 0.0, C[:], ALU.max, ALU.add, [a])
                yield
                sc = []
                for i in range(2):
                    rst = c2[:, RSTF:RSTF + N] if d == 0 else c2[:, RSTB + T - N:RSTB + T][:, ::-1]
                    o_, i_ = (C[:, i], tmp[:, i]) if d == 0 else (C[:, i][:, ::-1], tmp[:, i][:, ::-1])
                    sc.append(P.op("vector", lambda e, o_=o_, i_=i_, rst=rst: e.tensor_tensor_scan(
                        o_, rst, i_, 0.0, ALU.mult, ALU.add), [w, c2_ready]))
                C4 = C[:].rearrange("p i (c s) -> p i c s", s=64)
                cl = C4[:, :, :, 63 if d == 0 else 0]
                r_k = yield from wait_for("gk0", "gk1")
                dc = act(dec[:], cl, ACT.Exp, [sc, idle, sen_done], scale=-1.0 / 16)
                if full:
                    r_q = yield from wait_for("gq0", "gq1")
                    qa = act(qin[:], C[:], ACT.Exp, [sc, idle, q_done], scale=-1.0 / 16)
                    q_ = tt(qin[:], qin[:], gq[:], ALU.mult, [qa, r_q])
                    ka = act(kin[:], C[:], ACT.Exp, [sc, idle, k_done], scale=1.0 / 16)
                    k_ = tt(kin[:], kin[:], gk[:], ALU.mult, [ka, r_k], eng="gpsimd")
                yield
                t4 = tmp[:].rearrange("p i (c s) -> p i c s", s=64)
                e = tt(t4, C4, cl.unsqueeze(3).broadcast_to([128, 2, NCH, 64]), ALU.subtract, [sc])
                e = act(tmp[:], tmp[:], ACT.Exp, [e], scale=1.0 / 16)
                e = tt(tmp[:], tmp[:], gk[:], ALU.mult, [e, r_k])
                yield
                kt = []
                for i in range(2):
                    b = g4.next()
                    for n in range(NT):
                        t = tr(b.ap[:, 128 * n:128 * n + 128], tmp[:, i, 128 * n:128 * n + 128], ident, [e, b.free])
                    w = act(ktok[:, i], b.ap[:, 0:N], ACT.Copy, [t, idle, kt_done])
                    b.done(w)
                    kt.append(w)
                tmp_done = [t]
                yield
                cs = [None] * NCH
                for c0 in range(0, NCH, 4):
                    for p in range(2):
                        b = g4.next()
                        for x in range(2):
                            c = c0 + 2 * x + p
                            n = c // 2
                            for i in range(2):
                                t = mm(b.ap[:, 256 * x + 128 * i:256 * x + 128 * i + 128],
                                       ktok[hs[p], i, 128 * n:128 * n + 128], gvtok[hs[p], i, 128 * n:128 * n + 128],
                                       after=[kt, vt, b.free])
                        c = c0 + p
                        w = tt(Sen[:, c:c + 3:2], b.ap.rearrange("p (x i f) -> p x i f", x=2, i=2),
                               c2[:, BMASK:BMASK + 128].unsqueeze(1).unsqueeze(1).broadcast_to([128, 2, 2, 128]),
                               ALU.mult, [t, idle, sen_done, c2_ready])
                        b.done(w)
                        cs[c] = cs[c + 2] = w
                    yield
                kt_done = [t]
                order = list(range(NCH)) if d == 0 else list(range(NCH - 1, -1, -1))
                enter, e_ready = {}, {}
                cur, cr = (S0[:, d] if lat else S0[:]), [s_init]
                for c in order:
                    enter[c], e_ready[c] = cur, cr
                    cr = [stt(Sen[:, c, i], cur[:, i], dec[:, i, c:c + 1], Sen[:, c, i], ALU.mult, ALU.add,
                              [cr, dc, cs[c]]) for i in range(2)]
                    cur = Sen[:, c]
                    if c % 2:
                        yield
                if not lat:
                    m.S_out = m.S_out + [copy(r_S[:, d], cur, [cr, idle], eng="gpsimd")]
                    sen_done = [m.S_out]
                if not full:
                    continue
                for c in order:
                    for i in range(2):
                        t = mm(ob[i].ap[:, 64 * c:64 * c + 64], enter[c][:, i], qin[:, i, 64 * c:64 * c + 64],
                               o_first[i], False, [e_ready[c], q_, ob[i].free])
                        o_first[i] = False
                    if c % 4 == 3:
                        yield
                sen_done = sen_done + [t]
                for x in range(2):
                    z_ = memset(aT[x][:], 0.0, [idle, at_done])
                    at_done = at_done + [z_]
                for n0 in range(0, NT, 2):
                    bh = [g4.next(), g4.next()]
                    cp = []
                    for h in range(2):
                        for x in range(2):
                            for i in range(2):
                                tk = slice(128 * (n0 + x), 128 * (n0 + x) + 128)
                                t = mm(bh[h].ap[:, 256 * x + 128 * i:256 * x + 128 * i + 128], kin[hs[h], i, tk],
                                       qin[hs[h], i, tk], after=[k_, q_, bh[h].free])
                        w = cpred(aT[h][:], over(tri[:, d]), heads(bh[h].ap), [t, at_done, ld_c])
                        bh[h].done(w)
                        cp.append(w)
                    yield
                    for x in range(2):
                        for i in range(2):
                            for h in range(2):
                                tk = slice(128 * (n0 + x), 128 * (n0 + x) + 128)
                                t = mm(ob[i].ap[hs[h], tk], gvtok[:, i, 128 * (n0 + x) + 64 * h:128 * (n0 + x) + 64 * h + 64],
                                       aT[h][:, 2 * x + i], False, d == 1 and n0 + x == NT - 1, [cp, vt])
                    at_done = [t]
                    yield
                q_done, k_done = [t], [t]
            wa2_cell.free = wa_done
            if not full:
                return
            while not m.proj_done:
                yield
            r_g = ready["gg"]
            for i in range(2):
                s_ = act(tmp[:, i], ob[i].ap[:, 0:N], ACT.Square, [t, tmp_done])
                b = g4.next()
                x = mm(b.ap[:, 0:N], c2[:, ONESBD:ONESBD + 128], tmp[:, i], after=[s_, b.free])
                w = act(C[:, i], b.ap[:, 0:N], ACT.Ln, [x], bias=EPS, scale=1.0 / 64)
                b.done(w)
                w = act(C[:, i], C[:, i], ACT.Exp, [w], scale=-0.5)
                w = tt(tmp[:, i], ob[i].ap[:, 0:N], C[:, i], ALU.mult, [w, x])
                ob[i].free = [w]
                w = stt(tmp[:, i], tmp[:, i], cv(GNORM + 2 * l + i), gg[:, i], ALU.mult, ALU.mult, [w, r_g])
                hi, lo = hin[i]
                a = act(hi.ap, tmp[:, i], ACT.Copy, [w, hi.free])
                e = tt(lo.ap, tmp[:, i], hi.ap.bitcast(F32), ALU.subtract, [a, lo.free])
                hi.ready, lo.ready = [a], [e]
                m.gla_end = [a, e]
                yield

        m.S_out = []
        m.gla = gla

        def store_ctx():
            ws = []
            for i in range(3):
                b = g4.next()
                for n in range(2):
                    t = tr(b.ap[:, 128 * n:128 * n + 128], nvT[:, i, 128 * n:128 * n + 128], ident,
                           [ready[f"nv{i}"], b.free])
                w = copy(r_nv[:, :, 128 * i:128 * i + 128], b.ap[:, 0:256].rearrange("p (n f) -> p n f", n=2), [t, idle])
                b.done(w)
                ws.append(w)
                yield
            b = g4.next()
            for n in range(2):
                t = tr(b.ap[:, 128 * n:128 * n + 128], svT[:, 128 * n:128 * n + 128], ident, [ready["sv"], b.free])
            w = copy(r_sv, b.ap[:, 0:256].rearrange("p (n f) -> p n f", n=2), [t, idle])
            b.done(w)
            ws.append(w)
            yield
            m.v_ready = ws
            keys = [ready[k] for k in ("nk0", "nk1", "nk2", "sk")]
            res_written[l] = P.dma("sync", res_dram[l], res[:], "res", [ws, keys, m.S_out])
        m.store_ctx = store_ctx

        def attention():
            pairs = [bank[2:4], bank[4:6], bank[6:8]]
            ncol = 640 if lat else 256
            idle2 = m.gla_end
            k_ready = [ready[k] for k in ready if k[:2] in ("nk", "nq", "sq", "sk")]
            if lat:
                ld = P.dma("sync", res[:, 0:2048], res_dram[l][:, 0:2048], "resin", [idle2, res_written[l]])
                swm = buf("swm", [1152])
                ldm = P.dma("sync", swm[:], io["swa_mask"], "swm", [idle2])
                k_ready.append(ld)
                nvtok, svtok = buf("nvtok", [4, 2, 3, 128]), buf("svtok", [4, 128])
                r_rope = yield from rope()
                vt = []
                g8 = Ring(bank[4:8])
                for cb in range(4):
                    for x in range(2):
                        b = g8.next()
                        c0 = min(max(16 * cb - 8, 0), 32)
                        for i in range(3):
                            src = nvT[:, i, 256 * x + 4 * c0:256 * x + 4 * c0 + 128]
                            t = tr(b.ap[:, 128 * i:128 * i + 128], src, ident, [ready[f"nv{i}"], b.free])
                        w = (copy if x else acopy)(nvtok[:, cb, x].rearrange("p i f -> p (i f)"), b.ap[:, 0:384],
                                                   [t, idle2])
                        b.done(w)
                        vt.append(w)
                    yield
                b = g8.next()
                for n in range(4):
                    t = tr(b.ap[:, 128 * n:128 * n + 128], svT[:, 128 * n:128 * n + 128], ident, [ready["sv"], b.free])
                w = copy(svtok[:].rearrange("p n f -> p (n f)"), b.ap, [t, idle])
                b.done(w)
                vt.append(w)
                yield
                vt.append(ld)
            else:
                vt = m.v_ready
            items = []
            for h in range(6):
                i, p = divmod(h, 2)
                for n in range(NT):
                    if lat:
                        c0 = min(max(16 * n - 8, 0), 32)
                        kw = nk[hs[p], i].rearrange("p (x w) -> p x w", x=2)[:, :, 4 * c0:4 * c0 + 128]
                        keys = [(kw, 0, 256), (r_nk[hs[p], i], 256, 512)]
                        vals = [nvtok[:, n, x, i, hs[p]] for x in range(2)] + \
                               [r_nv[:, x, 64 * h:64 * h + 64] for x in range(2)]
                        o = lambda cell, n=n, p=p: cell.rearrange("p (r b c) -> p b r c", r=8, b=4)[hs[p], n]
                        items.append((nq[hs[p], i, 128 * n:128 * n + 128], keys, vals, 2 + i, p, o,
                                      ("dram", io["na_bias"][l, h, n]), None))
                    else:
                        items.append((nq[hs[p], i, 128 * n:128 * n + 128], [(r_nk[hs[p], i], 0, 256)],
                                      [r_nv[:, x, 64 * h:64 * h + 64] for x in range(2)], 2 + i, p,
                                      lambda cell, n=n, p=p: cell[hs[p], 128 * n:128 * n + 128], None, None))
            for i in range(3):
                for p in range(2):
                    sink = cv(SINK + 6 * l + 3 * p + i)
                    for n in range(NT):
                        o = lambda cell, n=n, p=p: cell[hs[p], 128 * n:128 * n + 128]
                        q = sq_[hs[p], i, 128 * n:128 * n + 128]
                        rv = [r_sv[:, x, 64 * p:64 * p + 64] for x in range(2)]
                        if lat:
                            lo, hi = max(n - 1, 0), min(n + 2, 4)
                            w = 128 * (hi - lo)
                            keys = [(sk[hs[p], 128 * lo:128 * hi], 0, w)]
                            if w == 384:
                                keys += [(r_sk[hs[p], 0:128], 384, 512), (r_sk[hs[p], 128:256], 512, 640)]
                            else:
                                keys += [(r_sk[hs[p], :], 256, 512)]
                            vals = [svtok[:, x, 64 * p:64 * p + 64] for x in range(lo, hi)] + rv
                            mask = swm[:, 128:640] if n == 0 else swm[:, 640:1152] if n == 3 else swm[:, 0:640]
                            items.append((q, keys, vals, 5 + i, p, o, ("sbuf", mask), sink))
                        else:
                            items.append((q, [(r_sk[hs[p], :], 0, 256)], rv, 5 + i, p, o, None, sink))
            for c in range(2, 8):
                hin[c][0].ready, hin[c][1].ready = [], []

            def pipe(x):
                B0, B1 = pairs[x]
                sp = psum[:, 2 + 2 * x:4 + 2 * x, :].rearrange("p a b -> p (a b)")
                S = buf("pipe", [ncol], F32, x * (7 if lat else 2), f"S{x}")
                PT = buf("pipe", [ncol], F32, x * (7 if lat else 2) + (2.5 if lat else 1), f"PT{x}")
                st = sb(f"{nm}_st{x}", (8.5 if lat else 8.75) + (x + 1) / 16, [16])
                if lat:
                    bb = Cell(buf("pipe", [512], F32, 7 * x + 5, f"bias{x}")[:])
                    zero = memset(bb.ap[:, 256:512], 0.0, [idle2])
                pt_done, s_done = [idle2], [idle2]
                for q, keys, vals, ch, p, o, bias, sink in items[x::3]:
                    n = keys[-1][2]
                    if bias and bias[0] == "dram":
                        bb.ready = [P.dma("sync", bb.ap[:, 0:256], bias[1], f"nab{x}", [bb.free, idle2]), zero]
                    for ap, c0, c1 in keys:
                        t = mm(sp[:, c0:c1], q, ap, after=[k_ready, r_rope if lat else [], B0.free, B1.free])
                    yield
                    mx, nmx, sm_, rc, es = [st[:, j:j + 1] for j in range(5)]
                    if bias:
                        mk = bb.ap if bias[0] == "dram" else bias[1]
                        init = -3e38 if sink is None else sink
                        w = P.op("vector", lambda e, mk=mk, n=n, init=init: e.tensor_tensor_reduce(
                            S[:, 0:n], sp[:, 0:n], mk, 1.0, init, ALU.add, ALU.max, mx),
                            [t, bb.ready, ldm, ld_c, s_done])
                        if bias[0] == "dram":
                            bb.free = [w]
                        src = S[:, 0:n]
                        B0.free, B1.free = [w], [w]
                    else:
                        w = P.op("vector", lambda e, n=n: e.tensor_reduce(mx, sp[:, 0:n], AX.X, ALU.max), [t, s_done])
                        if sink is not None:
                            w = tt(mx, mx, sink, ALU.max, [w, ld_c])
                        src = sp[:, 0:n]
                    w = ts(nmx, mx, -1.0, ALU.mult, [w])
                    ex = act(S[:, 0:n], src, ACT.Exp, [w, s_done], bias=nmx, accum=sm_)
                    if not bias:
                        B0.free, B1.free = [ex], [ex]
                    if sink is not None:
                        e2 = act(es, sink, ACT.Exp, [w, ld_c], bias=nmx)
                        w = tt(sm_, sm_, es, ALU.add, [ex, e2])
                    else:
                        w = ex
                    w = P.op("vector", lambda e: e.reciprocal(rc, sm_), [w])
                    w = ts(S[:, 0:n], S[:, 0:n], rc, ALU.mult, [w, ex])
                    yield
                    for j in range(n // 128):
                        t = tr(sp[:, 128 * j:128 * j + 128], S[:, 128 * j:128 * j + 128], ident, [w, B0.free, B1.free])
                    s_done = [t]
                    n0 = min(n, 512)
                    e1 = act(PT[:, 0:n0], sp[:, 0:n0], ACT.Copy, [t, pt_done])
                    B0.free = [e1]
                    pe = [e1]
                    if n > 512:
                        e2 = copy(PT[:, 512:n], sp[:, 512:n], [t, pt_done])
                        B1.free = [e2]
                        pe.append(e2)
                    yield
                    for j, va in enumerate(vals):
                        t = mm(sp[hs[p], 0:128], va, PT[:, 128 * j:128 * j + 128], j == 0, j == len(vals) - 1,
                               [pe, vt, B0.free])
                    pt_done = [t]
                    hi, lo = hin[ch]
                    src = sp[hs[p], 0:128]
                    if lat and ch < 5:
                        src = src.rearrange("p (r c) -> p r c", r=8)
                    a = act(o(hi.ap), src, ACT.Copy, [t, hi.free])
                    b = tt(o(lo.ap), src, o(hi.ap).bitcast(F32), ALU.subtract, [a, lo.free])
                    B0.free = [b]
                    hi.ready.append(a)
                    lo.ready.append(b)
                    yield

            live = [pipe(x) for x in range(3)]
            while live:
                for g in list(live):
                    try:
                        next(g)
                    except StopIteration:
                        live.remove(g)
                yield

        def rope():
            rt = buf("rope", [T])
            done, out = [], []
            cos, sin = c2[:, COS:COS + T], c2[:, SIN:SIN + T]
            g8 = Ring(bank[4:8])
            for x, key in [(sq_[:, 0], "sq0"), (sq_[:, 1], "sq1"), (sq_[:, 2], "sq2"), (sk[:], "sk")]:
                b = g8.next()
                t = mm(b.ap, c2[:, PERM:PERM + 128], x, after=[ready[key], b.free, c2_ready])
                w = tt(rt[:], b.ap, sin, ALU.mult, [t, done, idle])
                b.done(w)
                w2 = tt(x, x, cos, ALU.mult, [t], eng="gpsimd")
                w = tt(x, x, rt[:], ALU.add, [w, w2])
                done = [w]
                out.append(w)
                yield
            return out
        m.attention = attention
        return m

    def acopy(out, in_, after=()):
        return act(out, in_, ACT.Copy, after)

    def out_units(l, v, N, pairs, x, nrm, ring):
        def evac(o):
            def run(bks, done):
                w = stt(x[o].ap, bks[0].ap[:, 0:N], modv(l, v, 16 + o), x[o].ap, ALU.mult, ALU.add,
                        [done, x[o].ready, mod_ready[l]])
                bks[0].done(w)
                x[o].ready = [w]
                nrm.add(o, [w])
            return run
        return [Unit(io["w_out2"][l * 8 + o], lambda: whole(pairs), evac(o), ring) for o in range(8)]

    def ffn_units(l, v, N, pairs, x, nrm, kb, ring, after):
        z, nm = N / 256, f"f{v}{l}"
        hid_hi, hid_lo = sb(nm + "hi", kb, [HALF, N], F32R), sb(nm + "lo", kb + HALF * z, [HALF, N], F32R)
        hid = [(Cell(hid_hi[:, k]), Cell(hid_lo[:, k])) for k in range(HALF)]
        sg = Ring([Cell(sb(f"{nm}sg{i}", kb + 2 * HALF * z + z * i, [N])) for i in range(2)])
        held = {}
        units = []

        def gate(k):
            def run(bks, done):
                c = held[k] = sg.next()
                a = act(c.ap[:], bks[0].ap[:, 0:N], ACT.Silu, [done, c.free, after])
                bks[0].done(a)
                c.ready = [a]
            return run

        def up(k):
            def run(bks, done):
                c = held.pop(k)
                hi, lo = hid[k % HALF]
                w = tt(c.ap[:], bks[0].ap[:, 0:N], c.ap[:], ALU.mult, [done, c.ready])
                bks[0].done(w)
                a = act(hi.ap, c.ap[:], ACT.Copy, [w, hi.free, after])
                b = tt(lo.ap, c.ap[:], hi.ap.bitcast(F32), ALU.subtract, [a, lo.free, after])
                c.done(b)
                hi.ready, lo.ready = [a], [b]
            return run

        def down_groups(s):
            def run():
                out = []
                for b in range(8 * s, 8 * s + 8):
                    o, k = divmod(b, HALF)
                    if not out or out[-1][0] != (nm, o):
                        out.append([(nm, o), [], k == 0, False])
                    out[-1][1].append(hid[k])
                    out[-1][3] = k == HALF - 1
                return out
            return run

        def down(half, s):
            ends = [b // HALF for b in range(8 * s, 8 * s + 8) if b % HALF == HALF - 1]

            def run(bks, done):
                for o, bk, t in zip(ends, bks, done):
                    w = stt(x[o].ap, bk.ap[:, 0:N], modv(l, v, 40 + o), x[o].ap, ALU.mult, ALU.add, [t, x[o].ready])
                    bk.done(w)
                    x[o].ready = [w]
                    if half:
                        nrm.add(o, [w])
            return run

        for half in range(2):
            for k in range(HALF * half, HALF * half + HALF):
                units.append(Unit(io["w_gate2"][l * 22 + k], lambda: whole(pairs), gate(k), ring))
                units.append(Unit(io["w_up2"][l * 22 + k], lambda: whole(pairs), up(k), ring))
            for s in range(HALF):
                units.append(Unit(io["w_down2"][(l * 2 + half) * HALF + s], down_groups(s), down(half, s), ring))
        return units

    TC = 256
    xct = sb("xct", M0 + 12, [KC, TC])
    xc = [Cell(xct[:, c, :]) for c in range(KC)]
    hct = [sb("hchi", M0 + 20, [KC, TC], F32R), sb("hclo", M0 + 28, [KC, TC], F32R)]
    hc = [(Cell(hct[0][:, c]), Cell(hct[1][:, c])) for c in range(KC)]
    hl = list(zip(hhi, hlo))
    CB = M0 + 36
    cnorm = Norm("cn", CB + 50, TC, xc, late_banks)
    idle_c, idle_l = [[], []], [[], []]
    cm = [make_mixer(l, 1, TC, CB, hc, l == 0, idle_c[l]) for l in range(2)]
    lm = [make_mixer(l, 0, T, M0 + 12, hl, True, idle_l[l]) for l in range(2)]
    after_c, after_l = [], [[], []]
    u_cout = out_units(0, 1, TC, hc, xc, cnorm, late_banks)
    u_cffn = ffn_units(0, 1, TC, hc, xc, cnorm, CB, late_banks, after_c)
    u_lout = [out_units(l, 0, T, hl, xr, norm, late_banks) for l in range(2)]
    u_lffn = [ffn_units(l, 0, T, hl, xr, norm, M0 + 12, late_banks, after_l[l]) for l in range(2)]
    spine += u_dn + u_da + u_z + u_merge + u_out + mod_units
    spine += cm[0].units + u_cout + u_cffn + cm[1].units + u_wq + u_peer
    for l in range(2):
        spine += lm[l].units + u_lout[l] + u_lffn[l]

    def mixers(m):
        g = m.gla()
        run_spine(len(m.units), [g])
        m.proj_done = True
        drain(g)
        if m.v:
            drain(m.store_ctx())
        if m.full:
            drain(m.attention())

    def load_c2(after):
        c2_ready[:] = [P.dma("sync", c2[:], io["consts2"], "c2", after)]

    first_norm()
    start_conv([c.ready for c in hlo])
    run_spine(13, [])
    sides = [delta(), dilated()]
    run_spine(36, sides)
    run_spine(4, sides)
    for s in sides:
        drain(s)
    chain_end = [S_ready, o_ready]
    for c in range(KC):
        xr[c].ready = [P.dma("sync", xr[c].ap, io["xT"][:, c, :], f"x{c}", [chain_end] + [a.ready for a in odn_c[3]])]
    sides = [finish_mixers(chain_end)]
    run_spine(2, sides)
    for s in sides:
        drain(s)
    run_spine(22, [])
    run_spine(8, [])
    norm.rs()

    start_mod()
    idle_c[0] += flat(xr[7].ready)
    load_c2(idle_c[0])
    for c in range(KC):
        xc[c].ready = [P.dma("sync", xc[c].ap, io["ctxT"][:, c, :], f"x{c}", idle_c[0])]
        cnorm.add(c, xc[c].ready, idle_c[0])
    run_spine(len(mod_units), [])
    if until == "mod":
        P.emit(sem_of)
        return locals()
    cnorm.apply(lambda c: amod[:, 0, 1, 0, c:c + 1], hc, lambda c: modv(0, 1, c))
    mixers(cm[0])
    if until == "ctx0y":
        P.emit(sem_of)
        return locals()
    run_spine(8, [])
    after_c += flat(xc[7].ready)
    cnorm.apply(lambda c: amod[:, 0, 1, 1, c:c + 1], hc, lambda c: modv(0, 1, 24 + c))
    run_spine(len(u_cffn), [])
    if until == "ctx0":
        P.emit(sem_of)
        return locals()
    cnorm.apply(lambda c: amod[:, 1, 1, 0, c:c + 1], hc, lambda c: modv(1, 1, c))
    idle_c[1] += flat([xc[7].ready, res_written[0]])
    mixers(cm[1])
    norm.apply(lambda c: cv(G_FFN + c), hl)
    key_idle += flat([res_written, [n.free for p in hc for n in p]])
    run_spine(16, [])
    drain(top_keys())
    drain(dense_gates())
    load_gates(0)
    load_gates(1)
    run_spine(GJ, [])
    for g in range(NGR):
        run_spine(16 if g + 1 < NGR else 8, [])
        if g + 2 < NGR:
            load_gates(g + 2)
    rs = norm.rs()
    for c in range(KC):
        w = stt(xr[c].ap, xr[c].ap, cv(G_FIN + c), norm.r[:], ALU.mult, ALU.mult, [rs, xr[c].ready])
        xr[c].ready = [w]
        norm.used = [w]
        norm.add(c, [w])
    if until == "x1":
        P.emit(sem_of)
        return locals()
    load_c2(xr[7].ready)
    for l in range(2):
        idle_l[l] += flat(xr[7].ready)
        norm.apply(lambda c: amod[:, l, 0, 0, c:c + 1], hl, lambda c: modv(l, 0, c))
        mixers(lm[l])
        if until == f"lat{l}y":
            P.emit(sem_of)
            return locals()
        run_spine(8, [])
        after_l[l] += flat(xr[7].ready)
        norm.apply(lambda c: amod[:, l, 0, 1, c:c + 1], hl, lambda c: modv(l, 0, 24 + c))
        run_spine(len(u_lffn[l]), [])
        if until == f"lat{l}":
            P.emit(sem_of)
            return locals()
    rs = norm.rs()
    for c in range(KC):
        w = stt(xr[c].ap, xr[c].ap, cv(N2FIN + c), norm.r[:], ALU.mult, ALU.mult, [rs, xr[c].ready])
        P.dma("sync", io["out"][:, c, :], xr[c].ap, f"x{c}", [w])
    P.emit(sem_of)
    return locals()


def constants(a):
    c = np.zeros((128, NCONST), np.float32)
    i = np.arange(128)
    c[:, IDENT:IDENT + 128] = np.eye(128)
    c[:, UF:UF + 128] = i[:, None] <= i[None, :]
    c[:, UB:UB + 128] = i[:, None] >= i[None, :]
    c[:, MASKF:MASKF + 128] = np.where(i[None, :] <= i[:, None], 0.0, NEG)
    c[:, MASKB:MASKB + 128] = np.where(i[None, :] >= i[:, None], 0.0, NEG)

    def cols(v):
        return v.reshape(-1, 128).T
    c[:, G_MIX:G_MIX + 8] = cols(a["norm_mix"][0])
    c[:, G_FFN:G_FFN + 8] = cols(a["norm_ffn"][0])
    c[:, G_FIN:G_FIN + 8] = cols(a["norm_final"])
    c[:, CONVW:CONVW + 48] = a["dn_conv"][0].reshape(4, 12, 128).transpose(2, 1, 0).reshape(128, 48)
    c[:, DTB:DTB + 8] = a["dn_dt_bias"][0].reshape(1, 8)
    c[:, ALOG:ALOG + 8] = a["dn_a_log"][0].reshape(1, 8)
    for l in range(2):
        c[:, BMOD + 48 * l:BMOD + 48 * l + 48] = cols(a["b_mod_2"][l])
        c[:, N2MIX + 8 * l:N2MIX + 8 * l + 8] = cols(a["norm_mix_2"][l])
        c[:, N2FFN + 8 * l:N2FFN + 8 * l + 8] = cols(a["norm_ffn_2"][l])
        c[:, GBA + 4 * l:GBA + 4 * l + 2] = cols(a["gla_ba_f_2"][l])
        c[:, GBA + 4 * l + 2:GBA + 4 * l + 4] = cols(a["gla_ba_b_2"][l])
        c[:, GNORM + 2 * l:GNORM + 2 * l + 2] = cols(a["gla_norm_2"][l])
        c[:, SINK + 6 * l:SINK + 6 * l + 6] = a["swa_sink_2"][l][None, :]
    c[:, N2FIN:N2FIN + 8] = cols(a["final_norm_2"])
    c[:, CVEC:CVEC + 8] = cols(a["c_2"][0])
    c[:, CVEC + 8:CVEC + 16] = cols(a["c_ctx_2"])
    c[:, IOTA:IOTA + 128] = i[None, :]
    c[:, ONORM:ONORM + 1] = a["dn_out_norm"][0][:, None]
    return c


def level_masks():
    i = np.arange(128)
    out = np.zeros((128, 2, len(LEVELS), 128), np.float32)
    for n, b in enumerate(LEVELS):
        same = (i[:, None] // (2 * b)) == (i[None, :] // (2 * b))
        lower = same & ((i[:, None] // b) % 2 == 1) & ((i[None, :] // b) % 2 == 0)
        out[:, 0, n], out[:, 1, n] = lower, lower.T
    return out


def slabs(w):
    k, n = w.shape
    pad = -n % 128
    if pad:
        w = np.concatenate([w, np.zeros((k, pad), w.dtype)], axis=1)
    return np.ascontiguousarray(w.reshape(k // 128, 128, -1, 128).transpose(2, 1, 0, 3).reshape(-1, 128, k))


def feature_major(x):
    t, d = x.shape
    return np.ascontiguousarray(x.reshape(t, d // 128, 128).transpose(2, 1, 0))


def t5_bucket(rel):
    n = np.abs(rel)
    large = 8 + (np.log(np.maximum(n, 1) / 8) / np.log(1024 / 8) * 8).astype(np.int64)
    large = np.minimum(large, 15)
    return np.where(rel > 0, 16, 0) + np.where(n < 8, n, large)


def dilated_bias(rel_bias):
    l = np.arange(128)
    out = np.zeros((4, 4, 128, 768), np.float32)
    for r in range(4):
        q = (4 * l + r)[:, None]
        k0 = (4 * l[None, :] + np.arange(4)[:, None]).reshape(1, -1)
        k1 = (4 * l + r)[None, :]
        for g, (k, col) in enumerate(((k0, 0), (k1, 512), (k1, 640))):
            rel = k - q
            valid = (np.abs(rel) <= 64, np.abs(rel) <= 256, rel % 16 == 0)[g]
            b = t5_bucket(rel)
            for h in range(4):
                out[h, r, :, col:col + k.shape[1]] = np.where(valid, rel_bias[b, 4 * g + h], np.float32(NEG))
    return out


def constants2():
    c = np.zeros((128, NC2), np.float32)
    t = np.arange(T, dtype=np.int32)
    f32 = np.float32
    inv = (f32(10000.0) ** (-np.arange(16, dtype=f32) / f32(16))).astype(f32)
    ang = np.concatenate([(t // 64).astype(f32)[:, None] * inv, (t % 64).astype(f32)[:, None] * inv], axis=1)
    p = np.arange(128)
    c[:, COS:COS + T] = np.cos(ang).T[p % 32]
    c[:, SIN:SIN + T] = np.sin(ang).T[p % 32] * np.where(p % 64 < 32, -1.0, 1.0)[:, None]
    c[:, PERM:PERM + 128] = (p[:, None] ^ 32) == p[None, :]
    c[:, RSTF:RSTF + T] = t % 64 != 0
    c[:, RSTB:RSTB + T] = t % 64 != 63
    same = (p[:, None] // 64) == (p[None, :] // 64)
    c[:, ONESBD:ONESBD + 128] = same
    c[:, BMASK:BMASK + 128] = same
    return c


def tri_masks():
    p = np.arange(128)
    same = (p[:, None] // 64) == (p[None, :] // 64)
    out = np.zeros((128, 2, 128), np.float32)
    out[:, 0], out[:, 1] = same & (p[:, None] <= p[None, :]), same & (p[:, None] >= p[None, :])
    return out


def window_masks():
    q, k = np.arange(128)[:, None], np.arange(128)[None, :]
    left, right = np.where(k >= q, 0.0, NEG), np.where(k <= q, 0.0, NEG)
    z = np.zeros((128, 128))
    return np.concatenate([left, z, right, z, z, left, z, z, z], axis=1).astype(np.float32)


def grid_bias(rpb):
    out = np.zeros((2, 6, 4, 128, 256), np.float32)
    qr, qc = np.divmod(np.arange(128), 16)
    k = np.arange(256)
    kr, kc = 4 * (k // 128) + k % 4, (k % 128) // 4
    for b in range(4):
        col = kc + min(max(16 * b - 8, 0), 32)
        qcol = qc + 16 * b
        start = np.clip(qcol - 8, 0, 48)[:, None]
        valid = (col[None, :] >= start) & (col[None, :] < start + 16)
        dr = kr[None, :] - qr[:, None] + 7
        dc = np.clip(col[None, :] - qcol[:, None] + 15, 0, 30)
        out[:, :, b] = np.where(valid[None, None], rpb[:, :, dr, dc], np.float32(NEG))
    return out


def decay_weights(wf, wb):
    out = np.zeros((2, 128, 2, 256), np.float32)
    out[:, 0:16, 0], out[:, 16:32, 1] = wf, wb
    return out.reshape(2, 128, 512)


SWA_ORDER = np.concatenate([np.arange(64) + 64 * h for h in (0, 3, 1, 4, 2, 5)])


def in_slabs(w):
    w = np.concatenate([w[:, :1056], np.zeros((D, 96), w.dtype), w[:, 1056:2208], w[:, 2208 + SWA_ORDER], w[:, 2592:]],
                       axis=1)
    return slabs(w)


def down_slabs(w):
    w = w.reshape(2, HALF, 128, 8, 128).transpose(0, 3, 1, 2, 4).reshape(2, HALF, 8, 128, 128)
    return w.transpose(0, 1, 3, 2, 4).reshape(2 * HALF, 128, 1024)


def two(f, w):
    return np.ascontiguousarray(np.concatenate([f(w[0]), f(w[1])], axis=0))


def layout(a):
    w = a["w_in"][0]
    w = np.concatenate([w[:, :2048], w[:, 2048:2064], np.zeros((D, 112), w.dtype), w[:, 2064:]], axis=1)
    return {"consts": constants(a), "masks": np.concatenate([level_masks().reshape(128, -1), tri_masks().reshape(128, -1)], axis=1), "xT": feature_major(a["x"][0]), "w_in": slabs(w),
            "da_bias": dilated_bias(a["rel_bias"]),
            "w_br": np.concatenate([slabs(a["w_branch_dn"][0]), slabs(a["w_branch_da"][0])], axis=2),
            "w_out": slabs(a["w_out"][0]),
            "peer_wq": slabs(a["peer_wq"][0]),
            "peer_keys": np.ascontiguousarray(a["peer_sub_keys"][0].reshape(16, 128, 128).transpose(2, 0, 1)),
            "peer_u": np.ascontiguousarray(a["peer_u"][0].reshape(128, 128, 8, 128).transpose(1, 3, 2, 0)
                                           .reshape(128, 128, 1024)),
            "peer_v": np.ascontiguousarray(a["peer_v"][0].reshape(128, 16, 8, 8, 128).transpose(1, 3, 0, 2, 4)
                                           .reshape(128, 128, 1024)),
            "consts2": constants2(),
            "swa_mask": window_masks(),
            "na_bias": grid_bias(a["na_rpb_2"]),
            "wa2": decay_weights(a["gla_wa2_f_2"], a["gla_wa2_b_2"]),
            "ctxT": feature_major(a["ctx_2"][0]),
            "w_mod": np.ascontiguousarray(a["w_mod_2"].reshape(2, 8, 128, 6, 1024).transpose(0, 3, 1, 2, 4)
                                          .reshape(96, 128, 1024)),
            "w_in2": two(in_slabs, a["w_in_2"]),
            "w_out2": two(slabs, np.concatenate([a["w_out_2"][:, :640], a["w_out_2"][:, 640 + SWA_ORDER]], axis=1)),
            "w_gate2": two(slabs, a["w_gate_2"]),
            "w_up2": two(slabs, a["w_up_2"]),
            "w_down2": two(down_slabs, a["w_down_2"])}


def _build(nc, arrays):
    io = {n: nc.dram_tensor(n, v.shape, mybir.dt.from_np(v.dtype), kind="ExternalInput").ap() for n, v in arrays.items()}
    io["out"] = nc.dram_tensor("out_0_dram", (128, KC, T), F32, kind="ExternalOutput").ap()
    program(nc, io)


def kernel(**inputs):
    import concourse.bacc as _bacc
    from concourse.bass_utils import run_bass_kernel_spmd as _run

    arrays = layout({n: np.ascontiguousarray(v) for n, v in inputs.items()})
    nc = _bacc.Bacc("TRN2", target_bir_lowering=False, num_devices=1)
    _build(nc, arrays)
    r = _run(nc, [arrays], core_ids=[0])
    out = np.asarray(r.results[0]["out_0_dram"])
    return np.ascontiguousarray(out.transpose(2, 1, 0).reshape(1, T, D))
```

```python
import numpy as np
import concourse.bass as bass
from concourse import mybir

F32 = mybir.dt.float32
F32R = mybir.dt.float32r
U8 = mybir.dt.uint8
U32 = mybir.dt.uint32
I32 = mybir.dt.int32
ALU = mybir.AluOpType
ACT = mybir.ActivationFunctionType
AX = mybir.AxisListType

T = 512
TD = 384
D = 1024
KC = 8
EPS = 1e-6
NEG = -1e30

IDENT, UF, UB, MASKF, MASKB = 0, 128, 256, 384, 512
G_MIX, G_FFN, G_FIN = 640, 648, 656
CONVW = 664
DTB, ALOG, ONORM = 712, 720, 728
IOTA = 736
BMOD, N2MIX, N2FFN, N2FIN = 864, 960, 976, 992
CVEC, GBA, GNORM, SINK = 1000, 1016, 1024, 1028
NCONST = 1040
COS, SIN, PERM, RSTF, RSTB, ONESBD, BMASK = 0, 512, 1024, 1152, 1664, 2176, 2304
NC2, NC2C = 2432, 768
HALF = 11
LEVELS = (1, 2, 4, 8, 16, 32, 64)


class Op:
    __slots__ = ("eng", "fn", "after", "asked", "sem", "count", "end")

    def __init__(self, eng, fn, after):
        self.eng, self.fn, self.after = eng, fn, after
        self.asked, self.sem, self.count, self.end = False, None, 0, 0


def flat(x):
    if x is None:
        return []
    if isinstance(x, Op):
        return [x]
    out = []
    for y in x:
        out += flat(y)
    return out


class Plan:

    def __init__(self, nc):
        self.nc = nc
        self.queues = {e: [] for e in ("tensor", "vector", "scalar", "gpsimd", "sync")}
        self.dmas = []
        self.dma_counts = {}
        self.clock = {e: 0 for e in self.queues}
        self.clock["dma"] = 0

    def op(self, eng, fn, after=(), cost=200):
        o = Op(eng, fn, flat(after))
        start = self.clock[eng]
        for a in o.after:
            a.asked = True
            if eng != "tensor" or a.eng != eng:
                start = max(start, a.end + (200 if a.eng == "tensor" else 130))
        o.end = self.clock[eng] = start + cost
        self.queues[eng].append(o)
        return o

    def dma(self, eng, out, in_, sem, after=()):
        return self.counted(self.op(eng, lambda e: e.dma_start(out, in_), after, 60), sem, width(out))

    def counted(self, o, sem, size):
        self.clock["dma"] = max(self.clock["dma"], o.end) + 4 * 128 * size / DMA_RATE
        o.end = self.clock["dma"] + 2000
        n = self.dma_counts.get(sem, 0) + 16
        self.dma_counts[sem] = n
        o.sem, o.count = sem, n
        self.dmas.append(o)
        return o

    def gather(self, out, table, rows, sem, after=()):
        o = self.op("gpsimd", lambda e: e.indirect_dma_start(out, None, table, bass.IndirectOffsetOnAxis(ap=rows, axis=0)),
                    after, 1040)
        return self.counted(o, sem, width(out))

    def emit(self, sem_of):
        for eng, queue in self.queues.items():
            n = 0
            for o in queue:
                if o.sem is None and o.asked:
                    n += 1
                    o.sem, o.count = eng, n
        with self.nc.Block() as block:
            for eng, queue in self.queues.items():
                getter = {"tensor": block.tensor, "vector": block.vector, "scalar": block.scalar,
                          "gpsimd": block.gpsimd, "sync": block.sync}[eng]
                getter(self.body(eng, queue, sem_of))

    def body(self, eng, queue, sem_of):
        def run(e):
            seen = {}
            for o in queue:
                need = {}
                for a in o.after:
                    need[a.sem] = max(need.get(a.sem, 0), a.count)
                for sem, count in need.items():
                    if seen.get(sem, 0) < count:
                        e.wait_ge(sem_of(sem), count)
                        seen[sem] = count
                ins = o.fn(e)
                if o.sem is not None:
                    ins.then_inc(sem_of(o.sem), 16 if o.sem != eng else 1)
            if eng == "sync":
                for sem, count in self.dma_counts.items():
                    if seen.get(sem, 0) < count:
                        e.wait_ge(sem_of(sem), count)
        return run


def width(ap):
    n = 1
    for x in ap.shape[1:]:
        n *= x
    return n


POLL = "come back later"
DMA_RATE = 300


class Side:

    def __init__(self, gen, lag=1.0):
        self.gen, self.want, self.alive, self.polled, self.lag = gen, [], True, -1, lag

    def step(self):
        try:
            w = next(self.gen)
        except StopIteration:
            self.alive, self.want = False, []
            return
        self.want = POLL if w is POLL else flat(w)


class Cell:

    def __init__(self, ap):
        self.ap, self.ready, self.free, self.held = ap, [], [], False

    def done(self, *readers):
        self.free, self.held = flat(readers), False


class Ring:
    def __init__(self, cells):
        self.cells, self.n = cells, 0

    def next(self):
        for _ in self.cells:
            c = self.cells[self.n % len(self.cells)]
            self.n += 1
            if not c.held:
                c.held = True
                return c
        raise AssertionError("every cell is in use")


def program(nc, io, until=None):
    P = Plan(nc)
    sems = {}

    def sem_of(name):
        if name not in sems:
            sems[name] = nc.alloc_semaphore("s_" + name)
        return sems[name]

    BASE = 16512

    def sb(name, kb, shape, dt=F32):
        return nc.alloc_sbuf_tensor_at(name, [128] + list(shape), dt, offset=BASE + int(kb * 1024))

    psum = nc.alloc_psum_tensor("ps", [128, 8, 512], F32)
    bank = [Cell(psum[:, i, :]) for i in range(8)]

    def mm(out, lhsT, rhs, start=True, stop=True, after=(), at=None):
        cost = max(0.43 * width(rhs), 106) if rhs.dtype == F32R else max(1.67 * width(rhs), 112) * (1 if at is None else 0.27)
        if at is None:
            return P.op("tensor", lambda e: e.matmul(out, lhsT, rhs, start=start, stop=stop), after, cost)
        return P.op("tensor", lambda e: e.matmul(out, lhsT, rhs, start=start, stop=stop, tile_position=at), after, cost)

    def tr(out, in_, idn, after=()):
        return P.op("tensor", lambda e: e.transpose(out, in_, idn), after, 145)

    tables = {ACT.Exp: 0, ACT.Ln: 4, ACT.Silu: 1, ACT.Sigmoid: 2, ACT.Gelu_apprx_tanh: 3}
    table = [0]

    def act(out, in_, func, after=(), bias=0.0, scale=1.0, accum=None):
        cost = 60 + 0.87 * width(in_) + (0 if accum is None else 280)
        if tables.get(func, table[0]) != table[0]:
            table[0] = tables[func]
            cost += 1280
        if accum is None:
            return P.op("scalar", lambda e: e.activation(out, in_, func, bias=bias, scale=scale), after, cost)
        return P.op("scalar", lambda e: e.activation(out, in_, func, bias=bias, scale=scale, accum_out=accum), after,
                    cost)

    def elementwise(eng, ap):
        return 65 + 1.05 * width(ap) if eng == "vector" else 100 + 2 * width(ap)

    def dve(fn, after, n):
        return P.op("vector", fn, after, 65 + 1.05 * n)

    def tt(out, a, b, op, after=(), eng="vector"):
        return P.op(eng, lambda e: e.tensor_tensor(out, a, b, op), after, elementwise(eng, out))

    def ts(out, a, s1, op0, after=(), s2=None, op1=None, eng="vector"):
        if op1 is None:
            return P.op(eng, lambda e: e.tensor_scalar(out, a, s1, None, op0), after, elementwise(eng, out))
        return P.op(eng, lambda e: e.tensor_scalar(out, a, s1, s2, op0, op1), after, elementwise(eng, out))

    def stt(out, a, s, b, op0, op1, after=()):
        return P.op("vector", lambda e: e.scalar_tensor_tensor(out, a, s, b, op0, op1), after,
                    elementwise("vector", out))

    def copy(out, in_, after=(), eng="vector"):
        return P.op(eng, lambda e: e.tensor_copy(out, in_), after, elementwise(eng, out))

    def memset(ap, v, after=(), eng="gpsimd"):
        return P.op(eng, lambda e: e.memset(ap, v), after, elementwise(eng, ap))

    def cpred(out, mask, data, after=()):
        return P.op("vector", lambda e: e.copy_predicated(out, mask, data), after, elementwise("vector", out))

    def heads(ap):
        return ap.rearrange("p (h f) -> p h f", h=4)

    def along(col, n=128):
        return col.unsqueeze(2).broadcast_to([128, col.shape[1], n])

    def over(mat, n=4):
        return mat.unsqueeze(1).broadcast_to([128, n, mat.shape[1]])

    cst = sb("cst", 0, [NCONST])
    lvl = sb("lvl", 5, [2, len(LEVELS), 128], U8)
    tri = sb("tri", 6.75, [2, 128], U8)
    ones = sb("ones", 7, [128])
    mod = sb("mod", 7.5, [2, 2, 48])
    amod = sb("amod", 8.25, [2, 2, 2, 8])
    mask_in = sb("mask_in", 137, [2048])
    ld_c = P.dma("sync", cst[:], io["consts"], "cst")
    ld_m = P.dma("sync", mask_in[:], io["masks"], "masks")
    ld_c = [ld_c, copy(lvl[:].rearrange("p d l f -> p (d l f)"), mask_in[:, 0:1792], [ld_m]),
            copy(tri[:].rearrange("p d f -> p (d f)"), mask_in[:, 1792:2048], [ld_m])]
    w_ones = memset(ones[:], 1.0)
    ident = cst[:, IDENT:IDENT + 128]
    nsink = sb("nsink", 4.125, [12])
    nsink_ready = ts(nsink[:], cst[:, SINK:SINK + 12], -1.0, ALU.mult, ld_c)

    def cv(off, n=1):
        return cst[:, off:off + n]

    NRAW, NW, LOOK = 4, 3, 2
    raw = [Cell(sb(f"raw{i}", 9 + 4 * i, [1024])) for i in range(NRAW)]
    whi = [Cell(sb(f"whi{i}", 25 + 4 * i, [1024], F32R)) for i in range(NW)]
    wlo = [Cell(sb(f"wlo{i}", 37 + 4 * i, [1024], F32R)) for i in range(NW)]
    hhi_t, hlo_t = sb("hhi", 49, [KC, T], F32R), sb("hlo", 65, [KC, T], F32R)
    hhi = [Cell(hhi_t[:, c, :]) for c in range(KC)]
    hlo = [Cell(hlo_t[:, c, :]) for c in range(KC)]

    spine = []
    u_dn, u_da, u_z, u_merge, u_out, u_wq, u_peer = [], [], [], [], [], [], []

    class Unit:

        def __init__(self, slab, groups, evac, ring=None, split=True, lo="vector"):
            self.slab, self.groups, self.evac, self.ring, self.split, self.lo = slab, groups, evac, ring, split, lo
            self.guard, self.each = None, False

    state = {"loaded": 0, "split": 0, "unit": 0, "tick": 0}
    spine_banks = Ring(bank[0:2])
    spent, parts = set(), {}
    open_banks = {}

    def load_to(n):
        while state["loaded"] < min(n, len(spine)):
            i = state["loaded"]
            if i >= NRAW and i - NRAW not in spent:
                return
            c = raw[i % NRAW]
            c.ready = [P.dma("sync", c.ap[:], spine[i].slab, f"raw{i % NRAW}", c.free)]
            state["loaded"] += 1

    def raw_done(i, readers):
        raw[i % NRAW].free = readers
        spent.add(i)
        load_to(i + 1 + NRAW)

    def split_next():
        i = state["split"]
        load_to(i + 1)
        if i >= state["loaded"]:
            return False
        state["split"] += 1
        if spine[i].split:
            n = len(parts)
            r, hi, lo = raw[i % NRAW], whi[n % NW], wlo[n % NW]
            parts[i] = (hi, lo)
            a = act(hi.ap[:], r.ap[:], ACT.Copy, [r.ready, hi.free])
            eng = spine[i].lo
            if eng == "any":
                eng = "gpsimd" if P.clock["gpsimd"] < P.clock["tensor"] + 6000 else "vector"
            b = tt(lo.ap[:], r.ap[:], hi.ap[:].bitcast(F32), ALU.subtract, [r.ready, a, lo.free], eng)
            hi.ready, lo.ready, hi.free, lo.free = [a], [b], [], []
            raw_done(i, [b])
        return True

    def split_ahead(i):
        while sum(n > i for n in parts) < LOOK and split_next():
            pass

    def run_unit(sides):
        i = state["unit"]
        state["unit"] += 1
        u = spine[i]
        while state["split"] <= i:
            assert split_next()
        if not u.split:
            last = u.evac(raw[i % NRAW])
            raw_done(i, [last])
            split_ahead(i)
            return
        hi, lo = parts[i]
        groups, j = [], 0
        for key, pairs, opens, closes in u.groups():
            groups.append((key, pairs, opens, closes, j))
            j += len(pairs)
        banks, lasts, done = [], [], 0
        for part in [[g] for g in groups] if u.each else [groups]:
            for key, pairs, opens, closes, j in part:
                if opens:
                    open_banks[key] = (u.ring or spine_banks).next()
                bk = open_banks[key]
                if sides:
                    yield [hi.ready, pairs[0][0].ready, bk.free if opens else []]
                o = bk.ap[:, 0:pairs[0][0].ap.shape[-1]]
                for n, (xh, xl) in enumerate(pairs):
                    w = hi.ap[:, 128 * j:128 * j + 128]
                    mm(o, w, xh.ap, opens and n == 0, False, [hi.ready, xh.ready, bk.free if opens else []])
                    mm(o, w, xl.ap, False, False, [xl.ready])
                    j += 1
                    done += 1
                    if done == 8:
                        split_ahead(i)
                    if done % 4 == 0:
                        yield lo.ready if done == 8 else []
            for key, pairs, opens, closes, j in part:
                bk = open_banks[key]
                o = bk.ap[:, 0:pairs[0][0].ap.shape[-1]]
                for n, (xh, xl) in enumerate(pairs):
                    last = mm(o, lo.ap[:, 128 * j:128 * j + 128], xh.ap, False, closes and n == len(pairs) - 1,
                              [lo.ready])
                    j += 1
                for xh, xl in pairs:
                    xh.free, xl.free = [last], [last]
                if closes:
                    banks.append(bk)
                    lasts.append(last)
                    del open_banks[key]
            hi.free, lo.free = [last], [last]
            if banks:
                u.evac(banks, lasts)
                banks, lasts = [], []
        yield []

    def whole(*lists):
        return [(n, list(x), True, True) for n, x in enumerate(lists)]

    BACKLOG = {"vector": 3000, "scalar": 3000, "gpsimd": 8000}

    def pump(sides, want):
        moved = True
        while moved:
            moved = False
            for s in list(sides):
                now = P.clock["tensor"]
                if s.want is POLL:
                    if s.polled != state["tick"]:
                        s.polled = state["tick"]
                        s.step()
                elif all(o.end <= now for o in s.want) and \
                        all(P.clock[e] <= now + lag * s.lag for e, lag in BACKLOG.items()):
                    s.step()
                    moved = True
                if not s.alive:
                    sides.remove(s)
            if not moved:
                until = max([0] + [o.end for o in flat(want)])
                ready = [(when(s), n) for n, s in enumerate(sides) if s.want is not POLL]
                if until > P.clock["tensor"] + 300 and ready and min(ready)[0] < until:
                    sides[min(ready)[1]].step()
                    moved = True

    def when(s):
        return max([P.clock[e] - lag * s.lag for e, lag in BACKLOG.items()] + [o.end for o in s.want])

    def run_spine(n, sides):
        while n:
            u = spine[state["unit"]]
            if u.guard:
                drain(sides, u.guard)
            n -= u.split
            for want in run_unit(sides):
                state["tick"] += 1
                pump(sides, want)

    def drain(sides, until=None):
        while sides and not (until and until()):
            state["tick"] += 1
            ready = [s for s in sides if s.want is not POLL]
            if ready:
                min(ready, key=when).step()
            for s in [s for s in sides if s.want is POLL]:
                s.step()
                assert ready or s.want is not POLL, "nothing can go on"
            sides[:] = [s for s in sides if s.alive]

    def split_chunk(h32, c, after):
        a = act(hhi[c].ap, h32, ACT.Copy, [after, hhi[c].free])
        b = tt(hlo[c].ap, h32, hhi[c].ap.bitcast(F32), ALU.subtract, [after, a, hlo[c].free])
        hhi[c].ready, hlo[c].ready = [a], [b]
        hhi[c].free, hlo[c].free = [], []
        return [a, b]

    WK = 81
    xT0 = sb("xT0", WK + 40, [KC, T])
    xc0 = [Cell(xT0[:, c, :]) for c in range(KC)]
    for c in range(KC):
        xc0[c].ready = [P.dma("sync", xc0[c].ap, io["xT"][:, c, :], f"x{c}")]
    sq = Ring([Cell(sb(f"sq{i}", WK + 74 + 2 * i, [T])) for i in range(2)])
    h32 = Ring([Cell(sb(f"h32{i}", WK + 78 + 2 * i, [T])) for i in range(2)])
    rst = sb("rst", WK + 82, [T])

    def first_norm():
        b = bank[2]
        last = None
        for c in range(KC):
            s = sq.next()
            a = act(s.ap[:], xc0[c].ap, ACT.Square, [xc0[c].ready, s.free])
            last = mm(b.ap, ones[:], s.ap[:], c == 0, c == KC - 1, [w_ones, a, b.free])
            s.done(last)
        l = act(rst[:], b.ap, ACT.Ln, [last, ld_c], bias=EPS, scale=1.0 / D)
        b.done(l)
        r = act(rst[:], rst[:], ACT.Exp, [l], scale=-0.5)
        for c in range(KC):
            h = h32.next()
            w = stt(h.ap[:], xc0[c].ap, cv(G_MIX + c), rst[:], ALU.mult, ALU.mult, [r, ld_c, h.free])
            h.done(split_chunk(h.ap[:], c, [w]))
            xc0[c].free = [w]

    qT, kT = sb("qT", WK, [4, T]), sb("kT", WK + 8, [4, T])
    ktok, vtok = sb("ktok", WK + 16, [4, 4, 128]), sb("vtok", WK + 24, [4, 4, 128])
    oacc = sb("oacc", WK + 32, [4, 4, 128])
    vT = sb("vT", WK + 56, [4, T])
    cbuf = Ring([Cell(sb(f"cbuf{i}", WK + 40 + 2.25 * i, [516])) for i in range(2)])
    cacc = Ring([Cell(sb(f"cacc{i}", WK + 45 + 2 * i, [T])) for i in range(2)])
    abT = sb("abT", WK + 68, [T])
    qkv = {"k": [Cell(kT[:, h, :]) for h in range(4)], "q": [Cell(qT[:, h, :]) for h in range(4)],
           "v": [Cell(vT[:, h, :]) for h in range(4)]}
    abc = Cell(abT[:])
    convpad = []

    def start_conv(after):
        for c in cbuf.cells:
            convpad.append(memset(c.ap[:, 0:2], 0.0, after))
            convpad.append(memset(c.ap[:, 514:516], 0.0, after))

    def conv_evac(kind, h):
        col = CONVW + 4 * ({"q": 0, "k": 4, "v": 8}[kind] + h)
        dst = qkv[kind][h]

        def evac(bks, done):
            cb, ca = cbuf.next(), cacc.next()
            a = act(cb.ap[:, 2:514], bks[0].ap, ACT.Copy, [done, cb.free])
            bks[0].done(a)
            o = ts(ca.ap[:], cb.ap[:, 0:T], cv(col), ALU.mult, [a, convpad, ld_c, ca.free])
            for j in range(1, 4):
                o = stt(ca.ap[:], cb.ap[:, j:j + T], cv(col + j), ca.ap[:], ALU.mult, ALU.add, [o])
            cb.done(o)
            s = act(dst.ap, ca.ap[:], ACT.Silu, [o, dst.free])
            ca.done(s)
            dst.ready, dst.free = [s], []
        return evac

    def ab_evac(bks, done):
        a = act(abT[:], bks[0].ap, ACT.Copy, [done])
        bks[0].done(a)
        abc.ready = [a]

    def h_rhs():
        return whole(zip(hhi, hlo))

    for kind in "kqv":
        for h in range(4):
            u_dn.append(Unit(io["w_in"][{"q": 0, "k": 4, "v": 8}[kind] + h], h_rhs, conv_evac(kind, h)))
    u_dn.append(Unit(io["w_in"][16], h_rhs, ab_evac))

    dnbs = [Ring(bank[2:4]), Ring(bank[4:6])]
    dnb = Ring(bank[2:6])
    small = sb("dnsmall", WK + 72, [448])

    def sm(i, n=32):
        return small[:, i:i + n]
    ab_tok, x_, ax_, g_, beta, gc, eg, nbeta, nbeg = (
        sm(0, 64), sm(64), sm(96), sm(128), sm(160), sm(192), sm(224), sm(256), sm(288))
    gl, kdf = [sm(320, 4), sm(324, 4)], [sm(328, 4), sm(332, 4)]
    nea = sm(336, 8)
    CH = WK + 40
    slot = [[sb(f"ch{d}_{i}", CH + 16 * d + 2 * i, [T]) for i in range(8)] for d in range(2)]
    o_ready = [[] for _ in range(4)]
    oda_idle = []
    S_ready = [[], []]

    def dn_prepare():
        sq2 = Ring([Cell(sb(f"sqb{i}", WK + 49 + 2 * i, [T])) for i in range(2)])
        rs2 = sb("rsb", DA + 43, [4, T])
        free = []
        for kind, scale in (("k", 1.0), ("q", 128.0 ** -0.5)):
            ls = []
            for c in qkv[kind]:
                s, b = sq2.next(), dnb.next()
                a = act(s.ap[:], c.ap, ACT.Square, [c.ready, s.free])
                yield [a, b.free]
                m = mm(b.ap, ones[:], s.ap[:], after=[a, b.free, w_ones])
                s.done(m)
                l = act(rs2[:, len(ls)], b.ap, ACT.Ln, [m, free], bias=EPS)
                b.done(l)
                ls.append(l)
            x = act(rs2[:], rs2[:], ACT.Exp, ls, scale=-0.5)
            free = []
            for h, c in enumerate(qkv[kind]):
                w = stt(c.ap, c.ap, scale, rs2[:, h], ALU.mult, ALU.mult, [x])
                c.ready = [w]
                free.append(w)
        oda_idle.extend(free)
        tok = {}
        for kind, dst in (("k", ktok), ("v", vtok)):
            tok[kind] = []
            for n in range(4):
                b = dnb.next()
                yield [b.free, [c.ready for c in qkv[kind]]]
                for h in range(4):
                    m = tr(b.ap[:, 128 * h:128 * h + 128], qkv[kind][h].ap[:, 128 * n:128 * n + 128], ident,
                           [qkv[kind][h].ready, b.free, ld_c])
                w = act(dst[:, n], heads(b.ap), ACT.Copy, [m])
                b.done(w)
                tok[kind].append(w)
        b = dnb.next()
        yield b.free
        for n in range(4):
            m = tr(b.ap[:, 16 * n:16 * n + 16], abT[0:16, 128 * n:128 * n + 128], ident[0:16, 0:16],
                   [abc.ready, b.free])
        w = copy(ab_tok, b.ap[:, 0:64], [m])
        b.done(w)
        ab = ab_tok.rearrange("p (n k d h) -> p k d n h", n=4, k=2, d=2)

        def dnh(ap):
            return ap.rearrange("p (d n h) -> p d n h", d=2, n=4)
        xs = []
        for d in range(2):
            dtb = cv(DTB + 4 * d, 4).unsqueeze(1).broadcast_to([128, 4, 4])
            xs.append(tt(dnh(x_)[:, d], ab[:, 0, d], dtb, ALU.add, [w, ld_c]))
            xs.append(copy(dnh(beta)[:, d], ab[:, 1, d], [w]))
        a1 = act(ax_, x_, ACT.Abs, xs)
        a2 = act(ax_, ax_, ACT.Exp, [a1], scale=-1.0)
        a3 = act(ax_, ax_, ACT.Ln, [a2], bias=1.0)
        s1 = stt(x_, x_, 0.0, ax_, ALU.max, ALU.add, [a3])
        a4 = act(nea, cv(ALOG, 8), ACT.Exp, [ld_c])
        gs = []
        for d in range(2):
            al = nea[:, 4 * d:4 * d + 4].unsqueeze(1).broadcast_to([128, 4, 4])
            gs.append(stt(dnh(g_)[:, d], dnh(x_)[:, d], -1.0, al, ALU.mult, ALU.mult, [s1, a4]))
        a5 = act(beta, beta, ACT.Exp, xs, scale=-1.0)
        b1 = ts(beta, beta, 1.0, ALU.add, [a5])
        b2 = P.op("vector", lambda e: e.reciprocal(beta, beta), [b1])
        b = dnb.next()
        yield [gs, b.free]
        m = mm(b.ap[:, 0:16], cv(UF, 128), g_[:, 0:16], after=[gs, b.free])
        m = mm(b.ap[:, 16:32], cv(UB, 128), g_[:, 16:32])
        w = copy(gc, b.ap[:, 0:32], [m])
        e1 = act(eg, gc, ACT.Exp, [w])
        b.done(w)
        n1 = ts(nbeta, beta, -1.0, ALU.mult, [b2])
        n2 = tt(nbeg, nbeta, eg, ALU.mult, [n1, e1])
        tok["small"] = [n2, n1, w, e1, b2, gs, tok["k"], tok["v"]]
        return tok

    def chain(d, tok):
        B0, B1, B2, B3, B4, B5, B6, S = slot[d]
        U = cv(UF if d == 0 else UB, 128)
        MASK = cv(MASKF if d == 0 else MASKB, 128)
        last = 127 if d == 0 else 0
        free = [[] for _ in range(8)]
        dnb = dnbs[d]
        for step in range(4):
            n = step if d == 0 else 3 - step
            col = 16 * d + 4 * n
            ncol = slice(col, col + 4)
            hs = [slice(128 * h, 128 * h + 128) for h in range(4)]
            tc = slice(128 * n, 128 * n + 128)
            small_ready = tok["small"]
            gu = tt(heads(B5[:]), over(U), along(g_[:, ncol]), ALU.mult, [small_ready, free[5]], eng="gpsimd")
            b = dnb.next()
            yield [gu, b.free]
            m = mm(b.ap, ones[:], B5[:], after=[gu, b.free])
            dd = tt(heads(B0[:]), along(gc[:, ncol]), heads(b.ap), ALU.subtract, [m, free[0]])
            if step < 3:
                kd = tt(kdf[d], heads(b.ap)[:, :, last], gc[:, ncol], ALU.subtract, [m])
                kd2 = act(kdf[d], kdf[d], ACT.Exp, [kd])
                glast = act(gl[d], heads(b.ap)[:, :, last], ACT.Exp, [free[7]])
            eB = act(B6[:], b.ap, ACT.Exp, [dd, kd, free[6]])
            b.done(eB)
            dm = tt(heads(B0[:]), heads(B0[:]), over(MASK), ALU.add, [dd])
            dec = act(B0[:], B0[:], ACT.Exp, [dm])
            qd = tt(heads(B6[:]), qT[:, :, tc], heads(B6[:]), ALU.mult, [eB], eng="gpsimd")
            bk, bq = dnb.next(), dnb.next()
            yield [bk.free, bq.free]
            for h in range(4):
                mk = mm(bk.ap[:, hs[h]], kT[:, h, tc], kT[:, h, tc], after=[bk.free])
            for h in range(4):
                mq = mm(bq.ap[:, hs[h]], qT[:, h, tc], kT[:, h, tc], after=[bq.free])
            k1 = tt(heads(B1[:]), heads(bk.ap), along(nbeta[:, ncol]), ALU.mult, [mk, free[1]])
            nl = tt(B1[:], B1[:], B0[:], ALU.mult, [k1, dec])
            bk.done(k1)
            it = tt(B0[:], bq.ap, B0[:], ALU.mult, [mq, dec, nl])
            bq.done(it)
            vb = tt(heads(B3[:]), vtok[:, n], along(beta[:, ncol]), ALU.mult, [tok["v"], free[3]], eng="gpsimd")
            bn, bi = dnb.next(), dnb.next()
            yield [nl, it, bn.free, bi.free]
            for h in range(4):
                mn = tr(bn.ap[:, hs[h]], B1[:, hs[h]], ident, [nl, bn.free])
            for h in range(4):
                mi = tr(bi.ap[:, hs[h]], B0[:, hs[h]], ident, [it, bi.free])
            nlt = act(B2[:], bn.ap, ACT.Copy, [mn, free[2]])
            bn.done(nlt)
            itT = act(B0[:], bi.ap, ACT.Copy, [mi])
            bi.done(itT)
            x0 = copy(heads(B4[:]), over(ident), [free[4]], eng="gpsimd")
            y0 = copy(heads(B5[:]), over(ident), [m], eng="gpsimd")
            xr = cpred(heads(B4[:]), over(lvl[:, d, 0]), heads(B1[:]), [x0, nl, ld_c])
            yr = cpred(heads(B5[:]), over(lvl[:, 1 - d, 0]), heads(B2[:]), [y0, nlt])
            for i in range(1, 7):
                bt = dnb.next()
                yield [xr, nlt, bt.free]
                for h in range(4):
                    mt = mm(bt.ap[:, hs[h]], B2[:, hs[h]], B4[:, hs[h]], after=[xr, nlt, bt.free])
                ev = act(B1[:], bt.ap, ACT.Copy, [mt, xr])
                bt.done(ev)
                by = dnb.next()
                yield [ev, yr, by.free]
                for h in range(4):
                    my = mm(by.ap[:, hs[h]], B1[:, hs[h]], B5[:, hs[h]], after=[ev, yr, by.free])
                if i < 6:
                    bx = dnb.next()
                    for h in range(4):
                        mx = mm(bx.ap[:, hs[h]], B5[:, hs[h]], B1[:, hs[h]], after=[bx.free])
                    xr = cpred(heads(B4[:]), over(lvl[:, d, i]), heads(bx.ap), [mx])
                    bx.done(xr)
                yr = cpred(heads(B5[:]), over(lvl[:, 1 - d, i]), heads(by.ap), [my, mx])
                by.done(yr)
            kb = tt(heads(B1[:]), ktok[:, n], along(nbeg[:, ncol]), ALU.mult, [tok["k"], my], eng="gpsimd")
            if step < 3:
                kdc = tt(heads(B2[:]), ktok[:, n], along(kdf[d]), ALU.mult, [kd2, mt], eng="gpsimd")
            first = step == 0
            if not first:
                bw = dnb.next()
                yield [kb, yr, bw.free]
                for h in range(4):
                    mw = mm(bw.ap[:, hs[h]], B1[:, hs[h]], B5[:, hs[h]], after=[kb, yr, bw.free])
                wT = act(B4[:], bw.ap, ACT.Copy, [mw, mt])
                bw.done(wT)
            bv = dnb.next()
            yield [vb, yr, bv.free, [] if first else [wT, S_ready[d]]]
            for h in range(4):
                mv = mm(bv.ap[:, hs[h]], B5[:, hs[h]], B3[:, hs[h]], True, first, [vb, yr, bv.free])
                if not first:
                    mv = mm(bv.ap[:, hs[h]], B4[:, hs[h]], S[:, hs[h]], False, True, [wT, S_ready[d]])
            vn = act(B3[:], bv.ap, ACT.Copy, [mv])
            bv.done(vn)
            bo = dnb.next()
            yield [itT, vn, bo.free, [] if first else [qd, S_ready[d]]]
            for h in range(4):
                if not first:
                    mm(bo.ap[:, hs[h]], B6[:, hs[h]], S[:, hs[h]], True, False, [qd, bo.free, S_ready[d]])
                mo = mm(bo.ap[:, hs[h]], B0[:, hs[h]], B3[:, hs[h]], first, True, [itT, vn, bo.free])
            if step < 3:
                bs = dnb.next()
                for h in range(4):
                    ms = mm(bs.ap[:, hs[h]], B2[:, hs[h]], B3[:, hs[h]], after=[kdc, bs.free])
            if not o_ready[n]:
                ow = copy(oacc[:, n], heads(bo.ap), [mo])
            else:
                ow = tt(oacc[:, n], oacc[:, n], heads(bo.ap), ALU.add, [mo, o_ready[n]])
            o_ready[n] = [ow]
            bo.done(ow)
            end = mo
            if step < 3:
                if first:
                    sw = copy(S[:], bs.ap, [ms])
                else:
                    s1 = tt(heads(S[:]), heads(S[:]), along(gl[d]), ALU.mult, [glast, mo])
                    sw = tt(S[:], S[:], bs.ap, ALU.add, [s1, ms])
                bs.done(sw)
                S_ready[d] = [sw]
                end = ms
            free = [[end]] * 7 + [S_ready[d]]

    def delta(sides):
        tok = yield from dn_prepare()
        sides += [Side(chain(0, tok)), Side(chain(1, tok))]

    DA = WK + 74
    dq = [sb(f"dq{i}", DA + 12 * i, [3, T]) for i in range(2)]
    dk = [sb(f"dk{i}", DA + 6 + 12 * i, [3, T]) for i in range(2)]
    dqc = [[Cell(dq[i][:, g, :]) for g in range(3)] for i in range(2)]
    dkc = [[Cell(dk[i][:, g, :]) for g in range(3)] for i in range(2)]
    dv = sb("dv", DA + 24, [3, 4, 128])
    dvT = Ring([Cell(sb(f"dvT{i}", DA + 30 + 2 * i, [T])) for i in range(2)])
    dS = sb("dS", DA + 34, [768])
    dPT = sb("dPT", DA + 37, [6, 128])
    dB = Cell(sb("dB", DA + 40, [768]))
    oda = sb("oda", DA + 43, [4, T])
    dO = sb("dO", DA + 51, [128])
    dst_ = sb("dstat", DA + 51.5, [16])
    v_pending = {}
    dab = [bank[6], bank[7]]
    da_done = []

    def by_residue(ap):
        return ap.rearrange("p (l r) -> p r l", r=4)

    def da_evac(kind, h, g):
        def evac(bks, done):
            ps = by_residue(bks[0].ap)
            if kind == "v":
                c = dvT.next()
                a = act(c.ap[:].rearrange("p (r l) -> p r l", r=4), ps, ACT.Copy, [done, c.free])
                v_pending[h, g] = (c, a)
            else:
                c = (dqc if kind == "q" else dkc)[h % 2][g]
                o = c.ap.rearrange("p (r l) -> p r l", r=4)
                if kind == "q":
                    a = act(o, ps, ACT.Copy, [done, c.free], scale=128.0 ** -0.5)
                else:
                    a = copy(o, ps, [done, c.free])
                c.ready, c.free = [a], []
            bks[0].done(a)
        return evac

    for h in range(4):
        for kind, base in (("q", 17), ("k", 29), ("v", 41)):
            for g in range(3):
                u_da.append(Unit(io["w_in"][base + 4 * g + h], h_rhs, da_evac(kind, h, g)))

    def dilated():
        A, B = dab
        s_free, pv, out_done = list(msb_free), [], []
        for h in range(4):
            vt = []
            for g in range(3):
                while (h, g) not in v_pending:
                    yield POLL
                c, a = v_pending[h, g]
                b = (A, B)[g % 2]
                yield [a, b.free]
                for r in range(4):
                    m = tr(b.ap[:, 128 * r:128 * r + 128], c.ap[:, 128 * r:128 * r + 128], ident, [a, b.free])
                w = act(dv[:, g], heads(b.ap), ACT.Copy, [m, pv])
                c.done(m)
                b.free = [w]
                vt.append(w)
            q, k = dq[h % 2], dk[h % 2]
            qk_ready = [c.ready for c in dqc[h % 2] + dkc[h % 2]]
            for r in range(4):
                ld = P.dma("gpsimd", dB.ap[:], io["da_bias"][h, r], "dabias", dB.free)
                yield [qk_ready, A.free, B.free]
                t = slice(128 * r, 128 * r + 128)
                mm(A.ap, q[:, 0, t], k[:, 0, :], after=[qk_ready, A.free])
                mm(B.ap[:, 0:128], q[:, 1, t], k[:, 1, t], after=[B.free])
                m = mm(B.ap[:, 128:256], q[:, 2, t], k[:, 2, t])
                s2 = psum[:, 6:8, :].rearrange("p a b -> p (a b)")[:, 0:768]
                mx = P.op("vector", lambda e, s2=s2: e.tensor_tensor_reduce(
                    dS[:], s2, dB.ap[:], 1.0, -3e38, ALU.add, ALU.max, dst_[:, 0:1]), [m, ld, s_free])
                A.free, B.free, dB.free = [mx], [mx], [mx]
                nm = ts(dst_[:, 1:2], dst_[:, 0:1], -1.0, ALU.mult, [mx])
                ex = act(dS[:], dS[:], ACT.Exp, [nm], bias=dst_[:, 1:2], accum=dst_[:, 2:3])
                rc = P.op("vector", lambda e: e.reciprocal(dst_[:, 3:4], dst_[:, 2:3]), [ex])
                yield [ex]
                for i in range(6):
                    b = A if i < 4 else B
                    m = tr(b.ap[:, 128 * (i % 4):128 * (i % 4) + 128], dS[:, 128 * i:128 * i + 128], ident,
                           [ex, b.free])
                    if i == 3:
                        p1 = act(dPT[:, 0:4], heads(A.ap), ACT.Copy, [m, pv])
                s_free = [m]
                p2 = copy(dPT[:, 4:6], B.ap[:, 0:256].rearrange("p (a b) -> p a b", a=2), [m, pv])
                A.free, B.free = [p1], [p2]
                yield [p1, p2, vt]
                for i in range(6):
                    g, rr = (0, i) if i < 4 else (i - 3, r)
                    m = mm(A.ap[:, 0:128], dPT[:, i], dv[:, g, rr], i == 0, i == 5, [p1, p2, vt, A.free])
                pv = [m]
                o1 = act(dO[:], A.ap[:, 0:128], ACT.Copy, [m, rc, out_done], scale=dst_[:, 3:4])
                A.free = [o1]
                yield [o1, B.free]
                m = tr(B.ap[:, 0:128], dO[:], ident, [o1, B.free])
                w = copy(oda[:, h].rearrange("p (l r) -> p r l", r=4)[:, r], B.ap[:, 0:128], [m, oda_idle])
                out_done = [m]
                B.free = [w]
                da_done.append(w)
            for c in dqc[h % 2] + dkc[h % 2]:
                c.free = pv

    zs = sb("zs", DA, [4, T])
    zsc = [Cell(zs[:, h, :]) for h in range(4)]

    def z_evac(h):
        def evac(bks, done):
            w = act(zsc[h].ap, bks[0].ap, ACT.Silu, [done, [c.free for c in dqc[0] + dkc[0]]])
            bks[0].done(w)
            zsc[h].ready = [w]
        return evac

    for h in range(4):
        u_z.append(Unit(io["w_in"][12 + h], h_rhs, z_evac(h)))

    odn_hi, odn_lo = sb("odn_hi", WK + 16, [4, T], F32R), sb("odn_lo", WK + 24, [4, T], F32R)
    oda_hi, oda_lo = sb("oda_hi", WK + 40, [4, T], F32R), sb("oda_lo", WK + 48, [4, T], F32R)
    odn_c = [(Cell(odn_hi[:, h]), Cell(odn_lo[:, h])) for h in range(4)]
    oda_c = [(Cell(oda_hi[:, h]), Cell(oda_lo[:, h])) for h in range(4)]
    osq, of = sb("osq", WK + 64, [T]), sb("of", WK + 66, [T])
    orr = sb("orr", WK + 68, [16])

    def finish_mixers(chain_end):
        of_free, osq_free, sums = [], [], []
        for n in range(4):
            a = tt(heads(osq[:]), oacc[:, n], oacc[:, n], ALU.mult, [o_ready[n], chain_end, osq_free])
            osq_free = [dve(lambda e, n=n: e.tensor_reduce(orr[:, 4 * n:4 * n + 4], heads(osq[:]), AX.X, ALU.add), [a], T)]
        c = act(orr[:], orr[:], ACT.Ln, osq_free, bias=EPS, scale=1.0 / 128)
        d_ = act(orr[:], orr[:], ACT.Exp, [c], scale=-0.5)
        for n in range(4):
            e_ = tt(heads(osq[:]), oacc[:, n], along(orr[:, 4 * n:4 * n + 4]), ALU.mult, [d_, osq_free])
            bk = dnb.next()
            yield [e_, bk.free]
            for h in range(4):
                m = tr(bk.ap[:, 128 * h:128 * h + 128], osq[:, 128 * h:128 * h + 128], ident, [e_, bk.free])
            osq_free = [m]
            f = stt(heads(of[:]), heads(bk.ap), cv(ONORM), zs[:, :, 128 * n:128 * n + 128], ALU.mult, ALU.mult,
                    [m, of_free, [z.ready for z in zsc]])
            bk.done(f)
            hi = act(odn_hi[:, :, 128 * n:128 * n + 128], heads(of[:]), ACT.Copy, [f])
            lo = tt(odn_lo[:, :, 128 * n:128 * n + 128], heads(of[:]),
                    odn_hi[:, :, 128 * n:128 * n + 128].bitcast(F32), ALU.subtract, [hi])
            of_free = [lo]
            for h in range(4):
                odn_c[h][0].ready.append(hi)
                odn_c[h][1].ready.append(lo)
        for h in range(4):
            hi = act(oda_hi[:, h], oda[:, h], ACT.Copy, [da_done, chain_end])
            lo = tt(oda_lo[:, h], oda[:, h], oda_hi[:, h].bitcast(F32), ALU.subtract, [hi])
            oda_c[h][0].ready, oda_c[h][1].ready = [hi], [lo]

    gates = Ring([Cell(sb(f"gate{i}", WK + 86 + 2 * i, [T])) for i in range(6)])
    gate_of = {}
    mg_hi, mg_lo = sb("mg_hi", WK + 56, [KC, T], F32R), None
    mg_lo = sb("mg_lo", WK + 98, [KC, T], F32R)
    mgc = [(Cell(mg_hi[:, c]), Cell(mg_lo[:, c])) for c in range(KC)]

    def gate_evac(which, o):
        def evac(bks, done):
            c = gates.next()
            a = act(c.ap[:], bks[0].ap, ACT.Sigmoid, [done, c.free, da_done])
            bks[0].done(a)
            gate_of[which, o] = (c, a)
        return evac

    xres = sb("xres", WK, [KC, T])
    xr = [Cell(xres[:, c, :]) for c in range(KC)]

    def merge_evac(o):
        def evac(bks, done):
            (c1, r1), (c2, r2) = gate_of["dn", o], gate_of["da", o]
            a = tt(c1.ap[:], bks[0].ap, c1.ap[:], ALU.mult, [done, r1])
            b = tt(c2.ap[:], bks[1].ap, c2.ap[:], ALU.mult, [done, r2])
            bks[0].done(a)
            bks[1].done(b)
            s = tt(c1.ap[:], c1.ap[:], c2.ap[:], ALU.add, [a, b])
            hi = act(mgc[o][0].ap, c1.ap[:], ACT.Copy, [s])
            lo = tt(mgc[o][1].ap, c1.ap[:], mgc[o][0].ap.bitcast(F32), ALU.subtract, [hi])
            c1.done(lo)
            c2.done(s)
            mgc[o][0].ready, mgc[o][1].ready = [hi], [lo]
        return evac

    late_banks = Ring(bank[2:6])
    GL = 2
    for o in range(KC + GL):
        if o < KC:
            u_merge.append(Unit(io["w_in"][53 + o], h_rhs, gate_evac("dn", o)))
            u_merge.append(Unit(io["w_in"][61 + o], h_rhs, gate_evac("da", o)))
        if o >= GL:
            u_merge.append(Unit(io["w_br"][o - GL], lambda: whole(odn_c, oda_c), merge_evac(o - GL), late_banks))

    class Norm:

        def __init__(self, name, kb, n, cells, ring):
            z = n / 256
            self.n, self.x, self.ring = n, cells, ring
            self.sq = Ring([Cell(sb(f"{name}sq{i}", kb + z * i, [n])) for i in range(2)])
            self.acc, self.r = sb(f"{name}acc", kb + 2 * z, [n]), sb(f"{name}r", kb + 3 * z, [n])
            self.hn = Ring([Cell(sb(f"{name}hn", kb + 4 * z, [n]))])
            self.summed, self.used = [], []

        def add(self, c, ready, after=()):
            s = self.sq.next()
            a = act(s.ap[:], self.x[c].ap, ACT.Square, [ready, s.free, after])
            if c == 0:
                g = copy(self.acc[:], s.ap[:], [a, self.summed, after], eng="gpsimd")
            elif c < KC - 1:
                g = tt(self.acc[:], self.acc[:], s.ap[:], ALU.add, [a, self.summed], eng="gpsimd")
            else:
                self.bank = self.ring.next()
                o = self.bank.ap[:, 0:self.n]
                mm(o, ones[:], self.acc[:], True, False, [self.summed, self.bank.free])
                g = mm(o, ones[:], s.ap[:], False, True, [a])
            s.done(g)
            self.summed = [g]

        def rs(self):
            l = act(self.r[:], self.bank.ap[:, 0:self.n], ACT.Ln, [self.summed, self.used], bias=EPS, scale=1.0 / D)
            self.bank.done(l)
            self.bank = None
            self.ready = [act(self.r[:], self.r[:], ACT.Exp, [l], scale=-0.5)]
            return self.ready

        def apply(self, scale, pairs, shift=None, tap=None):
            rs = self.rs() if self.bank else self.ready
            for c in range(KC):
                yield
                h = self.hn.next()
                hi, lo = pairs[c]
                w = stt(h.ap[:], self.x[c].ap, scale(c), self.r[:], ALU.mult, ALU.mult, [rs, self.x[c].ready, h.free])
                if shift is None:
                    a = act(hi.ap, h.ap[:], ACT.Copy, [w, hi.free])
                    b = tt(lo.ap, h.ap[:], hi.ap.bitcast(F32), ALU.subtract, [a, lo.free])
                else:
                    a = act(hi.ap, h.ap[:], ACT.Identity, [w, hi.free], bias=shift(c))
                    b = stt(lo.ap, h.ap[:], shift(c), hi.ap.bitcast(F32), ALU.add, ALU.subtract, [a, lo.free])
                hi.ready, lo.ready = [a], [b]
                h.done(b)
                if tap:
                    yield [w]
                    h.done(b, tap(c, h.ap, [w]))
            self.used = [w]

    norm = Norm("n", WK + 116, T, xr, late_banks)

    def wout_evac(o):
        def evac(bks, done):
            w = tt(xr[o].ap, xr[o].ap, bks[0].ap, ALU.add, [done, xr[o].ready])
            bks[0].done(w)
            xr[o].ready = [w]
            norm.add(o, [w], da_done)
        return evac

    for o in range(KC):
        u_out.append(Unit(io["w_out"][o], lambda: whole(mgc), wout_evac(o), late_banks))

    pq = Ring([Cell(sb(f"pq{i}", kb, [T])) for i, kb in enumerate((113, 115, 136))])
    keys = Ring([Cell(sb(f"keys{i}", 119 + i / 2, [128])) for i in range(4)])
    rest = sb("rest", 117, [4, 128])
    sv, siu = sb("sv", 126, [4, 16, 16]), sb("siu", 130, [4, 16, 16], U32)
    cand, eqv, eqg = sb("cand", 49, [2048]), sb("eqv", 57, [2048]), sb("eqg", 65, [2048])
    sif = sb("sif", 73, [16, 16])
    cvl, ciu = sb("cvl", 74, [8, 16]), sb("ciu", 74.5, [8, 16], U32)
    su = sb("su", 75, [3, 128], U32)
    af, bf, tf = [sb(f"rank{i}", 76.5 + i / 2, [128]) for i in range(3)]
    i1f, i2f, gtf = [sb(f"chosen{i}", 78 + i / 2, [128]) for i in range(3)]
    ksm = sb("ksm", 79.5, [32])
    i1T, i2T, gT = sb("i1T", 197, [TD]), sb("i2T", 198.5, [TD]), sb("gT", 200, [TD])
    rows, rgate, ract = sb("rows", 201.5, [128], I32), sb("rgate", 202, [128]), sb("ract", 202.5, [128])
    NEGF = -3.0e38
    wq_idle = []
    pq_of = {}

    def wq_evac(i):
        def evac(bks, done):
            c = pq.next()
            a = act(c.ap[:], bks[0].ap, ACT.Copy, [done, c.free, wq_idle])
            bks[0].done(a)
            pq_of[i] = (c, a)
        return evac

    for i in range(16):
        u_wq.append(Unit(io["peer_wq"][i], h_rhs, wq_evac(i), spine_banks, lo="any"))
        u_wq[i].guard = lambda: not all(c.held for c in pq.cells)

    keyb = Ring(bank[6:8])
    tile_keys, rows_ready = [], []

    def vmax(out, in_, after):
        return dve(lambda e: e.max(out, in_), after, width(in_))

    def vindex(out, vals, in_, after):
        return dve(lambda e: e.max_index(out, vals, in_), after, width(in_))

    def vreplace(out, vals, in_, after):
        return dve(lambda e: e.match_replace(out, vals, in_, NEGF), after, width(in_))

    def top_keys():
        loaded = []

        def load(i):
            if i < 16:
                c = keys.next()
                c.ready = [P.dma("gpsimd", c.ap[:], io["peer_keys"][:, i, :], f"keys{i % 4}", [c.free, wq_idle])]
                loaded.append(c)
        for i in range(3):
            load(i)
        x2, r1 = [], []
        for i in range(16):
            while i not in pq_of:
                yield POLL
            c, a = pq_of[i]
            k, b = loaded[i], keyb.next()
            yield [a, k.ready, b.free]
            src = [b.ap[:, 128 * n:128 * n + 128] for n in range(4)]
            for n in range(4):
                m = mm(src[n], c.ap[:, 128 * n:128 * n + 128], k.ap[:], after=[a, k.ready, b.free])
            c.done(m)
            k.done(m)
            load(i + 3)
            m1 = [vmax(sv[:, n, i, 0:8], src[n], [m, wq_idle]) for n in range(4)]
            yield
            r1 = [vreplace(rest[:, n, :], sv[:, n, i, 0:8], src[n], [m1[n], x2]) for n in range(4)]
            x1 = [vindex(siu[:, n, i, 0:8], sv[:, n, i, 0:8], src[n], [m1[n]]) for n in range(4)]
            b.done(x1)
            yield
            m2 = [vmax(sv[:, n, i, 8:16], rest[:, n, :], [r1[n]]) for n in range(4)]
            x2 = [vindex(siu[:, n, i, 8:16], sv[:, n, i, 8:16], rest[:, n, :], [m2[n]]) for n in range(4)]
            yield
        return [m2, x2]

    NC = 72

    def top_pairs(sel):
        free = {"sel": [], "cand": flat([[c.free for c in hhi + hlo], norm.summed]), "i": []}
        for n in range(4):
            t = slice(128 * n, 128 * n + 128)
            s4 = sv[:, n].rearrange("p (h c) k -> p h c k", c=2)
            s5 = sif[:].rearrange("p (h c) k -> p h c k", c=2)
            c4 = cand[:, 0:8 * NC].rearrange("p (h j) -> p h j", h=8)
            w = []
            for at, a0, a1, nb in ((0, 0, 2, 16), (32, 2, 4, 8), (48, 4, 8, 4), (64, 8, 16, 1)):
                na = a1 - a0
                w.append(tt(c4[:, :, at:at + na * nb].rearrange("p h (a b) -> p h a b", a=na),
                            s4[:, :, 0, a0:a1].unsqueeze(3).broadcast_to([128, 8, na, nb]),
                            s4[:, :, 1, 0:nb].unsqueeze(2).broadcast_to([128, 8, na, nb]), ALU.add, [sel, free["cand"]]))
            fi = copy(sif[:], siu[:, n], [sel, free["sel"], w])
            yield
            ch = [c4[:, h] for h in range(8)]
            rh = [eqv[:, NC * h:NC * h + NC] for h in range(8)]
            m1 = [vmax(cvl[:, h, 0:8], ch[h], [w, free["i"]]) for h in range(8)]
            r1, x1 = [], []
            for h in range(8):
                r1.append(vreplace(rh[h], cvl[:, h, 0:8], ch[h], [m1[h], free["cand"]]))
                x1.append(vindex(ciu[:, h, 0:8], cvl[:, h, 0:8], ch[h], [m1[h]]))
            yield
            m2 = [vmax(cvl[:, h, 8:16], rh[h], [r1[h]]) for h in range(8)]
            x2 = [vindex(ciu[:, h, 8:16], cvl[:, h, 8:16], rh[h], [m2[h]]) for h in range(8)]
            yield
            cf = ciu[:].rearrange("p h k -> p (h k)")
            s1 = [ts(su[:, j], cf, 4 - j, ALU.logical_shift_right, [x1, x2]) for j in range(3)]
            a = stt(af[:], su[:, 1], -2.0, su[:, 0], ALU.add, ALU.max, s1)
            a = stt(af[:], su[:, 2], -8.0, af[:], ALU.add, ALU.max, [a])
            a = stt(af[:], cf, -56.0, af[:], ALU.add, ALU.max, [a])
            b1 = ts(bf[:], af[:], 8.0, ALU.mult, [a], 16.0, ALU.add)
            b2 = ts(tf[:], af[:], 4.0, ALU.mult, [a], 32.0, ALU.add)
            b1 = stt(bf[:], af[:], 16.0, bf[:], ALU.mult, ALU.min, [b1])
            b2 = stt(tf[:], af[:], 56.0, tf[:], ALU.add, ALU.min, [b2])
            b1 = tt(bf[:], bf[:], tf[:], ALU.min, [b1, b2])
            b = tt(bf[:], cf, bf[:], ALU.subtract, [b1])
            i16 = cst[:, IOTA:IOTA + 16].unsqueeze(1).broadcast_to([128, 128, 16])
            e3, g3 = eqv[:].rearrange("p (q j) -> p q j", j=16), eqg[:].rearrange("p (q j) -> p q j", j=16)

            def table(c):
                return s5[:, :, c, :].unsqueeze(2).broadcast_to([128, 8, 16, 16])

            def look_up(eq, c, ready):
                e4 = eq[:].rearrange("p (h k j) -> p h k j", h=8, j=16)
                return tt(e4, e4, table(c), ALU.mult, [ready, fi], eng="gpsimd")
            yield
            v1 = tt(e3, along(af[:], 16), i16, ALU.is_equal, [a, x2, m2, ld_c])
            v2 = look_up(eqv, 0, v1)
            yield
            p1 = tt(g3, along(bf[:], 16), i16, ALU.is_equal, [b, free["cand"]])
            p2 = look_up(eqg, 1, p1)
            d0 = tt(gtf[:].rearrange("p (h k) -> p h k", h=8), cvl[:], cvl[:, :, 0:1].broadcast_to([128, 8, 16]),
                    ALU.subtract, [m1, m2, free["i"]])
            d1 = act(gtf[:], gtf[:], ACT.Exp, [d0])
            yield [d1]
            d2 = dve(lambda e: e.tensor_reduce(ksm[:, 0:8], gtf[:].rearrange("p (h k) -> p h k", h=8),
                                               AX.X, ALU.add), [d1], 128)
            d3 = dve(lambda e: e.reciprocal(ksm[:, 8:16], ksm[:, 0:8]), [d2], 8)
            d4 = tt(gtf[:].rearrange("p (h k) -> p h k", h=8), gtf[:].rearrange("p (h k) -> p h k", h=8),
                    ksm[:, 8:16].unsqueeze(2).broadcast_to([128, 8, 16]), ALU.mult, [d3])
            yield [v2]
            v3 = dve(lambda e: e.tensor_reduce(i1f[:], e3, AX.X, ALU.add), [v2, free["i"]], 2048)
            yield [p2]
            p3 = dve(lambda e: e.tensor_reduce(i2f[:], g3, AX.X, ALU.add), [p2, free["i"]], 2048)
            if n == TD // 128:
                r1 = stt(rows[:], i1f[:], 128.0, i2f[:], ALU.mult, ALU.add, [v3, p3])
                rows_ready.extend([r1, copy(rgate[:], gtf[:], [d4])])
                free["cand"] = [x1, p3, v3]
                continue
            bk = keyb.next()
            yield [v3, p3, d4, bk.free]
            q = [tr(bk.ap[:, 0:128], i1f[:], ident, [v3, bk.free]), tr(bk.ap[:, 128:256], i2f[:], ident, [p3]),
                 tr(bk.ap[:, 256:384], gtf[:], ident, [d4])]
            k = [copy(i1T[:, t], bk.ap[:, 0:128], q), copy(i2T[:, t], bk.ap[:, 128:256], q),
                 copy(gT[:, t], bk.ap[:, 256:384], q)]
            bk.done(k)
            tile_keys.append(k)
            free = {"sel": [v2, p2], "cand": [x1, p3, v3], "i": [q, d0]}
        for c in hhi + hlo:
            c.free = flat(list(free.values()))

    NG = TD // 16
    gate_dram = nc.dram_tensor("gate_dram", [NG, 128, 128, 16], F32, kind="Internal").ap()
    GT = 4
    ea = Ring([Cell(sb(f"ea{i}", 81 + 2 * i, [GT, 128])) for i in range(4)])
    eb = Ring([Cell(sb(f"eb{i}", 89 + 2 * i, [GT, 128])) for i in range(4)])
    stage = Ring([Cell(sb(f"stage{i}", 152 + 8 * i, [128, 16])) for i in range(2)])
    g_written, g_idle, g_readers = [], [], []

    def dense_gates():
        io_b = cst[:, IOTA:IOTA + 128].unsqueeze(1).broadcast_to([128, GT, 128])

        def one_hots(n):
            t = slice(GT * n, GT * n + GT)
            k = tile_keys[GT * n // 128]
            A, B = ea.next(), eb.next()
            a1 = tt(A.ap[:], io_b, along(i1T[:, t]), ALU.is_equal, [k, A.free, g_idle])
            a2 = tt(A.ap[:], A.ap[:], along(gT[:, t]), ALU.mult, [a1], eng="gpsimd")
            b1 = tt(B.ap[:], io_b, along(i2T[:, t]), ALU.is_equal, [k, B.free])
            return A, B, [a2, b1]
        while not g_idle or not tile_keys:
            yield POLL
        ahead, made = [], 0
        for n in range(TD // GT):
            while made < TD // GT and len(ahead) < 3:
                if len(tile_keys) <= GT * made // 128:
                    if ahead:
                        break
                    yield POLL
                    continue
                yield
                ahead.append(one_hots(made))
                made += 1
            A, B, ab = ahead.pop(0)
            if n % 4 == 0:
                S, ws = stage.next(), []
            b = keyb.next()
            yield [ab, b.free]
            for v in range(GT):
                m = mm(b.ap[:, 128 * v:128 * v + 128], A.ap[:, v, :], B.ap[:, v, :], after=[ab, b.free])
            c = GT * (n % 4)
            w = act(S.ap[:, :, c:c + 4], b.ap.rearrange("p (v j) -> p j v", v=4), ACT.Copy, [m, S.free, g_idle])
            b.done(w)
            ws.append(w)
            A.done(m)
            B.done(m)
            if n % 4 == 3:
                g = n // 4
                d = P.dma("sync", gate_dram[g].rearrange("p j t -> p (j t)"), S.ap[:].rearrange("p j t -> p (j t)"),
                          f"stage{g % 2}", ws)
                S.done(d)
                g_written.append(d)
        g_readers.append(m)

    GJ = 8
    gin = [Cell(sb(f"gin{i}", kb, [NG, GJ, 16])) for i, kb in enumerate((145, 157))]
    ag_hi = [sb(f"ag_hi{i}", kb, [GJ, TD], F32R) for i, kb in enumerate((97, 169))]
    ag_lo = [sb(f"ag_lo{i}", kb, [GJ, TD], F32R) for i, kb in enumerate((109, 181))]
    agc = [[(Cell(ag_hi[i][:, j]), Cell(ag_lo[i][:, j])) for j in range(GJ)] for i in range(2)]
    uact = Ring([Cell(sb(f"uact{i}", 193 + 1.5 * i, [TD])) for i in range(2)])
    hd = [(Cell(hhi[c].ap[:, 0:TD]), Cell(hlo[c].ap[:, 0:TD])) for c in range(KC)]

    def load_gates(g):
        c = gin[g % 2]
        c.ready = [P.dma("sync", c.ap[:].rearrange("p n j t -> p n (j t)"),
                         gate_dram[:, :, GJ * g:GJ * g + GJ, :].rearrange("n p j t -> p n (j t)"),
                         f"gin{g % 2}", [g_written, c.free])]
        c.free = []

    def u_evac(j):
        g, jj = divmod(j, GJ)

        def evac(bks, done):
            c, gc_ = uact.next(), gin[g % 2]
            hi, lo = agc[g % 2][jj]
            a = act(c.ap[:], bks[0].ap[:, 0:TD], ACT.Gelu_apprx_tanh, [done, c.free])
            bks[0].done(a)
            t3 = c.ap[:].rearrange("p (n t) -> p n t", t=16)
            w = tt(t3, t3, gc_.ap[:, :, jj, :], ALU.mult, [a, gc_.ready])
            gc_.free = gc_.free + [w]
            h = act(hi.ap, c.ap[:], ACT.Copy, [w, hi.free])
            l = tt(lo.ap, c.ap[:], hi.ap.bitcast(F32), ALU.subtract, [h, lo.free])
            c.done(l)
            hi.ready, lo.ready = [h], [l]
        return evac

    def v_evac(g, dt):
        def evac(bks, done):
            w = tt(xr[dt].ap[:, 0:TD], xr[dt].ap[:, 0:TD], bks[0].ap[:, 0:TD], ALU.add, [done, xr[dt].ready])
            bks[0].done(w)
            xr[dt].ready = [w]
            if g == 128 // GJ - 1:
                xr[dt].ready = [w] + row_sums
                norm.add(dt, xr[dt].ready)
        return evac

    NGR = 128 // GJ
    u_units = [[Unit(io["peer_u"][GJ * g + j], lambda: whole(hd), u_evac(GJ * g + j), spine_banks, lo="any") for j in range(GJ)]
               for g in range(NGR)]
    v_units = [[Unit(io["peer_v"][8 * g + d], lambda g=g: whole(agc[g % 2]), v_evac(g, d), late_banks, lo="any") for d in range(8)]
               for g in range(NGR)]
    u_peer += u_units[0]
    for g in range(NGR):
        for j in range(8):
            if g + 1 < NGR:
                u_peer.append(u_units[g + 1][j])
            u_peer.append(v_units[g][j])

    xtok = sb("xtok", 126, [D])
    fetched = [Cell(sb(f"fetched{i}", kb, [D])) for i, kb in enumerate((130, 134, 138, 121, 196))]
    row_sums, x_tok = [], []

    def to_tokens(c, h, ready):
        b = keyb.next()
        t = tr(b.ap[:, 0:128], h[:, TD:T], ident, [ready, b.free])
        w = copy(xtok[:, 128 * c:128 * c + 128], b.ap[:, 0:128], [t, rows_ready])
        b.done(w)
        x_tok.append(w)
        return t

    def chosen_experts(idle):
        R = len(fetched)

        def fetch(i):
            if i < 256:
                c = fetched[i % R]
                c.ready = [P.gather(c.ap[:], io["peer_v_rows" if i >= 128 else "peer_u_rows"],
                                    rows[:, i % 128:i % 128 + 1], f"fetched{i % R}", [c.free, rows_ready, idle])]
        for i in range(R - 1):
            fetch(i)
        ws = []
        for i in range(128):
            c = fetched[i % R]
            yield [c.ready, x_tok]
            w = dve(lambda e, c=c, i=i: e.tensor_tensor_reduce(c.ap[:], c.ap[:], xtok[:], 1.0, 0.0, ALU.mult, ALU.add,
                                                              ract[:, i:i + 1]), [c.ready, x_tok, idle], D + 120)
            c.free = [w]
            ws.append(w)
            fetch(i + R - 1)
        yield [ws]
        a = act(ract[:], ract[:], ACT.Gelu_apprx_tanh, [ws])
        b = tt(ract[:], ract[:], rgate[:], ALU.mult, [a, rows_ready])
        for i in range(128):
            c = fetched[(i + 128) % R]
            yield [c.ready, b]
            if i == 0:
                w = ts(xtok[:], c.ap[:], ract[:, 0:1], ALU.mult, [c.ready, b, ws])
            else:
                w = stt(xtok[:], c.ap[:], ract[:, i:i + 1], xtok[:], ALU.mult, ALU.add, [c.ready, w])
            c.free = [w]
            fetch(i + 128 + R - 1)
        for x in range(2):
            b = keyb.next()
            yield [w, b.free]
            for c in range(4):
                t = tr(b.ap[:, 128 * c:128 * c + 128], xtok[:, 512 * x + 128 * c:512 * x + 128 * c + 128], ident,
                       [w, b.free])
            us = [tt(xr[4 * x + c].ap[:, TD:T], xr[4 * x + c].ap[:, TD:T], b.ap[:, 128 * c:128 * c + 128], ALU.add,
                     [t, xr[4 * x + c].ready]) for c in range(4)]
            b.done(us)
            row_sums.extend(us)

    M0 = 97
    svec = sb("svec", 4.25, [46])
    mod_ready = [[], []]
    svec_ready, mod_pending = [], []
    msb = [sb(f"msb{i}", kb, [512]) for i, kb in enumerate((DA + 34, DA + 36, WK + 84, 134))]

    def start_mod():
        a = memset(svec[:], 0.0)
        sv_ = svec[:, 0:16].rearrange("p (k v) -> p v k", v=2)
        svec_ready.append(act(sv_, cv(CVEC, 16).rearrange("p (v k) -> p v k", v=2), ACT.Silu, [a, ld_c]))

    def mod_finish():
        for l, r, bk, m, w in mod_pending:
            for x in range(4):
                t = tr(bk.ap[:, 128 * x:128 * x + 128], m[:, 128 * x:128 * x + 128], ident, [w])
            msb_free[:] = [t]
            src = bk.ap.rearrange("p (x j v) -> p j x v", x=4, j=4)[:, :, :, 0:2]
            dst = mod[:, l, :, 16 * r:16 * r + 16].rearrange("p v (j x) -> p j x v", x=4)
            for v in range(2):
                w = tt(dst[:, :, :, v], src[:, :, :, v],
                       cv(BMOD + 48 * l + 16 * r, 16).rearrange("p (j x) -> p j x", x=4), ALU.add, [t, ld_c])
                mod_ready[l].append(w)
            bk.done(w)
            if r == 2:
                for v in range(2):
                    for x, (nrm, sc) in enumerate(((N2MIX, 8), (N2FFN, 32))):
                        mod_ready[l].append(stt(amod[:, l, v, x], mod[:, l, v, sc:sc + 8], 1.0,
                                                cv(nrm + 8 * l, 8), ALU.add, ALU.mult, [mod_ready[l], ld_c]))
        mod_pending.clear()

    msb_free = []

    def mod_unit(l, r, k, half, bk, m):
        def run(rawc):
            if k == 0 and half == 0:
                mod_finish()
            for j in (2 * half, 2 * half + 1):
                t = mm(bk.ap[32 * j:32 * j + 32, :], svec[:, 2 * k:2 * k + 32],
                       rawc.ap[:, 512 * (j % 2):512 * (j % 2) + 512], k == 0, k == KC - 1,
                       [rawc.ready, svec_ready, bk.free], (0, 32 * j))
            if k == KC - 1 and half == 1:
                w = act(m[:], bk.ap, ACT.Copy, [t, msb_free, msb_idle])
                mod_pending.append((l, r, bk, m, w))
            return t
        return run

    msb_idle = []
    place = {(0, 0): (bank[6], msb[0]), (0, 1): (bank[7], msb[1]), (0, 2): (bank[6], msb[2])}
    mod_units = [[Unit(io["w_mod"][((3 * l + r) * 8 + k) * 2 + h], None,
                       mod_unit(l, r, k, h, *place.get((l, r), (bank[5], msb[3]))), None, False)
                  for r in range(3) for k in range(8) for h in range(2)] for l in range(2)]

    def modv(l, v, chunk):
        return mod[:, l, v, chunk:chunk + 1]

    c2, c2c = sb("c2", M0, [NC2]), sb("c2c", 140, [NC2C])
    wa2, wa2c = sb("wa2", M0 + 9.5, [2, 256]), sb("wa2c", 143, [2, 256])
    res_dram = nc.dram_tensor("ctx_res", [2, 128, 2560], F32, kind="Internal").ap()
    res_written = [None, None]

    class Mixer:
        pass

    lat_in, ctx_in = Mixer(), Mixer()
    lat_in.reset = [c2[:, RSTF:RSTF + T], c2[:, RSTB:RSTB + T][:, ::-1]]
    lat_in.onesbd, lat_in.bmask = c2[:, ONESBD:ONESBD + 128], c2[:, BMASK:BMASK + 128]
    lat_in.wa, lat_in.ready = Cell(wa2[:]), []
    lat_in.out = [(bank[2], bank[2].ap), (bank[3], bank[3].ap)]
    lat_in.work = Ring(bank[4:6])
    ctx_in.reset = [c2c[:, 0:256], c2c[:, 256:512][:, ::-1]]
    ctx_in.onesbd, ctx_in.bmask = c2c[:, 512:640], c2c[:, 640:768]
    ctx_in.wa, ctx_in.ready = Cell(wa2c[:]), []
    ctx_in.out = [(bank[2], bank[2].ap[:, 0:256]), (bank[2], bank[2].ap[:, 256:512])]
    ctx_in.work = Ring(bank[3:5])

    def make_mixer(l, v, N, base, hin, full, idle, shared):
        m = Mixer()
        m.l, m.v, m.N, m.full, m.hin = l, v, N, full, hin
        NT, z = N // 128, N / 512
        nm = f"{'cl'[v == 0]}{l}"
        lat = v == 0
        lay = (dict(gq=0, gk=4, gvT=8, gvtok=12, gg=16, za=20, C=22, qin=26, kin=30, ktok=34, Sen=38, aT=46, tmp=50,
                    S0=54, nq=56, nk=62, nvT=68, sq=74, sk=80, svT=82, svtok=84, rope=86, nvtok=0, swm=18,
                    res=197 - base) if lat else
               dict(gq=0, gk=2, gvT=4, gvtok=6, gg=8, za=10, C=11, qin=13, kin=15, ktok=17, Sen=19, aT=23, tmp=27,
                    S0=29, nq=30, nvT=33, sq=36, svT=39, pipe=0, res=40) if full else
               dict(gk=0, gvT=2, gvtok=4, za=6, C=7, ktok=9, Sen=11, tmp=15, S0=17, nvT=18, svT=21, res=22))

        def buf(key, shape, dt=F32, off=0.0, name=None):
            if key not in lay:
                return None
            return sb(f"{nm}_{name or key}", base + lay[key] + off, shape, dt)
        res = buf("res", [2560])
        r_nk = res[:, 0:768].rearrange("p (i t) -> p i t", i=3)
        r_nv = res[:, 768:1536].rearrange("p (n f) -> p n f", n=2)
        r_sk = res[:, 1536:1792]
        r_sv = res[:, 1792:2048].rearrange("p (n f) -> p n f", n=2)
        r_S = res[:, 2048:2560].rearrange("p (d i f) -> p d i f", d=2, i=2)
        gq, gk, gvT, gvtok, gg = [buf(k, [2, N]) for k in ("gq", "gk", "gvT", "gvtok", "gg")]
        za, C, qin, kin, ktok, tmp = buf("za", [N]), *[buf(k, [2, N]) for k in ("C", "qin", "kin", "ktok", "tmp")]
        NCH = N // 64
        Sen = buf("Sen", [NCH, 2, 128])
        aT = [buf("aT", [4, 128], F32, 2 * i, f"aT{i}") for i in range(2)]
        dec = sb(f"{nm}_dec", 8.5 if lat else 8.75, [2, NCH])
        S0 = buf("S0", [2, 2, 128] if lat else [2, 128])
        nq, nvT, sq_, svT = buf("nq", [3, N]), buf("nvT", [3, N]), buf("sq", [3, N]), buf("svT", [N])
        nk = buf("nk", [3, N]) if lat else r_nk
        sk = buf("sk", [N]) if lat else r_sk
        ready = {}

        def plain(dst, key, scale=None, perm=False):
            def evac(bks, done):
                ps, o = bks[0].ap[:, 0:N], dst
                if perm:
                    if perm == "query":
                        ps = ps.rearrange("p (r b c) -> p b r c", r=8, b=4)
                        o = dst.rearrange("p (b r c) -> p b r c", b=4, r=8)
                    else:
                        ps = ps.rearrange("p (x r w) -> p x w r", x=2, r=4)
                        o = dst.rearrange("p (x w r) -> p x w r", x=2, r=4)
                    if scale is not None:
                        w = ts(o, ps, scale, ALU.mult, [done, idle])
                    else:
                        w = copy(o, ps, [done, idle])
                elif scale is not None:
                    w = act(o, ps, ACT.Copy, [done, idle], scale=scale)
                else:
                    w = act(o, ps, ACT.Copy, [done, idle])
                bks[0].done(w)
                ready[key] = [w]
            return evac

        def silu_evac(dst, i):
            def evac(bks, done):
                w = act(dst, bks[0].ap[:, 0:N], ACT.Silu, [done, idle])
                bks[0].done(w)
                ready["gg"] = ready.get("gg", []) + [w]
            return evac

        proj = []
        for i in range(2):
            proj.append((4 + i, plain(gvT[:, i], f"gv{i}")))
        proj.append((8, plain(za[:], "za")))
        for i in range(2):
            proj.append((2 + i, plain(gk[:, i], f"gk{i}")))
        if full:
            for i in range(2):
                proj.append((i, plain(gq[:, i], f"gq{i}", 0.125)))
            for i in range(2):
                proj.append((6 + i, silu_evac(gg[:, i], i)))
        for i in range(3):
            if full:
                proj.append((9 + i, plain(nq[:, i], f"nq{i}", 0.125 if lat else -0.125, lat and "query")))
            proj.append((12 + i, plain(nk[:, i], f"nk{i}", None, lat and "key")))
            proj.append((15 + i, plain(nvT[:, i], f"nv{i}", None, lat and "key")))
        if full:
            for i in range(3):
                proj.append((18 + i, plain(sq_[:, i], f"sq{i}", 0.125 if lat else -0.125)))
        proj.append((21, plain(sk[:] if lat else sk, "sk")))
        proj.append((22, plain(svT[:], "sv")))
        m.units = [Unit(io["w_in2"][l * 23 + t], lambda: whole(hin), ev, lo="vector" if lat else "any") for t, ev in proj]
        m.proj_done = False
        ob, g4 = shared.out, shared.work
        one_bank = ob[0][0] is ob[1][0]
        hs = [slice(0, 64), slice(64, 128)]

        def wait_for(*keys):
            while not all(k in ready for k in keys):
                yield POLL
            return [ready[k] for k in keys]

        def gla():
            wa = shared.wa.ap
            w_wa = P.dma("sync", wa, io["wa2"][l], f"wa2{v}", [shared.wa.free, shared.ready])
            if lat:
                s_init = P.dma("sync", S0[:].rearrange("p d i f -> p (d i f)"), res_dram[l][:, 2048:2560], "S0",
                               [idle, res_written[l]])
            else:
                s_init = memset(S0[:], 0.0, [idle])
            vt = []
            for i in range(2):
                rd = yield from wait_for(f"gv{i}")
                b = g4.next()
                yield [rd, b.free]
                for n in range(NT):
                    t = tr(b.ap[:, 128 * n:128 * n + 128], gvT[:, i, 128 * n:128 * n + 128], ident, [rd, b.free])
                w = copy(gvtok[:, i], b.ap[:, 0:N], [t, idle])
                b.done(w)
                vt.append(w)
            r_za = yield from wait_for("za")
            yield [r_za]
            o_begun = set()
            q_done, k_done, kt_done, sen_done, at_done, wa_done = [], [], [], [], [], []
            tmp_done = []
            for d in range(2):
                zb = []
                for i in range(2):
                    b = g4.next()
                    t = mm(b.ap[:, 0:N], wa[:, d, 128 * i:128 * i + 128], za[:], after=[w_wa, r_za, b.free])
                    w = ts(tmp[:, i], b.ap[:, 0:N], cv(GBA + 4 * l + 2 * d + i), ALU.add,
                           [t, ld_c, idle, tmp_done], -1.0, ALU.mult)
                    b.done(w)
                    zb.append(w)
                wa_done.append(t)
                a = act(C[:], tmp[:], ACT.Abs, [zb, idle, q_done, k_done])
                a = act(C[:], C[:], ACT.Exp, [a], scale=-1.0)
                a = act(C[:], C[:], ACT.Ln, [a], bias=1.0)
                w = stt(tmp[:], tmp[:], 0.0, C[:], ALU.max, ALU.add, [a])
                sc = []
                for i in range(2):
                    rst = shared.reset[d]
                    o_, i_ = (C[:, i], tmp[:, i]) if d == 0 else (C[:, i][:, ::-1], tmp[:, i][:, ::-1])
                    sc.append(P.op("vector", lambda e, o_=o_, i_=i_, rst=rst: e.tensor_tensor_scan(
                        o_, rst, i_, 0.0, ALU.mult, ALU.add), [w, shared.ready]))
                C4 = C[:].rearrange("p i (c s) -> p i c s", s=64)
                cl = C4[:, :, :, 63 if d == 0 else 0]
                r_k = yield from wait_for("gk0", "gk1")
                dc = act(dec[:], cl, ACT.Exp, [sc, idle, sen_done], scale=-1.0 / 16)
                if full:
                    r_q = yield from wait_for("gq0", "gq1")
                    qa = act(qin[:], C[:], ACT.Exp, [sc, idle, q_done], scale=-1.0 / 16)
                    q_ = tt(qin[:], qin[:], gq[:], ALU.mult, [qa, r_q])
                    ka = act(kin[:], C[:], ACT.Exp, [sc, idle, k_done], scale=1.0 / 16)
                    k_ = tt(kin[:], kin[:], gk[:], ALU.mult, [ka, r_k], eng="gpsimd")
                t4 = tmp[:].rearrange("p i (c s) -> p i c s", s=64)
                e = tt(t4, C4, cl.unsqueeze(3).broadcast_to([128, 2, NCH, 64]), ALU.subtract, [sc])
                e = act(tmp[:], tmp[:], ACT.Exp, [e], scale=1.0 / 16)
                e = tt(tmp[:], tmp[:], gk[:], ALU.mult, [e, r_k])
                if d == 1:
                    m.qk_used = [q_, k_, e, vt] if full else [e, vt]
                kt = []
                for i in range(2):
                    b = g4.next()
                    yield [e, b.free]
                    for n in range(NT):
                        t = tr(b.ap[:, 128 * n:128 * n + 128], tmp[:, i, 128 * n:128 * n + 128], ident, [e, b.free])
                    w = act(ktok[:, i], b.ap[:, 0:N], ACT.Copy, [t, idle, kt_done])
                    b.done(w)
                    kt.append(w)
                tmp_done = [t]
                cs = [None] * NCH
                for c0 in range(0, NCH, 4):
                    for p in range(2):
                        b = g4.next()
                        yield [kt, vt, b.free]
                        for x in range(2):
                            c = c0 + 2 * x + p
                            n = c // 2
                            for i in range(2):
                                t = mm(b.ap[:, 256 * x + 128 * i:256 * x + 128 * i + 128],
                                       ktok[hs[p], i, 128 * n:128 * n + 128], gvtok[hs[p], i, 128 * n:128 * n + 128],
                                       after=[kt, vt, b.free])
                        c = c0 + p
                        w = tt(Sen[:, c:c + 3:2], b.ap.rearrange("p (x i f) -> p x i f", x=2, i=2),
                               shared.bmask.unsqueeze(1).unsqueeze(1).broadcast_to([128, 2, 2, 128]),
                               ALU.mult, [t, idle, sen_done, shared.ready])
                        b.done(w)
                        cs[c] = cs[c + 2] = w
                kt_done = [t]
                order = list(range(NCH)) if d == 0 else list(range(NCH - 1, -1, -1))
                enter, e_ready = {}, {}
                cur, cr = (S0[:, d] if lat else S0[:]), [s_init]
                for c in order:
                    enter[c], e_ready[c] = cur, cr
                    cr = [stt(Sen[:, c, i], cur[:, i], dec[:, i, c:c + 1], Sen[:, c, i], ALU.mult, ALU.add,
                              [cr, dc, cs[c]]) for i in range(2)]
                    cur = Sen[:, c]
                if not lat:
                    m.S_out = m.S_out + [copy(r_S[:, d], cur, [cr, idle], eng="gpsimd")]
                    sen_done = [m.S_out]
                if not full:
                    continue
                for c in order:
                    yield [e_ready[c], q_, ob[0][0].free, ob[1][0].free]
                    for i in range(2):
                        t = mm(ob[i][1][:, 64 * c:64 * c + 64], enter[c][:, i], qin[:, i, 64 * c:64 * c + 64],
                               ob[i][0] not in o_begun, False, [e_ready[c], q_, ob[i][0].free])
                        o_begun.add(ob[i][0])
                sen_done = sen_done + [t]
                for x in range(2):
                    z_ = memset(aT[x][:], 0.0, [idle, at_done])
                    at_done = at_done + [z_]
                for n0 in range(0, NT, 2):
                    bh = [g4.next(), g4.next()]
                    yield [k_, q_, bh[0].free, bh[1].free]
                    cp = []
                    for h in range(2):
                        for x in range(2):
                            for i in range(2):
                                tk = slice(128 * (n0 + x), 128 * (n0 + x) + 128)
                                t = mm(bh[h].ap[:, 256 * x + 128 * i:256 * x + 128 * i + 128], kin[hs[h], i, tk],
                                       qin[hs[h], i, tk], after=[k_, q_, bh[h].free])
                        w = cpred(aT[h][:], over(tri[:, d]), heads(bh[h].ap), [t, at_done, ld_c])
                        bh[h].done(w)
                        cp.append(w)
                    yield [cp, vt]
                    for x in range(2):
                        for i in range(2):
                            for h in range(2):
                                tk = slice(128 * (n0 + x), 128 * (n0 + x) + 128)
                                t = mm(ob[i][1][hs[h], tk],
                                       gvtok[:, i, 128 * (n0 + x) + 64 * h:128 * (n0 + x) + 64 * h + 64],
                                       aT[h][:, 2 * x + i], False,
                                       d == 1 and n0 + x == NT - 1 and (i == 1 or not one_bank), [cp, vt])
                    at_done = [t]
                q_done, k_done = [t], [t]
            shared.wa.free = wa_done
            if not full:
                return
            m.mixed = [t]
            while not m.proj_done:
                yield POLL
            r_g = ready["gg"]
            squares = [act(tmp[:, i], ob[i][1][:, 0:N], ACT.Square, [t, tmp_done]) for i in range(2)]
            ends, ls = [], []
            for i in range(2):
                b = g4.next()
                yield [squares[i], b.free]
                x = mm(b.ap[:, 0:N], shared.onesbd, tmp[:, i], after=[squares[i], b.free])
                ls.append(act(C[:, i], b.ap[:, 0:N], ACT.Ln, [x], bias=EPS, scale=1.0 / 64))
                b.done(ls[-1])
            rs = act(C[:], C[:], ACT.Exp, ls, scale=-0.5)
            for i in range(2):
                w = tt(tmp[:, i], ob[i][1][:, 0:N], C[:, i], ALU.mult, [rs, x, squares])
                ends.append(w)
                w = stt(tmp[:, i], tmp[:, i], cv(GNORM + 2 * l + i), gg[:, i], ALU.mult, ALU.mult, [w, r_g])
                hi, lo = hin[i]
                a = act(hi.ap, tmp[:, i], ACT.Copy, [w, hi.free])
                e = tt(lo.ap, tmp[:, i], hi.ap.bitcast(F32), ALU.subtract, [a, lo.free])
                hi.ready, lo.ready = [a], [e]
                m.gla_end = [a, e]
            for i in range(2):
                ob[i][0].free = ends

        m.S_out, m.gla_end, m.qk_used, m.mixed = [], [], [], []
        m.gla = gla

        def store_ctx():
            ws = []
            yield from wait_for("nv0", "nv1", "nv2", "sv", "nk0", "nk1", "nk2", "sk")
            for i in range(3):
                b = g4.next()
                yield [ready[f"nv{i}"], b.free]
                for n in range(2):
                    t = tr(b.ap[:, 128 * n:128 * n + 128], nvT[:, i, 128 * n:128 * n + 128], ident,
                           [ready[f"nv{i}"], b.free])
                w = copy(r_nv[:, :, 128 * i:128 * i + 128], b.ap[:, 0:256].rearrange("p (n f) -> p n f", n=2), [t, idle])
                b.done(w)
                ws.append(w)
            b = g4.next()
            yield [ready["sv"], b.free]
            for n in range(2):
                t = tr(b.ap[:, 128 * n:128 * n + 128], svT[:, 128 * n:128 * n + 128], ident, [ready["sv"], b.free])
            w = copy(r_sv, b.ap[:, 0:256].rearrange("p (n f) -> p n f", n=2), [t, idle])
            b.done(w)
            ws.append(w)
            m.v_ready = ws
            keys = [ready[k] for k in ("nk0", "nk1", "nk2", "sk")]
            res_written[l] = P.dma("sync", res_dram[l], res[:], "res", [ws, keys, m.S_out])
        m.store_ctx = store_ctx

        class Mixed:

            def __init__(self, ch, cell, count, arrange):
                self.ch, self.cell, self.count, self.arrange, self.ws = ch, cell, count, arrange, []

        def attend(items, cells, sp, mem, x, idle2, ready_in):
            S, PT, bias_mem = mem
            st = sb(f"{nm}_st{x}{S.name}", (8.5 if lat else 8.75) + (x + 1) / 32, [8])
            least, sm_, rc, es = [st[:, j:j + 1] for j in range(4)]
            if bias_mem is not None:
                bb = Cell(bias_mem[:])
                zero = memset(bb.ap[:, 256:512], 0.0, [idle2])
            pt_done, s_done = [idle2], [idle2]
            m.open += 1
            while items:
                out, n_, p, q, keys, vals, bias, sink = items.pop(0)
                n = keys[-1][2]
                if bias and bias[0] == "dram":
                    bb.ready = [P.dma("sync", bb.ap[:, 0:256], bias[1], f"nab{x}", [bb.free, idle2]), zero]
                free = [c.free for c in cells]
                yield [ready_in, free]
                for ap, c0, c1 in keys:
                    t = mm(sp[:, c0:c1], q, ap, after=[ready_in, free])
                if bias:
                    mk, got = (bb.ap, bb.ready) if bias[0] == "dram" else bias[1:]
                    init = 3e38 if sink is None else sink
                    w = dve(lambda e, mk=mk, n=n, init=init: e.tensor_tensor_reduce(
                        S[:, 0:n], sp[:, 0:n], mk, -1.0, init, ALU.add, ALU.min, least),
                        [t, got, nsink_ready, s_done], n + 120)
                    if bias[0] == "dram":
                        bb.free = [w]
                    src = S[:, 0:n]
                    for c in cells:
                        c.free = [w]
                else:
                    w = dve(lambda e, n=n: e.tensor_reduce(least, sp[:, 0:n], AX.X, ALU.min), [t, s_done], n)
                    if sink is not None:
                        w = tt(least, least, sink, ALU.min, [w, nsink_ready])
                    src = sp[:, 0:n]
                r = act(S[:, 0:n], src, ACT.Exp, [w, s_done], bias=least, scale=-1.0, accum=sm_)
                ex = r
                if not bias:
                    for c in cells:
                        c.free = [ex]
                if sink is not None:
                    e2 = act(es, sink, ACT.Exp, [w], bias=least, scale=-1.0)
                    r = tt(sm_, sm_, es, ALU.add, [ex, e2])
                yield [ex]
                for j in range(n // 128):
                    t = tr(sp[:, 128 * j:128 * j + 128], S[:, 128 * j:128 * j + 128], ident,
                           [ex, [c.free for c in cells]])
                s_done = [t]
                r = dve(lambda e: e.reciprocal(rc, sm_), [r], 8)
                n0 = min(n, 512)
                if P.clock["scalar"] <= P.clock["vector"]:
                    e1 = act(PT[:, 0:n0], sp[:, 0:n0], ACT.Copy, [t, pt_done])
                else:
                    e1 = copy(PT[:, 0:n0], sp[:, 0:n0], [t, pt_done])
                cells[0].free = pe = [e1]
                if n > 512:
                    e2 = copy(PT[:, 512:n], sp[:, 512:n], [t, pt_done])
                    cells[1].free = [e2]
                    pe = pe + [e2]
                yield [pe, m.v_ready]
                for j, va in enumerate(vals):
                    t = mm(sp[:, 0:64], PT[:, 128 * j:128 * j + 128], va, j == 0, j == len(vals) - 1,
                           [pe, m.v_ready, cells[0].free])
                pt_done = [t]
                o = out.cell
                w = ts(o.ap[:, 128 * n_ + 64 * p:128 * n_ + 64 * p + 64], sp[:, 0:64], rc, ALU.mult, [t, r, o.free])
                s_done = s_done + [w]
                cells[0].free = [w]
                out.ws.append(w)
                m.end = m.end + [t, w]
                if len(out.ws) == out.count:
                    yield [out.ws]
                    for j in range(out.count // 2):
                        t = tr(sp[:, 128 * j:128 * j + 128], o.ap[:, 128 * j:128 * j + 128], ident,
                               [out.ws, cells[0].free])
                    o.done(t)
                    hi, lo = hin[out.ch]
                    src, to = out.arrange
                    a = act(to(hi.ap), src(sp[:, 0:N]), ACT.Copy, [t, hi.free])
                    b = tt(to(lo.ap), src(sp[:, 0:N]), to(hi.ap).bitcast(F32), ALU.subtract, [a, lo.free])
                    cells[0].free = [b]
                    hi.ready.append(a)
                    lo.ready.append(b)
                    m.end = m.end + [t, a, b]
            m.open -= 1

        m.open, m.end, m.last = 0, [], []

        def same(ap):
            return ap

        def begin_outputs():
            for c in range(2, 8):
                hin[c][0].ready, hin[c][1].ready = [], []

        def ctx_attention(sides):
            items = []
            turn = Ring([Cell(buf("nvT", [N], F32, x, f"o{x}")[:]) for x in range(3)])
            for i in range(6):
                out = Mixed(2 + i, turn.next(), 2 * NT, (same, same))
                out.cell.held = False
                for n in range(NT):
                    for p in range(2):
                        h = 2 * i + p
                        if i < 3:
                            items.append((out, n, p, nq[hs[p], i, 128 * n:128 * n + 128], [(r_nk[hs[p], i], 0, 256)],
                                          [r_nv[:, x, 64 * h:64 * h + 64] for x in range(2)], None, None))
                        else:
                            items.append((out, n, p, sq_[hs[p], i - 3, 128 * n:128 * n + 128], [(r_sk[hs[p], :], 0, 256)],
                                          [r_sv[:, x, 64 * p:64 * p + 64] for x in range(2)], None,
                                          nsink[:, 6 * l + 3 * p + i - 3:6 * l + 3 * p + i - 2]))
            begin_outputs()
            k_ready = [ready[k] for k in ready if k[:2] in ("nk", "nq", "sq", "sk")]
            for x in range(3):
                mem = [sb(f"{nm}_{a}{x}", base + 2 * x + i, [256]) for i, a in enumerate(("S", "PT"))] + [None]
                sides.insert(x, Side(attend(items, [bank[2 + x]], bank[2 + x].ap, mem, x, m.gla_end, k_ready), 2.0))
            while m.open or items:
                yield POLL

        def lat_attention(sides):
            g2 = Ring(bank[6:8])
            nvtok, svtok = buf("nvtok", [4, 2, 3, 128]), buf("svtok", [4, 128])
            ld = P.dma("sync", res[:, 0:2048], res_dram[l][:, 0:2048], f"res{l}", [m.res_idle, res_written[l]])
            yield from wait_for("nv0", "nv1", "nv2")
            while not m.qk_used:
                yield POLL
            vt = []
            for cb in range(4):
                c0 = min(max(16 * cb - 8, 0), 32)
                for x in range(2):
                    b = g2.next()
                    yield [b.free, [ready[f"nv{i}"] for i in range(3)], m.qk_used]
                    for i in range(3):
                        src = nvT[:, i, 256 * x + 4 * c0:256 * x + 4 * c0 + 128]
                        t = tr(b.ap[:, 128 * i:128 * i + 128], src, ident, [ready[f"nv{i}"], b.free])
                    w = (copy if x else acopy)(nvtok[:, cb, x].rearrange("p i f -> p (i f)"), b.ap[:, 0:384],
                                               [t, m.qk_used])
                    b.done(w)
                    vt.append(w)
            yield from wait_for("sq0", "sq1", "sq2", "sk", "sv")
            r_rope = yield from rope(g2)
            b = g2.next()
            yield [b.free, ready["sv"]]
            for n in range(4):
                t = tr(b.ap[:, 128 * n:128 * n + 128], svT[:, 128 * n:128 * n + 128], ident, [ready["sv"], b.free])
            w = copy(svtok[:].rearrange("p n f -> p (n f)"), b.ap, [t, idle])
            b.done(w)
            m.v_ready = vt + [w, ld]
            na, swa, na_sides = [], [], []
            turns = [Ring([Cell(buf(k, [N], F32, o, f"o{k}{x}")[:]) for x, (k, o) in enumerate(places)])
                     for places in ((("nvT", 0), ("nvT", 2)), (("nvT", 4), ("rope", 0)))]

            def by_rows(ap):
                return ap.rearrange("p (r b c) -> p b r c", r=8, b=4)

            def by_blocks(ap):
                return ap.rearrange("p (b r c) -> p b r c", r=8, b=4)
            for i in range(3):
                out = Mixed(2 + i, turns[0].next(), 8, (by_blocks, by_rows))
                out.cell.held = False
                for n in range(NT):
                    for p in range(2):
                        h = 2 * i + p
                        c0 = min(max(16 * n - 8, 0), 32)
                        kw = nk[hs[p], i].rearrange("p (x w) -> p x w", x=2)[:, :, 4 * c0:4 * c0 + 128]
                        na.append((out, n, p, nq[hs[p], i, 128 * n:128 * n + 128],
                                   [(kw, 0, 256), (r_nk[hs[p], i], 256, 512)],
                                   [nvtok[:, n, x, i, hs[p]] for x in range(2)] +
                                   [r_nv[:, x, 64 * h:64 * h + 64] for x in range(2)],
                                   ("dram", io["na_bias"][l, h, n]), None))
            swm = buf("swm", [1152])
            ldm = []
            for i in range(3):
                out = Mixed(5 + i, turns[1].next(), 8, (same, same))
                out.cell.held = False
                for n in range(NT):
                    for p in range(2):
                        lo, hi = max(n - 1, 0), min(n + 2, 4)
                        w = 128 * (hi - lo)
                        keys = [(sk[hs[p], 128 * lo:128 * hi], 0, w)]
                        if w == 384:
                            keys += [(r_sk[hs[p], 0:128], 384, 512), (r_sk[hs[p], 128:256], 512, 640)]
                        else:
                            keys += [(r_sk[hs[p], :], 256, 512)]
                        vals = [svtok[:, x, 64 * p:64 * p + 64] for x in range(lo, hi)] + \
                               [r_sv[:, x, 64 * p:64 * p + 64] for x in range(2)]
                        mask = swm[:, 128:640] if n == 0 else swm[:, 640:1152] if n == 3 else swm[:, 0:640]
                        swa.append((out, n, p, sq_[hs[p], i, 128 * n:128 * n + 128], keys, vals, ("sbuf", mask, ldm),
                                    nsink[:, 6 * l + 3 * p + i:6 * l + 3 * p + i + 1]))
            while not m.mixed or not m.proj_done:
                yield POLL
            begin_outputs()
            k_ready = [ready[k] for k in ready if k[:2] in ("nk", "nq")] + [ld]
            for x in range(2):
                mem = [sb(f"{nm}_{a}{x}", base + 26 + 6 * x + 2 * i, [512]) for i, a in enumerate(("NS", "NPT", "NB"))]
                na_sides.append(Side(attend(na, [bank[6 + x]], bank[6 + x].ap, mem, x, m.mixed, k_ready), 2.0))
            sides[0:0] = na_sides
            while not m.gla_end:
                yield POLL
            ldm.append(P.dma("sync", swm[:], io["swa_mask"], "swm", [m.gla_end]))

            def window(x, k, off, after):
                sp = psum[:, k:k + 2, :].rearrange("p a b -> p (a b)")
                mem = [sb(f"{nm}_{a}{x}", base + off + 2.5 * i, [640]) for i, a in enumerate(("SS", "SPT"))]
                return Side(attend(swa, bank[k:k + 2], sp, mem + [None], 2 + x, after, [r_rope, ld]), 2.0)
            for x, off in ((2, 12), (3, 48)):
                mem = [sb(f"{nm}_{a}{x}", base + off + 2 * i, [512]) for i, a in enumerate(("NS", "NPT", "NB"))]
                na_sides.append(Side(attend(na, [bank[x - 2]], bank[x - 2].ap, mem, 5 + x, m.gla_end, k_ready), 2.0))
            sides[0:0] = na_sides[2:] + [window(0, 2, 38, m.gla_end), window(1, 4, 43, m.gla_end)]
            yield
            while na or any(x.alive for x in na_sides):
                yield POLL
            m.na_done = True
            sides.insert(0, window(2, 6, 26, m.end))
            yield
            while m.open or swa:
                yield POLL
            m.swa_done = True
        m.na_done = m.swa_done = False

        def rope(g8):
            rt = buf("rope", [T])
            done, out = [], []
            cos, sin = c2[:, COS:COS + T], c2[:, SIN:SIN + T]
            for x, key in [(sq_[:, 0], "sq0"), (sq_[:, 1], "sq1"), (sq_[:, 2], "sq2"), (sk[:], "sk")]:
                b = g8.next()
                yield [ready[key], b.free]
                t = mm(b.ap, c2[:, PERM:PERM + 128], x, after=[ready[key], b.free, shared.ready])
                w = tt(rt[:], b.ap, sin, ALU.mult, [t, done, idle])
                b.done(w)
                w2 = tt(x, x, cos, ALU.mult, [t], eng="gpsimd")
                w = tt(x, x, rt[:], ALU.add, [w, w2])
                done = [w]
                out.append(w)
            return out
        m.attention = lat_attention if lat else ctx_attention
        return m

    def acopy(out, in_, after=()):
        return act(out, in_, ACT.Copy, after)

    def out_units(l, v, N, pairs, x, nrm, after=()):
        def evac(part, o):
            def run(bks, done):
                w = stt(x[o[0]].ap, bks[0].ap[:, 0:N], modv(l, v, 16 + o[0]), x[o[0]].ap, ALU.mult, ALU.add,
                        [done, x[o[0]].ready, mod_ready[l]])
                bks[0].done(w)
                x[o[0]].ready = [w]
                if part:
                    nrm.add(o[0], [w], after)
                o.pop(0)
            return run
        units = []
        for part in range(2):
            for s in range(4):
                u = Unit(io["w_out2"][l * 8 + 4 * part + s], lambda part=part: whole(*[pairs[4 * part:4 * part + 4]] * 2),
                         evac(part, [2 * s, 2 * s + 1]), None, lo="any" if v else "vector")
                u.each = True
                units.append(u)
        return units

    def ffn_units(l, v, N, pairs, x, nrm, places, ring, after):
        nm = f"f{v}{l}"
        hid = [tuple(Cell(sb(f"{nm}h{k}{y}", places[2 * k + y], [N], F32R)[:]) for y in range(2)) for k in range(HALF)]
        sg = Ring([Cell(sb(f"{nm}sg{i}", places[2 * HALF + i], [N])) for i in range(2)])
        held = {}
        units = []
        lo_eng = "any" if v else "vector"

        def gate(k):
            def run(bks, done):
                c = held[k] = sg.next()
                a = act(c.ap[:], bks[0].ap[:, 0:N], ACT.Silu, [done, c.free, after])
                bks[0].done(a)
                c.ready = [a]
            return run

        def up(k):
            def run(bks, done):
                c = held.pop(k)
                hi, lo = hid[k % HALF]
                w = tt(c.ap[:], bks[0].ap[:, 0:N], c.ap[:], ALU.mult, [done, c.ready])
                bks[0].done(w)
                a = act(hi.ap, c.ap[:], ACT.Copy, [w, hi.free, after])
                b = tt(lo.ap, c.ap[:], hi.ap.bitcast(F32), ALU.subtract, [a, lo.free, after])
                c.done(b)
                hi.ready, lo.ready = [a], [b]
            return run

        def down_groups(s):
            def run():
                out = []
                for b in range(8 * s, 8 * s + 8):
                    o, k = divmod(b, HALF)
                    if not out or out[-1][0] != (nm, o):
                        out.append([(nm, o), [], k == 0, False])
                    out[-1][1].append(hid[k])
                    out[-1][3] = k == HALF - 1
                return out
            return run

        def down(half, s):
            ends = [b // HALF for b in range(8 * s, 8 * s + 8) if b % HALF == HALF - 1]

            def run(bks, done):
                for o, bk, t in zip(ends, bks, done):
                    w = stt(x[o].ap, bk.ap[:, 0:N], modv(l, v, 40 + o), x[o].ap, ALU.mult, ALU.add, [t, x[o].ready])
                    bk.done(w)
                    x[o].ready = [w]
                    if half:
                        nrm.add(o, [w])
            return run

        for half in range(2):
            for k in range(HALF * half, HALF * half + HALF):
                units.append(Unit(io["w_gate2"][l * 22 + k], lambda: whole(pairs), gate(k), ring, lo=lo_eng))
                units.append(Unit(io["w_up2"][l * 22 + k], lambda: whole(pairs), up(k), ring, lo=lo_eng))
            for s in range(HALF):
                units.append(Unit(io["w_down2"][(l * 2 + half) * HALF + s], down_groups(s), down(half, s), ring,
                                  lo=lo_eng))
        return units

    TC = 256
    xct = sb("xct", 113, [KC, TC])
    xc = [Cell(xct[:, c, :]) for c in range(KC)]
    hct = [sb("hchi", 97, [KC, TC], F32R), sb("hclo", 105, [KC, TC], F32R)]
    hc = [(Cell(hct[0][:, c]), Cell(hct[1][:, c])) for c in range(KC)]
    hl = list(zip(hhi, hlo))
    ctx_late = Ring(bank[2:5])
    cnorm = Norm("cn", 121, TC, xc, ctx_late)
    idle_c, idle_l = [[], []], [[], []]
    cm = [make_mixer(l, 1, TC, kb, hc, l == 0, idle_c[l], ctx_in) for l, kb in ((0, 145), (1, 163))]
    lm = [make_mixer(l, 0, T, M0 + 12, hl, True, idle_l[l], lat_in) for l in range(2)]
    after_c, after_l = [], [[], []]
    u_cout = out_units(0, 1, TC, hc, xc, cnorm)
    u_cffn = ffn_units(0, 1, TC, hc, xc, cnorm, list(range(145, 152)) + list(range(168, 185)), ctx_late, after_c)
    u_lout = [out_units(l, 0, T, hl, xr, norm, lm[l].last) for l in range(2)]
    u_lffn = [ffn_units(l, 0, T, hl, xr, norm, [M0 + 12 + 2 * i for i in range(24)], late_banks, after_l[l])
              for l in range(2)]

    def mixed(main, other):
        out, n = [], 0
        for i, u in enumerate(main):
            upto = -(-len(other) * (i + 1) // len(main))
            out += other[n:upto] + [u]
            n = upto
        return out

    def frontier():
        return [P.queues[e][-1] for e in ("tensor", "vector", "scalar", "gpsimd")]

    NWQ = 3
    m0, m1 = mod_units
    spine += mixed(u_dn, m0[:32]) + u_da + u_z + mixed(u_merge, m0[32:]) + u_out
    w1 = cm[0].units[:6] + mixed(cm[0].units[6:], u_wq[:NWQ])
    spine += mixed(w1 + u_wq[NWQ:] + u_cout + u_cffn, m1) + cm[1].units + u_peer
    for l in range(2):
        spine += lm[l].units + u_lout[l] + u_lffn[l]

    def mixers(m, out):
        m.res_idle = frontier()
        sides = []
        sides += [Side(m.gla(), 2.0), Side(m.attention(sides))]
        run_spine(len(m.units), sides)
        m.proj_done = True
        drain(sides, lambda: m.na_done)
        run_spine(4, sides)
        drain(sides)
        m.last += m.end
        run_spine(4, sides)

    def ctx_mixers(m, sides):
        yield from m.gla()
        yield from m.store_ctx()
        if m.full:
            yield from m.attention(sides)

    selected = []
    x_dram = nc.dram_tensor("residual", [128, KC, T], F32, kind="Internal").ap()

    def choose():
        sel = yield from top_keys()
        selected.append(sel)
        for c in range(KC):
            xc[c].ready = [P.dma("sync", xc[c].ap, io["ctxT"][:, c, :], f"c{c}",
                                 [sel, [k.free for k in pq.cells + keys.cells]])]
        yield from top_pairs(sel)

    def gate():
        yield from dense_gates()
        for c in range(KC):
            xr[c].ready = [P.dma("sync", xr[c].ap, x_dram[:, c, :], f"x{c}", [g_readers])]
        for c in range(KC):
            yield [xr[c].ready]
        yield from norm.apply(lambda c: cv(G_FFN + c), hl, None, to_tokens)
        for p, q in zip(hd, hl):
            for x, y in zip(p, q):
                x.ready = y.ready

    start_mod()
    first_norm()
    start_conv([c.ready for c in hlo])
    run_spine(13, [])
    mod_finish()
    sides = [Side(dilated())]
    sides.insert(0, Side(delta(sides)))
    run_spine(36, sides)
    run_spine(4, sides)
    drain(sides)
    chain_end = [S_ready, o_ready]
    for c in range(KC):
        xr[c].ready = [P.dma("sync", xr[c].ap, io["xT"][:, c, :], f"x{c}", [chain_end] + [a.ready for a in odn_c[3]])]
    sides = [Side(finish_mixers(chain_end))]
    run_spine(2, sides)
    drain(sides)
    msb_free[:] = frontier()
    run_spine(22, [])
    mod_finish()

    def ctx_norm():
        for c in range(KC):
            xc[c].ready = [P.dma("sync", xc[c].ap, io["ctxT"][:, c, :], f"c{c}", idle)]
        for c in range(KC):
            yield [xc[c].ready]
            cnorm.add(c, xc[c].ready, idle)
        for p in hc:
            for x in p:
                x.free = idle
        yield from cnorm.apply(lambda c: amod[:, 0, 1, 0, c:c + 1], hc, lambda c: modv(0, 1, c))
    idle = frontier()
    sides = [Side(ctx_norm())]
    run_spine(8, sides)
    drain(sides)
    norm.rs()
    idle_c[0] += frontier()
    ctx_in.ready.append(P.dma("sync", c2c[:], io["consts2"][:, NC2:], "c2c", idle_c[0]))
    wq_idle += idle_c[0] + flat([c.ready for c in xc])
    msb_free[:] = idle_c[0]

    saved = [P.dma("sync", x_dram[:, c, :], xr[c].ap, f"x{c}", [xr[c].ready]) for c in range(KC)]
    sides = [Side(norm.apply(lambda c: cv(G_FFN + c), hl))]
    run_spine(6, sides)
    drain(sides)
    saved += norm.used
    sides.append(Side(ctx_mixers(cm[0], sides), 2.0))
    sides.append(Side(gate()))
    sides.append(Side(choose()))
    run_spine(17 + NWQ, sides)
    cm[0].proj_done = True
    run_spine(16 - NWQ, sides)
    drain(sides, lambda: cm[0].gla_end)
    g_idle += saved + cm[0].gla_end
    drain(sides, lambda: cm[0].end and not cm[0].open and selected)
    after_c += cm[0].end + cm[0].gla_end
    run_spine(8, sides)

    def until_done(side):
        s = Side(side)
        sides.insert(0, s)
        drain(sides, lambda: not s.alive)
    until_done(cnorm.apply(lambda c: amod[:, 0, 1, 1, c:c + 1], hc, lambda c: modv(0, 1, 24 + c)))
    run_spine(len(u_cffn), sides)
    mod_finish()
    until_done(cnorm.apply(lambda c: amod[:, 1, 1, 0, c:c + 1], hc, lambda c: modv(1, 1, c)))
    drain(sides, lambda: g_readers)
    idle_c[1] += frontier() + [res_written[0]] + g_written
    gin[0].free = frontier() + g_written
    load_gates(0)
    sides.insert(0, Side(ctx_mixers(cm[1], sides), 2.0))
    run_spine(13, sides)
    drain(sides)
    end_w = frontier() + [res_written[1]]
    gin[1].free = end_w
    for p in agc[0] + agc[1]:
        for x in p:
            x.free = end_w
    for c in uact.cells:
        c.free = end_w
    load_gates(1)
    sides.append(Side(chosen_experts(end_w)))
    run_spine(GJ, sides)
    for g in range(NGR):
        if g + 2 < NGR:
            load_gates(g + 2)
        if g + 1 == NGR:
            drain(sides)
        run_spine(16 if g + 1 < NGR else 8, sides)
    for p, q in zip(hd, hl):
        for x, y in zip(p, q):
            y.free = x.free
    rs = norm.rs()
    for c in range(KC):
        w = stt(xr[c].ap, xr[c].ap, cv(G_FIN + c), norm.r[:], ALU.mult, ALU.mult, [rs, xr[c].ready])
        xr[c].ready = [w]
        norm.used = [w]
        norm.add(c, [w])
    if until == "x1":
        P.emit(sem_of)
        return locals()
    lat_in.ready.append(P.dma("sync", c2[:], io["consts2"][:, 0:NC2], "c2", xr[7].ready))
    for l in range(2):
        idle_l[l] += flat(xr[7].ready)
        drain([Side(norm.apply(lambda c: amod[:, l, 0, 0, c:c + 1], hl, lambda c: modv(l, 0, c)))])
        mixers(lm[l], u_lout[l])
        if until == f"lat{l}y":
            P.emit(sem_of)
            return locals()
        after_l[l] += flat(xr[7].ready)
        drain([Side(norm.apply(lambda c: amod[:, l, 0, 1, c:c + 1], hl, lambda c: modv(l, 0, 24 + c)))])
        run_spine(len(u_lffn[l]), [])
        if until == f"lat{l}":
            P.emit(sem_of)
            return locals()
    rs = norm.rs()
    for c in range(KC):
        w = stt(xr[c].ap, xr[c].ap, cv(N2FIN + c), norm.r[:], ALU.mult, ALU.mult, [rs, xr[c].ready])
        P.dma("sync", io["out"][:, c, :], xr[c].ap, f"x{c}", [w])
    P.emit(sem_of)
    return locals()


def constants(a):
    c = np.zeros((128, NCONST), np.float32)
    i = np.arange(128)
    c[:, IDENT:IDENT + 128] = np.eye(128)
    c[:, UF:UF + 128] = i[:, None] <= i[None, :]
    c[:, UB:UB + 128] = i[:, None] >= i[None, :]
    c[:, MASKF:MASKF + 128] = np.where(i[None, :] <= i[:, None], 0.0, NEG)
    c[:, MASKB:MASKB + 128] = np.where(i[None, :] >= i[:, None], 0.0, NEG)

    def cols(v):
        return v.reshape(-1, 128).T
    c[:, G_MIX:G_MIX + 8] = cols(a["norm_mix"][0])
    c[:, G_FFN:G_FFN + 8] = cols(a["norm_ffn"][0])
    c[:, G_FIN:G_FIN + 8] = cols(a["norm_final"])
    c[:, CONVW:CONVW + 48] = a["dn_conv"][0].reshape(4, 12, 128).transpose(2, 1, 0).reshape(128, 48)
    c[:, DTB:DTB + 8] = a["dn_dt_bias"][0].reshape(1, 8)
    c[:, ALOG:ALOG + 8] = a["dn_a_log"][0].reshape(1, 8)
    for l in range(2):
        c[:, BMOD + 48 * l:BMOD + 48 * l + 48] = cols(a["b_mod_2"][l])
        c[:, N2MIX + 8 * l:N2MIX + 8 * l + 8] = cols(a["norm_mix_2"][l])
        c[:, N2FFN + 8 * l:N2FFN + 8 * l + 8] = cols(a["norm_ffn_2"][l])
        c[:, GBA + 4 * l:GBA + 4 * l + 2] = cols(a["gla_ba_f_2"][l])
        c[:, GBA + 4 * l + 2:GBA + 4 * l + 4] = cols(a["gla_ba_b_2"][l])
        c[:, GNORM + 2 * l:GNORM + 2 * l + 2] = cols(a["gla_norm_2"][l])
        c[:, SINK + 6 * l:SINK + 6 * l + 6] = a["swa_sink_2"][l][None, :]
    c[:, N2FIN:N2FIN + 8] = cols(a["final_norm_2"])
    c[:, CVEC:CVEC + 8] = cols(a["c_2"][0])
    c[:, CVEC + 8:CVEC + 16] = cols(a["c_ctx_2"])
    c[:, IOTA:IOTA + 128] = i[None, :]
    c[:, ONORM:ONORM + 1] = a["dn_out_norm"][0][:, None]
    return c


def level_masks():
    i = np.arange(128)
    out = np.zeros((128, 2, len(LEVELS), 128), np.float32)
    for n, b in enumerate(LEVELS):
        same = (i[:, None] // (2 * b)) == (i[None, :] // (2 * b))
        lower = same & ((i[:, None] // b) % 2 == 1) & ((i[None, :] // b) % 2 == 0)
        out[:, 0, n], out[:, 1, n] = lower, lower.T
    return out


def slabs(w):
    k, n = w.shape
    pad = -n % 128
    if pad:
        w = np.concatenate([w, np.zeros((k, pad), w.dtype)], axis=1)
    return np.ascontiguousarray(w.reshape(k // 128, 128, -1, 128).transpose(2, 1, 0, 3).reshape(-1, 128, k))


def feature_major(x):
    t, d = x.shape
    return np.ascontiguousarray(x.reshape(t, d // 128, 128).transpose(2, 1, 0))


def t5_bucket(rel):
    n = np.abs(rel)
    large = 8 + (np.log(np.maximum(n, 1) / 8) / np.log(1024 / 8) * 8).astype(np.int64)
    large = np.minimum(large, 15)
    return np.where(rel > 0, 16, 0) + np.where(n < 8, n, large)


def dilated_bias(rel_bias):
    l = np.arange(128)
    out = np.zeros((4, 4, 128, 768), np.float32)
    for r in range(4):
        q = (4 * l + r)[:, None]
        k0 = (4 * l[None, :] + np.arange(4)[:, None]).reshape(1, -1)
        k1 = (4 * l + r)[None, :]
        for g, (k, col) in enumerate(((k0, 0), (k1, 512), (k1, 640))):
            rel = k - q
            valid = (np.abs(rel) <= 64, np.abs(rel) <= 256, rel % 16 == 0)[g]
            b = t5_bucket(rel)
            for h in range(4):
                out[h, r, :, col:col + k.shape[1]] = np.where(valid, rel_bias[b, 4 * g + h], np.float32(NEG))
    return out


def constants2():
    c = np.zeros((128, NC2 + NC2C), np.float32)
    t = np.arange(T, dtype=np.int32)
    f32 = np.float32
    inv = (f32(10000.0) ** (-np.arange(16, dtype=f32) / f32(16))).astype(f32)
    ang = np.concatenate([(t // 64).astype(f32)[:, None] * inv, (t % 64).astype(f32)[:, None] * inv], axis=1)
    p = np.arange(128)
    c[:, COS:COS + T] = np.cos(ang).T[p % 32]
    c[:, SIN:SIN + T] = np.sin(ang).T[p % 32] * np.where(p % 64 < 32, -1.0, 1.0)[:, None]
    c[:, PERM:PERM + 128] = (p[:, None] ^ 32) == p[None, :]
    c[:, RSTF:RSTF + T] = t % 64 != 0
    c[:, RSTB:RSTB + T] = t % 64 != 63
    same = (p[:, None] // 64) == (p[None, :] // 64)
    c[:, ONESBD:ONESBD + 128] = same
    c[:, BMASK:BMASK + 128] = same
    c[:, NC2:NC2 + 256], c[:, NC2 + 256:NC2 + 512] = c[:, RSTF:RSTF + 256], c[:, RSTB:RSTB + 256]
    c[:, NC2 + 512:] = c[:, ONESBD:ONESBD + 256]
    return c


def tri_masks():
    p = np.arange(128)
    same = (p[:, None] // 64) == (p[None, :] // 64)
    out = np.zeros((128, 2, 128), np.float32)
    out[:, 0], out[:, 1] = same & (p[:, None] <= p[None, :]), same & (p[:, None] >= p[None, :])
    return out


def window_masks():
    q, k = np.arange(128)[:, None], np.arange(128)[None, :]
    left, right = np.where(k >= q, 0.0, NEG), np.where(k <= q, 0.0, NEG)
    z = np.zeros((128, 128))
    return np.concatenate([left, z, right, z, z, left, z, z, z], axis=1).astype(np.float32)


def grid_bias(rpb):
    out = np.zeros((2, 6, 4, 128, 256), np.float32)
    qr, qc = np.divmod(np.arange(128), 16)
    k = np.arange(256)
    kr, kc = 4 * (k // 128) + k % 4, (k % 128) // 4
    for b in range(4):
        col = kc + min(max(16 * b - 8, 0), 32)
        qcol = qc + 16 * b
        start = np.clip(qcol - 8, 0, 48)[:, None]
        valid = (col[None, :] >= start) & (col[None, :] < start + 16)
        dr = kr[None, :] - qr[:, None] + 7
        dc = np.clip(col[None, :] - qcol[:, None] + 15, 0, 30)
        out[:, :, b] = np.where(valid[None, None], rpb[:, :, dr, dc], np.float32(NEG))
    return out


def decay_weights(wf, wb):
    out = np.zeros((2, 128, 2, 256), np.float32)
    out[:, 0:16, 0], out[:, 16:32, 1] = wf, wb
    return out.reshape(2, 128, 512)


SWA_ORDER = np.concatenate([np.arange(64) + 64 * h for h in (0, 3, 1, 4, 2, 5)])


def in_slabs(w):
    w = np.concatenate([w[:, :1056], np.zeros((D, 96), w.dtype), w[:, 1056:2208], w[:, 2208 + SWA_ORDER], w[:, 2592:]],
                       axis=1)
    return slabs(w)


def out_slabs(w):
    w = w.reshape(2, 4, 128, 4, 2, 128).transpose(0, 3, 2, 4, 1, 5)
    return w.reshape(8, 128, 1024)


def down_slabs(w):
    w = w.reshape(2, HALF, 128, 8, 128).transpose(0, 3, 1, 2, 4).reshape(2, HALF, 8, 128, 128)
    return w.transpose(0, 1, 3, 2, 4).reshape(2 * HALF, 128, 1024)


def two(f, w):
    return np.ascontiguousarray(np.concatenate([f(w[0]), f(w[1])], axis=0))


def layout(a):
    w = a["w_in"][0]
    w = np.concatenate([w[:, :2048], w[:, 2048:2064], np.zeros((D, 112), w.dtype), w[:, 2064:]], axis=1)
    return {"consts": constants(a), "masks": np.concatenate([level_masks().reshape(128, -1), tri_masks().reshape(128, -1)], axis=1), "xT": feature_major(a["x"][0]), "w_in": slabs(w),
            "da_bias": dilated_bias(a["rel_bias"]),
            "w_br": np.concatenate([slabs(a["w_branch_dn"][0]), slabs(a["w_branch_da"][0])], axis=2),
            "w_out": slabs(a["w_out"][0]),
            "peer_wq": slabs(a["peer_wq"][0]),
            "peer_keys": np.ascontiguousarray(a["peer_sub_keys"][0].reshape(16, 128, 128).transpose(2, 0, 1)),
            "peer_u": np.ascontiguousarray(a["peer_u"][0].reshape(128, 128, 8, 128).transpose(1, 3, 2, 0)
                                           .reshape(128, 128, 1024)),
            "peer_v": np.ascontiguousarray(a["peer_v"][0].reshape(128, 16, 8, 8, 128).transpose(1, 3, 0, 2, 4)
                                           .reshape(128, 128, 1024)),
            "peer_u_rows": a["peer_u"][0],
            "peer_v_rows": a["peer_v"][0],
            "consts2": constants2(),
            "swa_mask": window_masks(),
            "na_bias": grid_bias(a["na_rpb_2"]),
            "wa2": decay_weights(a["gla_wa2_f_2"], a["gla_wa2_b_2"]),
            "ctxT": feature_major(a["ctx_2"][0]),
            "w_mod": np.ascontiguousarray(a["w_mod_2"].reshape(2, 8, 128, 3, 2, 1024).transpose(0, 3, 1, 4, 2, 5)
                                          .reshape(96, 128, 1024)),
            "w_in2": two(in_slabs, a["w_in_2"]),
            "w_out2": two(out_slabs, np.concatenate([a["w_out_2"][:, :640], a["w_out_2"][:, 640 + SWA_ORDER]], axis=1)),
            "w_gate2": two(slabs, a["w_gate_2"]),
            "w_up2": two(slabs, a["w_up_2"]),
            "w_down2": two(down_slabs, a["w_down_2"])}


def _build(nc, arrays):
    io = {n: nc.dram_tensor(n, v.shape, mybir.dt.from_np(v.dtype), kind="ExternalInput").ap() for n, v in arrays.items()}
    io["out"] = nc.dram_tensor("out_0_dram", (128, KC, T), F32, kind="ExternalOutput").ap()
    program(nc, io)


def kernel(**inputs):
    import concourse.bacc as _bacc
    from concourse.bass_utils import run_bass_kernel_spmd as _run

    arrays = layout({n: np.ascontiguousarray(v) for n, v in inputs.items()})
    nc = _bacc.Bacc("TRN2", target_bir_lowering=False, num_devices=1)
    _build(nc, arrays)
    r = _run(nc, [arrays], core_ids=[0])
    out = np.asarray(r.results[0]["out_0_dram"])
    return np.ascontiguousarray(out.transpose(2, 1, 0).reshape(1, T, D))
```

```python
import numpy as np
import concourse.bass as bass
from concourse import mybir

F32 = mybir.dt.float32
F32R = mybir.dt.float32r
U8 = mybir.dt.uint8
U32 = mybir.dt.uint32
I32 = mybir.dt.int32
ALU = mybir.AluOpType
ACT = mybir.ActivationFunctionType
AX = mybir.AxisListType

T = 512
TD = 384
D = 1024
KC = 8
EPS = 1e-6
NEG = -1e30

IDENT, UF, UB, MASKF, MASKB = 0, 128, 256, 384, 512
G_MIX, G_FFN, G_FIN = 640, 648, 656
CONVW = 664
DTB, ALOG, ONORM = 712, 720, 728
IOTA = 736
BMOD, N2MIX, N2FFN, N2FIN = 864, 960, 976, 992
CVEC, GBA, GNORM, SINK = 1000, 1016, 1024, 1028
NCONST = 1040
COS, SIN, PERM, RSTF, RSTB, ONESBD, BMASK = 0, 512, 1024, 1152, 1664, 2176, 2304
NC2, NC2C = 2432, 768
HALF = 11
LEVELS = (1, 2, 4, 8, 16, 32)


class Op:
    __slots__ = ("eng", "fn", "after", "asked", "sem", "count", "end")

    def __init__(self, eng, fn, after):
        self.eng, self.fn, self.after = eng, fn, after
        self.asked, self.sem, self.count, self.end = False, None, 0, 0


def flat(x):
    if x is None:
        return []
    if isinstance(x, Op):
        return [x]
    out = []
    for y in x:
        out += flat(y)
    return out


class Plan:

    def __init__(self, nc):
        self.nc = nc
        self.queues = {e: [] for e in ("tensor", "vector", "scalar", "gpsimd", "sync")}
        self.dmas = []
        self.dma_counts = {}
        self.clock = {e: 0 for e in self.queues}
        self.clock["dma"] = 0

    def op(self, eng, fn, after=(), cost=200):
        o = Op(eng, fn, flat(after))
        start = self.clock[eng]
        for a in o.after:
            a.asked = True
            if eng != "tensor" or a.eng != eng:
                start = max(start, a.end + (200 if a.eng == "tensor" else 130))
        o.end = self.clock[eng] = start + cost
        self.queues[eng].append(o)
        return o

    def dma(self, eng, out, in_, sem, after=()):
        return self.counted(self.op(eng, lambda e: e.dma_start(out, in_), after, 60), sem, width(out))

    def counted(self, o, sem, size):
        self.clock["dma"] = max(self.clock["dma"], o.end) + 4 * 128 * size / DMA_RATE
        o.end = self.clock["dma"] + 2000
        n = self.dma_counts.get(sem, 0) + 16
        self.dma_counts[sem] = n
        o.sem, o.count = sem, n
        self.dmas.append(o)
        return o

    def gather(self, out, table, rows, sem, after=()):
        o = self.op("gpsimd", lambda e: e.indirect_dma_start(out, None, table, bass.IndirectOffsetOnAxis(ap=rows, axis=0)),
                    after, 1040)
        return self.counted(o, sem, width(out))

    def emit(self, sem_of):
        for eng, queue in self.queues.items():
            n = 0
            for o in queue:
                if o.sem is None and o.asked:
                    n += 1
                    o.sem, o.count = eng, n
        with self.nc.Block() as block:
            for eng, queue in self.queues.items():
                getter = {"tensor": block.tensor, "vector": block.vector, "scalar": block.scalar,
                          "gpsimd": block.gpsimd, "sync": block.sync}[eng]
                getter(self.body(eng, queue, sem_of))

    def body(self, eng, queue, sem_of):
        def run(e):
            seen = {}
            for o in queue:
                need = {}
                for a in o.after:
                    need[a.sem] = max(need.get(a.sem, 0), a.count)
                for sem, count in need.items():
                    if seen.get(sem, 0) < count:
                        e.wait_ge(sem_of(sem), count)
                        seen[sem] = count
                ins = o.fn(e)
                if o.sem is not None:
                    ins.then_inc(sem_of(o.sem), 16 if o.sem != eng else 1)
            if eng == "sync":
                for sem, count in self.dma_counts.items():
                    if seen.get(sem, 0) < count:
                        e.wait_ge(sem_of(sem), count)
        return run


def width(ap):
    n = 1
    for x in ap.shape[1:]:
        n *= x
    return n


POLL = "come back later"
DMA_RATE = 300


class Side:

    def __init__(self, gen, lag=1.0):
        self.gen, self.want, self.alive, self.polled, self.lag = gen, [], True, -1, lag

    def step(self):
        try:
            w = next(self.gen)
        except StopIteration:
            self.alive, self.want = False, []
            return
        self.want = POLL if w is POLL else flat(w)


class Cell:

    def __init__(self, ap, plain=None):
        self.ap, self.plain, self.ready, self.free, self.held = ap, plain, [], [], False

    def done(self, *readers):
        self.free, self.held = flat(readers), False


class Ring:
    def __init__(self, cells):
        self.cells, self.n = cells, 0

    def next(self):
        for _ in self.cells:
            c = self.cells[self.n % len(self.cells)]
            self.n += 1
            if not c.held:
                c.held = True
                return c
        raise AssertionError("every cell is in use")


def program(nc, io):
    P = Plan(nc)
    sems = {}

    def sem_of(name):
        if name not in sems:
            sems[name] = nc.alloc_semaphore("s_" + name)
        return sems[name]

    BASE = 16512

    def sb(name, kb, shape, dt=F32):
        return nc.alloc_sbuf_tensor_at(name, [128] + list(shape), dt, offset=BASE + int(kb * 1024))

    psum = nc.alloc_psum_tensor("ps", [128, 8, 512], F32)
    bank = [Cell(psum[:, i, :]) for i in range(8)]

    def mm(out, lhsT, rhs, start=True, stop=True, after=(), at=None):
        if rhs.dtype == F32R:
            cost = max(0.43 * width(rhs), 106)
        elif width(lhsT) <= 64 and at is None:
            cost = 30 + 0.82 * width(rhs)
        else:
            cost = max(1.67 * width(rhs), 214) * (1 if at is None else 0.27)
        if at is None:
            return P.op("tensor", lambda e: e.matmul(out, lhsT, rhs, start=start, stop=stop), after, cost)
        return P.op("tensor", lambda e: e.matmul(out, lhsT, rhs, start=start, stop=stop, tile_position=at), after, cost)

    def tr(out, in_, idn, after=()):
        return P.op("tensor", lambda e: e.transpose(out, in_, idn), after, 145)

    tables = {ACT.Exp: 0, ACT.Ln: 4, ACT.Sqrt: 5, ACT.Silu: 1, ACT.Sigmoid: 2, ACT.Gelu_apprx_tanh: 3}
    table = [0]

    def act(out, in_, func, after=(), bias=0.0, scale=1.0, accum=None):
        cost = 60 + 0.87 * width(in_) + (0 if accum is None else 280)
        if tables.get(func, table[0]) != table[0]:
            table[0] = tables[func]
            cost += 1280
        if accum is None:
            return P.op("scalar", lambda e: e.activation(out, in_, func, bias=bias, scale=scale), after, cost)
        return P.op("scalar", lambda e: e.activation(out, in_, func, bias=bias, scale=scale, accum_out=accum), after,
                    cost)

    def acopy(out, in_, after=()):
        return act(out, in_, ACT.Copy, after)

    def elementwise(eng, ap):
        return 65 + 1.05 * width(ap) if eng == "vector" else 100 + 2 * width(ap)

    def dve(fn, after, n):
        return P.op("vector", fn, after, 65 + 1.05 * n)

    def tt(out, a, b, op, after=(), eng="vector"):
        return P.op(eng, lambda e: e.tensor_tensor(out, a, b, op), after, elementwise(eng, out))

    def ts(out, a, s1, op0, after=(), s2=None, op1=None, eng="vector"):
        if op1 is None:
            return P.op(eng, lambda e: e.tensor_scalar(out, a, s1, None, op0), after, elementwise(eng, out))
        return P.op(eng, lambda e: e.tensor_scalar(out, a, s1, s2, op0, op1), after, elementwise(eng, out))

    def stt(out, a, s, b, op0, op1, after=()):
        return P.op("vector", lambda e: e.scalar_tensor_tensor(out, a, s, b, op0, op1), after,
                    elementwise("vector", out))

    def copy(out, in_, after=(), eng="vector"):
        return P.op(eng, lambda e: e.tensor_copy(out, in_), after, elementwise(eng, out))

    def memset(ap, v, after=(), eng="gpsimd"):
        return P.op(eng, lambda e: e.memset(ap, v), after, elementwise(eng, ap))

    def cpred(out, mask, data, after=()):
        return P.op("vector", lambda e: e.copy_predicated(out, mask, data), after, elementwise("vector", out))

    def heads(ap):
        return ap.rearrange("p (h f) -> p h f", h=4)

    def along(col, n=128):
        return col.unsqueeze(2).broadcast_to([128, col.shape[1], n])

    def over(mat, n=4):
        return mat.unsqueeze(1).broadcast_to([mat.shape[0], n, mat.shape[1]])

    cst = sb("cst", 0, [NCONST])
    lvl = sb("lvl", 5, [2, len(LEVELS), 64], U8)
    identc = sb("identc", 8.5, [64])
    tri = sb("tri", 6.75, [2, 128], U8)
    ones = sb("ones", 7, [128])
    mod = sb("mod", 7.5, [2, 2, 48])
    amod = sb("amod", 8.25, [2, 2, 2, 8])
    mask_in = sb("mask_in", 137, [1024])
    w_ones = memset(ones[:], 1.0)
    ident = cst[:, IDENT:IDENT + 128]
    nsink, spare = sb("nsink", 4.125, [12]), sb("spare", 4.1875, [1])
    gchain, gboth = sb("gchain", 4.0625, [8]), sb("gboth", 4.09375, [8])
    ld_c, nsink_ready, identc_ready = [], [], []

    def load_constants():
        ld_c.append(P.dma("sync", cst[:], io["consts"], "cst"))

    def load_masks():
        ld_m = P.dma("sync", mask_in[:], io["masks"], "masks")
        identc_ready.append(tt(identc[:], ident[:, 0:64], ident[:, 64:128], ALU.add, ld_c))
        nsink_ready.append(ts(nsink[:], cst[:, SINK:SINK + 12], -1.0, ALU.mult, ld_c))
        ld_c.append(copy(lvl[:].rearrange("p d l f -> p (d l f)"), mask_in[:, 0:768], [ld_m]))
        ld_c.append(copy(tri[:].rearrange("p d f -> p (d f)"), mask_in[:, 768:1024], [ld_m]))

    def cv(off, n=1):
        return cst[:, off:off + n]

    NRAW, NW, LOOK = 4, 3, 2
    raw = [Cell(sb(f"raw{i}", 9 + 4 * i, [1024])) for i in range(NRAW)]
    whi = [Cell(sb(f"whi{i}", 25 + 4 * i, [1024], F32R)) for i in range(NW)]
    wlo = [Cell(sb(f"wlo{i}", 37 + 4 * i, [1024], F32R)) for i in range(NW)]
    hhi_t, hlo_t = sb("hhi", 49, [KC, T], F32R), sb("hlo", 65, [KC, T], F32R)
    hhi = [Cell(hhi_t[:, c, :]) for c in range(KC)]
    hlo_plain = sb("hlo_plain", 65, [KC, T])
    hlo = [Cell(hlo_t[:, c, :], hlo_plain[:, c, :]) for c in range(KC)]
    hl = list(zip(hhi, hlo))

    spine = []
    u_dn, u_da, u_z, u_merge, u_out, u_wq, u_peer = [], [], [], [], [], [], []

    class Unit:

        def __init__(self, slab, groups, evac, ring=None, split=True, lo="vector"):
            self.slab, self.groups, self.evac, self.ring, self.split, self.lo = slab, groups, evac, ring, split, lo
            self.guard, self.each, self.hi, self.early = None, False, "scalar", False

    state = {"loaded": 0, "split": 0, "unit": 0, "tick": 0, "drain": False}
    spine_banks = Ring(bank[0:2])
    spent, ran, parts = set(), set(), {}
    open_banks = {}

    def load_to(n, after=()):
        while state["loaded"] < min(n, len(spine)):
            i = state["loaded"]
            if i >= NRAW and i - NRAW not in spent:
                return
            c = raw[i % NRAW]
            c.ready = [P.dma("sync", c.ap[:], spine[i].slab, f"raw{i % NRAW}", [c.free, after])]
            state["loaded"] += 1

    def raw_done(i, readers):
        raw[i % NRAW].free = readers
        spent.add(i)
        load_to(i + 1 + NRAW)

    def split_next():
        i = state["split"]
        load_to(i + 1)
        if i >= state["loaded"]:
            return False
        state["split"] += 1
        if spine[i].split:
            n = len(parts)
            r, hi, lo = raw[i % NRAW], whi[n % NW], wlo[n % NW]
            parts[i] = (hi, lo)
            assert not hi.held
            hi.held = True
            a = (acopy if spine[i].hi == "scalar" else copy)(hi.ap[:], r.ap[:], [r.ready, hi.free])
            eng = spine[i].lo
            if eng == "any":
                eng = "gpsimd" if P.clock["gpsimd"] < P.clock["tensor"] + 6000 else "vector"
            b = tt(lo.ap[:], r.ap[:], hi.ap[:].bitcast(F32), ALU.subtract, [r.ready, a, lo.free], eng)
            hi.ready, lo.ready, hi.free, lo.free = [a], [b], [], []
            raw_done(i, [b])
        return True

    def split_ahead(i):
        while sum(n > i for n in parts) < LOOK and split_next():
            pass

    def run_unit(sides):
        i = state["unit"]
        state["unit"] += 1
        u = spine[i]
        while state["split"] <= i:
            assert split_next()
        if not u.split:
            last = u.evac(raw[i % NRAW])
            raw_done(i, [last])
            split_ahead(i)
            return
        hi, lo = parts[i]
        groups, j = [], 0
        for key, pairs, opens, closes in u.groups():
            groups.append((key, pairs, opens, closes, j))
            j += len(pairs)
        banks, lasts, done = [], [], 0
        for part in [[g] for g in groups] if u.each else [groups]:
            for key, pairs, opens, closes, j in part:
                if opens:
                    open_banks[key] = (u.ring or spine_banks).next()
                bk = open_banks[key]
                if sides:
                    yield [hi.ready, pairs[0][0].ready, bk.free if opens else []]
                o = bk.ap[:, 0:pairs[0][0].ap.shape[-1]]
                for n, (xh, xl) in enumerate(pairs):
                    w = hi.ap[:, 128 * j:128 * j + 128]
                    mm(o, w, xh.ap, opens and n == 0, False, [hi.ready, xh.ready, bk.free if opens else []])
                    mm(o, w, xl.ap, False, False, [xl.ready])
                    j += 1
                    done += 1
                    if done == 8:
                        split_ahead(i)
                    if done % 4 == 0:
                        yield lo.ready if done == 8 else []
            for key, pairs, opens, closes, j in part:
                bk = open_banks[key]
                o = bk.ap[:, 0:pairs[0][0].ap.shape[-1]]
                for n, (xh, xl) in enumerate(pairs):
                    last = mm(o, lo.ap[:, 128 * j:128 * j + 128], xh.ap, False, closes and n == len(pairs) - 1,
                              [lo.ready])
                    j += 1
                for xh, xl in pairs:
                    xh.free, xl.free = [last], [last]
                if closes:
                    banks.append(bk)
                    lasts.append(last)
                    del open_banks[key]
            hi.done(last)
            lo.done(last)
            if banks:
                u.evac(banks, lasts)
                banks, lasts = [], []
        yield []

    def run_early():
        i = state["unit"] + 2
        while state["split"] < i:
            assert split_next()
        while spine[i].early:
            if state["split"] <= i:
                assert split_next()
            raw_done(i, [spine[i].evac(raw[i % NRAW])])
            ran.add(i)
            i += 1

    def run_pair(sides, in_turn=True):
        run_early()
        two = [state["unit"], state["unit"] + 1]
        state["unit"] += 2
        units = [spine[i] for i in two]
        blocks = units[0].groups()[0][1]
        banks = [(u.ring or spine_banks).next() for u in units]
        outs = [b.ap[:, 0:blocks[0][0].ap.shape[-1]] for b in banks]
        split_ahead(two[0])
        def uppers(i, j):
            hi, lo = parts[two[i]]
            w = slice(128 * j, 128 * j + 128)
            mm(outs[i], hi.ap[:, w], blocks[j][0].ap, j == 0, False, [hi.ready, blocks[j][0].ready, banks[i].free])
            lo.free = blocks[j][0].free = [mm(outs[i], lo.ap[:, w], blocks[j][0].ap, False, False, [lo.ready])]
            state["tick"] += 1
            pump(sides, [])

        def lowers(i):
            hi = parts[two[i]][0]
            for j in range(KC):
                xl = blocks[j][1]
                xl.free = [mm(outs[i], hi.ap[:, 128 * j:128 * j + 128], xl.ap, False, j == KC - 1, [xl.ready])]
            hi.done(xl.free)
            units[i].evac([banks[i]], [xl.free])
            split_ahead(two[i])
            state["tick"] += 1
            pump(sides, [])
        if in_turn:
            for j in range(KC):
                uppers(0, j)
                uppers(1, j)
        for i in range(2):
            if not in_turn:
                for j in range(KC):
                    uppers(i, j)
            lowers(i)

    def whole(*lists):
        return [(n, list(x), True, True) for n, x in enumerate(lists)]

    BACKLOG = {"vector": 3000, "scalar": 3000, "gpsimd": 8000}

    def pump(sides, want):
        moved = True
        while moved:
            moved = False
            for s in list(sides):
                now = P.clock["tensor"]
                if s.want is POLL:
                    if s.polled != state["tick"]:
                        s.polled = state["tick"]
                        s.step()
                elif all(o.end <= now - 200 for o in s.want) and \
                        all(P.clock[e] <= now + lag * s.lag for e, lag in BACKLOG.items()):
                    s.step()
                    moved = True
                if not s.alive:
                    sides.remove(s)
            if not moved:
                until = max([0] + [o.end for o in flat(want)])
                ready = [(when(s), n) for n, s in enumerate(sides) if s.want is not POLL]
                if until > P.clock["tensor"] + 300 and ready and min(ready)[0] < until:
                    sides[min(ready)[1]].step()
                    moved = True

    def when(s):
        return max([P.clock[e] - lag * s.lag for e, lag in BACKLOG.items()] + [o.end for o in s.want])

    def run_spine(n, sides):
        while n:
            u = spine[state["unit"]]
            if state["unit"] in ran:
                state["unit"] += 1
                continue
            if u.guard:
                drain(sides, u.guard)
            n -= u.split
            for want in run_unit(sides):
                state["tick"] += 1
                pump(sides, want)

    def drain(sides, until=None):
        state["drain"] = True
        while sides and not (until and until()):
            state["tick"] += 1
            ready = [s for s in sides if s.want is not POLL]
            if ready:
                min(ready, key=when).step()
            for s in [s for s in sides if s.want is POLL]:
                s.step()
                assert ready or s.want is not POLL, "nothing can go on"
            sides[:] = [s for s in sides if s.alive]
        state["drain"] = False

    WK = 81
    xT0 = sb("xT0", WK + 40, [KC, T])
    xc0 = [Cell(xT0[:, c, :]) for c in range(KC)]

    class Norm:

        def __init__(self, name, kb, n, cells, ring):
            z = n / 256
            self.n, self.x, self.ring = n, cells, ring
            self.sq = Ring([Cell(sb(f"{name}sq{i}", kb + z * i, [n])) for i in range(2)])
            self.acc, self.r = sb(f"{name}acc", kb + 2 * z, [n]), sb(f"{name}r", kb + 3 * z, [n])
            self.bank, self.summed, self.used = None, [], []

        def add(self, c, ready, after=(), gain=1.0):
            s = self.sq.next()
            a = act(s.ap[:], self.x[c].ap, ACT.Square, [ready, s.free, after], scale=gain)
            if c == 0:
                prepare_ln()
            if c == KC - 1:
                self.bank = self.ring.next()
                o = self.bank.ap[:, 0:self.n]
                mm(o, ones[:], self.acc[:], True, False, [self.summed, self.bank.free])
                g = mm(o, ones[:], s.ap[:], False, True, [a])
            elif c == 0:
                g = copy(self.acc[:], s.ap[:], [a, self.summed, after], eng="gpsimd")
            else:
                g = tt(self.acc[:], self.acc[:], s.ap[:], ALU.add, [a, self.summed], eng="gpsimd")
            s.done(g)
            self.summed = [g]

        def rs(self, eps=EPS):
            l = act(self.r[:], self.bank.ap[:, 0:self.n], ACT.Ln, [self.summed, self.used], bias=eps, scale=1.0 / D)
            self.bank.done(l)
            self.bank = None
            self.ready = [act(self.r[:], self.r[:], ACT.Exp, [l], scale=-0.5)]
            return self.ready

        def apply(self, scale, pairs, shift=None, tap=None, at_once=False, needs=()):
            rs = [self.rs() if self.bank else self.ready, needs]
            made, upper, taken = [], [], []

            def lower(c, eng):
                hi, lo = pairs[c]
                f, left = lo.plain, [upper[c], taken[c]]
                if shift is not None and eng == "gpsimd":
                    left.append(act(f, f, ACT.Identity, left, bias=shift(c)))
                if shift is None or eng == "gpsimd":
                    b = tt(lo.ap, f, hi.ap.bitcast(F32), ALU.subtract, left, eng)
                else:
                    b = stt(lo.ap, f, shift(c), hi.ap.bitcast(F32), ALU.add, ALU.subtract, left)
                lo.ready = [b]
            for c in range(KC):
                yield
                hi, lo = pairs[c]
                made.append(stt(lo.plain, self.x[c].ap, scale(c), self.r[:], ALU.mult, ALU.mult,
                                [rs, ld_c, self.x[c].ready, lo.free]))
                if tap:
                    yield made[c]
                taken.append(tap(c, lo.plain, [made[c]]) if tap else [])
                if shift is None:
                    upper.append(act(hi.ap, lo.plain, ACT.Copy, [made[c], hi.free]))
                else:
                    upper.append(act(hi.ap, lo.plain, ACT.Identity, [made[c], hi.free], bias=shift(c)))
                hi.ready, hi.free, lo.free = [upper[c]], [], []
                if not at_once and c:
                    lower(c - 1, "vector")
                elif at_once and c in (2, 4, 6):
                    lower(c // 2 - 1, "gpsimd")
            for c in range(3, KC) if at_once else [KC - 1]:
                lower(c, "vector")
            self.used = [made[-1]]

    ln_ready = []

    def prepare_ln():
        ln_ready[:] = [act(spare[:], ones[:, 0:1], ACT.Ln, [w_ones, ln_ready])]

    def now(gen):
        for _ in gen:
            pass

    def first_norm():
        for c in range(0, KC, 2):
            xc0[c].ready = xc0[c + 1].ready = [P.dma("sync", xT0[:, c:c + 2], io["xT"][:, c:c + 2], f"x{c}")]
        load_to(1, xc0[2].ready)
        load_constants()
        load_to(4, xc0[6].ready)
        nrm = Norm("f", WK + 74, T, xc0, Ring(bank[2:3]))
        nrm.bank = bank[2]
        for c in range(KC):
            s = sb(f"fsquare{c}", WK + 2 * c, [T])
            a = act(s[:], xc0[c].ap, ACT.Square, [xc0[c].ready])
            if c == 0:
                prepare_ln()
            if c < 3:
                mm(bank[2].ap, ones[:], s[:], c == 0, False, [a, w_ones])
            elif c == 3:
                acc, w = s, a
            else:
                w = tt(acc[:], acc[:], s[:], ALU.add, [w, a])
        nrm.summed = [mm(bank[2].ap, ones[:], acc[:], False, True, [w])]
        spine[0].hi = "vector"
        split_next()
        now(nrm.apply(lambda c: cv(G_MIX + c), hl, at_once=True))
        split_next()

    qT, kT = sb("qT", WK, [4, T]), sb("kT", WK + 8, [4, T])
    ktok, vtok = sb("ktok", WK + 16, [4, 4, 128]), sb("vtok", WK + 24, [4, 4, 128])
    oacc = sb("oacc", WK + 32, [4, 4, 128])
    vT = sb("vT", WK + 56, [4, T])
    cbuf = Ring([Cell(sb(f"cbuf{i}", WK + 40 + 2.25 * i, [516])) for i in range(2)])
    cacc = Ring([Cell(sb(f"cacc{i}", WK + 45 + 2 * i, [T])) for i in range(2)])
    abT = sb("abT", WK + 68, [T])
    qkv = {"k": [Cell(kT[:, h, :]) for h in range(4)], "q": [Cell(qT[:, h, :]) for h in range(4)],
           "v": [Cell(vT[:, h, :]) for h in range(4)]}
    abc = Cell(abT[:])
    convpad = []

    def start_conv(after):
        for c in cbuf.cells:
            convpad.append(memset(c.ap[:, 0:2], 0.0, after))
            convpad.append(memset(c.ap[:, 514:516], 0.0, after))

    def conv_evac(kind, h):
        col = CONVW + 4 * ({"q": 0, "k": 4, "v": 8}[kind] + h)
        dst = qkv[kind][h]

        def evac(bks, done):
            cb, ca = cbuf.next(), cacc.next()
            a = act(cb.ap[:, 2:514], bks[0].ap, ACT.Copy, [done, cb.free])
            bks[0].done(a)
            o = ts(ca.ap[:], cb.ap[:, 0:T], cv(col), ALU.mult, [a, convpad, ld_c, ca.free])
            for j in range(1, 4):
                o = stt(ca.ap[:], cb.ap[:, j:j + T], cv(col + j), ca.ap[:], ALU.mult, ALU.add, [o])
            cb.done(o)
            s = act(dst.ap, ca.ap[:], ACT.Silu, [o, dst.free])
            ca.done(s)
            dst.ready, dst.free = [s], []
        return evac

    def ab_evac(bks, done):
        a = act(abT[:], bks[0].ap, ACT.Copy, [done])
        bks[0].done(a)
        abc.ready = [a]

    def h_rhs():
        return whole(zip(hhi, hlo))

    for kind in "kqv":
        for h in range(4):
            u_dn.append(Unit(io["w_in"][{"q": 0, "k": 4, "v": 8}[kind] + h], h_rhs, conv_evac(kind, h)))
    u_dn.append(Unit(io["w_in"][16], h_rhs, ab_evac))

    dnbs = [Ring(bank[2:4]), Ring(bank[4:6])]
    dnb = Ring(bank[2:6])
    small = sb("dnsmall", WK + 72, [448])

    def sm(i, n=32):
        return small[:, i:i + n]
    ab_tok, x_, ax_, g_, beta, gc, eg, nbeta, nbeg = (
        sm(0, 64), sm(64), sm(96), sm(128), sm(160), sm(192), sm(224), sm(256), sm(288))
    gl, kdf = [sm(320, 4), sm(324, 4)], [sm(328, 4), sm(332, 4)]
    nea = sm(336, 8)
    CH = WK + 40
    slot = [[sb(f"ch{d}_{i}", CH + 16 * d + 2 * i, [T]) for i in range(8)] for d in range(2)]
    o_ready = [[] for _ in range(4)]
    oda_idle = []
    S_ready = [[], []]

    def dn_prepare():
        sq2 = Ring([Cell(sb(f"sqb{i}", WK + 49 + 2 * i, [T])) for i in range(2)])
        rs2 = sb("rsb", DA + 43, [4, T])
        free = []
        for kind, scale in (("k", 1.0), ("q", 128.0 ** -0.5)):
            ls = []
            for c in qkv[kind]:
                s, b = sq2.next(), dnb.next()
                a = act(s.ap[:], c.ap, ACT.Square, [c.ready, s.free])
                yield [a, b.free]
                m = mm(b.ap, ones[:], s.ap[:], after=[a, b.free, w_ones])
                s.done(m)
                l = act(rs2[:, len(ls)], b.ap, ACT.Ln, [m, free], bias=EPS)
                b.done(l)
                ls.append(l)
            x = act(rs2[:], rs2[:], ACT.Exp, ls, scale=-0.5)
            free = []
            for h, c in enumerate(qkv[kind]):
                w = stt(c.ap, c.ap, scale, rs2[:, h], ALU.mult, ALU.mult, [x])
                c.ready = [w]
                free.append(w)
        oda_idle.extend(free)
        tok = {}
        for kind, dst in (("k", ktok), ("v", vtok)):
            tok[kind] = []
            for n in range(4):
                b = dnb.next()
                yield [b.free, [c.ready for c in qkv[kind]]]
                for h in range(4):
                    m = tr(b.ap[:, 128 * h:128 * h + 128], qkv[kind][h].ap[:, 128 * n:128 * n + 128], ident,
                           [qkv[kind][h].ready, b.free, ld_c])
                w = act(dst[:, n], heads(b.ap), ACT.Copy, [m])
                b.done(w)
                tok[kind].append(w)
        b = dnb.next()
        yield b.free
        for n in range(4):
            m = tr(b.ap[:, 16 * n:16 * n + 16], abT[0:16, 128 * n:128 * n + 128], ident[0:16, 0:16],
                   [abc.ready, b.free])
        w = copy(ab_tok, b.ap[:, 0:64], [m])
        b.done(w)
        ab = ab_tok.rearrange("p (n k d h) -> p k d n h", n=4, k=2, d=2)

        def dnh(ap):
            return ap.rearrange("p (d n h) -> p d n h", d=2, n=4)
        xs = []
        for d in range(2):
            dtb = cv(DTB + 4 * d, 4).unsqueeze(1).broadcast_to([128, 4, 4])
            xs.append(tt(dnh(x_)[:, d], ab[:, 0, d], dtb, ALU.add, [w, ld_c]))
            xs.append(copy(dnh(beta)[:, d], ab[:, 1, d], [w]))
        a1 = act(ax_, x_, ACT.Abs, xs)
        a2 = act(ax_, ax_, ACT.Exp, [a1], scale=-1.0)
        a3 = act(ax_, ax_, ACT.Ln, [a2], bias=1.0)
        s1 = stt(x_, x_, 0.0, ax_, ALU.max, ALU.add, [a3])
        a4 = act(nea, cv(ALOG, 8), ACT.Exp, [ld_c])
        gs = []
        for d in range(2):
            al = nea[:, 4 * d:4 * d + 4].unsqueeze(1).broadcast_to([128, 4, 4])
            gs.append(stt(dnh(g_)[:, d], dnh(x_)[:, d], -1.0, al, ALU.mult, ALU.mult, [s1, a4]))
        a5 = act(beta, beta, ACT.Exp, xs, scale=-1.0)
        b1 = ts(beta, beta, 1.0, ALU.add, [a5])
        b2 = P.op("vector", lambda e: e.reciprocal(beta, beta), [b1])
        b = dnb.next()
        yield [gs, b.free]
        m = mm(b.ap[:, 0:16], cv(UF, 128), g_[:, 0:16], after=[gs, b.free])
        m = mm(b.ap[:, 16:32], cv(UB, 128), g_[:, 16:32])
        w = copy(gc, b.ap[:, 0:32], [m])
        e1 = act(eg, gc, ACT.Exp, [w])
        b.done(w)
        n1 = ts(nbeta, beta, -1.0, ALU.mult, [b2])
        n2 = tt(nbeg, nbeta, eg, ALU.mult, [n1, e1])
        tok["small"] = [n2, n1, w, e1, b2, gs, tok["k"], tok["v"]]
        return tok

    def chain(d, tok):
        B0, B1, B2, B3, B4, B5, B6, S = slot[d]
        U = cv(UF if d == 0 else UB, 128)
        MASK = cv(MASKF if d == 0 else MASKB, 128)
        last = 127 if d == 0 else 0
        free = [[] for _ in range(8)]
        dnb = dnbs[d]
        half = [slice(0, 64), slice(64, 128)]
        r1, r2 = half[d], half[1 - d]
        X, Y, L = heads(B4[:, 0:256]), heads(B4[:, 256:512]), heads(B1[:, 0:256])
        zeroed = memset(B5[:], 0.0, tok["small"])
        for step in range(4):
            n = step if d == 0 else 3 - step
            col = 16 * d + 4 * n
            ncol = slice(col, col + 4)
            hs = [slice(128 * h, 128 * h + 128) for h in range(4)]
            tc = slice(128 * n, 128 * n + 128)
            small_ready = tok["small"]
            gu = tt(heads(B1[:]), over(U), along(g_[:, ncol]), ALU.mult, [small_ready, free[1]], eng="gpsimd")
            b = dnb.next()
            yield [gu, b.free]
            m = mm(b.ap, ones[:], B1[:], after=[gu, b.free])
            dd = tt(heads(B0[:]), along(gc[:, ncol]), heads(b.ap), ALU.subtract, [m, free[0]])
            if step < 3:
                kd = tt(kdf[d], heads(b.ap)[:, :, last], gc[:, ncol], ALU.subtract, [m])
                kd2 = act(kdf[d], kdf[d], ACT.Exp, [kd])
                glast = act(gl[d], heads(b.ap)[:, :, last], ACT.Exp, [free[7]])
            eB = act(B6[:], b.ap, ACT.Exp, [dd, kd, free[6]])
            b.done(eB)
            dm = tt(heads(B0[:]), heads(B0[:]), over(MASK), ALU.add, [dd])
            dec = act(B0[:], B0[:], ACT.Exp, [dm])
            qd = tt(heads(B6[:]), qT[:, :, tc], heads(B6[:]), ALU.mult, [eB], eng="gpsimd")
            bk, bq = dnb.next(), dnb.next()
            yield [bk.free, bq.free]
            for h in range(4):
                mk = mm(bk.ap[:, hs[h]], kT[:, h, tc], kT[:, h, tc], after=[bk.free])
            for h in range(4):
                mq = mm(bq.ap[:, hs[h]], qT[:, h, tc], kT[:, h, tc], after=[bq.free])
            k1 = tt(heads(B1[:]), heads(bk.ap), along(nbeta[:, ncol]), ALU.mult, [mk, m])
            nl = tt(B1[:], B1[:], B0[:], ALU.mult, [k1, dec])
            bk.done(k1)
            it = tt(B0[:], bq.ap, B0[:], ALU.mult, [mq, dec, nl])
            bq.done(it)
            vb = tt(heads(B3[:]), vtok[:, n], along(beta[:, ncol]), ALU.mult, [tok["v"], free[3]], eng="gpsimd")
            bn, bi = dnb.next(), dnb.next()
            yield [nl, it, bn.free, bi.free]
            for h in range(4):
                mn = tr(bn.ap[:, hs[h]], B1[:, hs[h]], ident, [nl, bn.free])
            for h in range(4):
                mi = tr(bi.ap[:, hs[h]], B0[:, hs[h]], ident, [it, bi.free])
            nlt = act(B2[:], bn.ap, ACT.Copy, [mn, free[2]])
            bn.done(nlt)
            itT = act(B0[:], bi.ap, ACT.Copy, [mi])
            bi.done(itT)
            xy = copy(B4[:].rearrange("p (h f) -> p h f", h=8), over(identc[:], 8), [free[4], identc_ready], eng="gpsimd")
            xr = [cpred(X[r], over(lvl[r, d, 0]), heads(B1[:])[r, :, r], [xy, nl, ld_c]) for r in half]
            yr = [cpred(Y[r], over(lvl[r, 1 - d, 0]), heads(B2[:])[r, :, r], [xy, nlt]) for r in half]
            for i in range(1, len(LEVELS)):
                bt = dnb.next()
                yield [xr, nlt, bt.free]
                for h in range(4):
                    for r in half:
                        mt = mm(heads(bt.ap[:, 0:256])[r, h], heads(B2[:])[r, h, r], X[r, h], after=[xr, nlt, bt.free])
                ev = act(L[:], heads(bt.ap[:, 0:256]), ACT.Copy, [mt, xr])
                bt.done(ev)
                bx = dnb.next()
                yield [ev, yr, bx.free]
                for h in range(4):
                    for r in half:
                        mx = mm(heads(bx.ap[:, 0:256])[r, h], Y[r, h], L[r, h], after=[ev, yr, bx.free])
                xr = cpred(X, over(lvl[:, d, i]), heads(bx.ap[:, 0:256]), [mx])
                bx.done(xr)
                by = dnb.next()
                for h in range(4):
                    for r in half:
                        my = mm(heads(by.ap[:, 0:256])[r, h], L[r, h], Y[r, h], after=[ev, yr, by.free])
                yr = cpred(Y, over(lvl[:, 1 - d, i]), heads(by.ap[:, 0:256]), [my])
                by.done(yr)
            bt = dnb.next()
            yield [xr, nlt, bt.free]
            for h in range(4):
                mt = mm(heads(bt.ap[:, 0:256])[r2, h], heads(B2[:])[r1, h, r2], X[r1, h], after=[xr, nlt, bt.free])
            ev = act(L[r2], heads(bt.ap[:, 0:256])[r2], ACT.Copy, [mt, xr])
            bt.done(ev)
            dg = [copy(heads(B5[:])[r, :, r], Y[r], [yr, zeroed, free[5]]) for r in half]
            by = dnb.next()
            yield [ev, yr, by.free]
            for h in range(4):
                my = mm(heads(by.ap[:, 0:256])[r1, h], L[r2, h], Y[r2, h], after=[ev, yr, by.free])
            yr = dg + [copy(heads(B5[:])[r1, :, r2], heads(by.ap[:, 0:256])[r1], [my, dg])]
            by.done(yr)
            kb = tt(heads(B1[:]), ktok[:, n], along(nbeg[:, ncol]), ALU.mult, [tok["k"], my], eng="gpsimd")
            if step < 3:
                kdc = tt(heads(B2[:]), ktok[:, n], along(kdf[d]), ALU.mult, [kd2, mt], eng="gpsimd")
            first = step == 0
            if not first:
                bw = dnb.next()
                yield [kb, yr, bw.free]
                for h in range(4):
                    mw = mm(bw.ap[:, hs[h]], B1[:, hs[h]], B5[:, hs[h]], after=[kb, yr, bw.free])
                wT = act(B4[:], bw.ap, ACT.Copy, [mw, mt])
                bw.done(wT)
            bv = dnb.next()
            yield [vb, yr, bv.free, [] if first else [wT, S_ready[d]]]
            for h in range(4):
                mv = mm(bv.ap[:, hs[h]], B5[:, hs[h]], B3[:, hs[h]], True, first, [vb, yr, bv.free])
                if not first:
                    mv = mm(bv.ap[:, hs[h]], B4[:, hs[h]], S[:, hs[h]], False, True, [wT, S_ready[d]])
            vn = act(B3[:], bv.ap, ACT.Copy, [mv])
            bv.done(vn)
            bo = dnb.next()
            yield [itT, vn, bo.free, [] if first else [qd, S_ready[d]]]
            for h in range(4):
                if not first:
                    mm(bo.ap[:, hs[h]], B6[:, hs[h]], S[:, hs[h]], True, False, [qd, bo.free, S_ready[d]])
                mo = mm(bo.ap[:, hs[h]], B0[:, hs[h]], B3[:, hs[h]], first, True, [itT, vn, bo.free])
            if step < 3:
                bs = dnb.next()
                for h in range(4):
                    ms = mm(bs.ap[:, hs[h]], B2[:, hs[h]], B3[:, hs[h]], after=[kdc, bs.free])
            if not o_ready[n]:
                ow = copy(oacc[:, n], heads(bo.ap), [mo])
            else:
                ow = tt(oacc[:, n], oacc[:, n], heads(bo.ap), ALU.add, [mo, o_ready[n]])
            o_ready[n] = [ow]
            bo.done(ow)
            end = mo
            if step < 3:
                if first:
                    sw = copy(S[:], bs.ap, [ms])
                else:
                    s1 = tt(heads(S[:]), heads(S[:]), along(gl[d]), ALU.mult, [glast, mo])
                    sw = tt(S[:], S[:], bs.ap, ALU.add, [s1, ms])
                bs.done(sw)
                S_ready[d] = [sw]
                end = ms
            free = [[end]] * 7 + [S_ready[d]]

    def delta(sides):
        tok = yield from dn_prepare()
        sides += [Side(chain(0, tok)), Side(chain(1, tok))]

    DA = WK + 74
    dq = [sb(f"dq{i}", DA + 12 * i, [3, T]) for i in range(2)]
    dk = [sb(f"dk{i}", DA + 6 + 12 * i, [3, T]) for i in range(2)]
    dqc = [[Cell(dq[i][:, g, :]) for g in range(3)] for i in range(2)]
    dkc = [[Cell(dk[i][:, g, :]) for g in range(3)] for i in range(2)]
    dv = sb("dv", DA + 24, [3, 4, 128])
    dvT = Ring([Cell(sb(f"dvT{i}", DA + 30 + 2 * i, [T])) for i in range(2)])
    dS = sb("dS", DA + 34, [768])
    dPT = sb("dPT", DA + 37, [6, 128])
    dB = Cell(sb("dB", DA + 40, [768]))
    oda = sb("oda", DA + 43, [4, T])
    dO = sb("dO", DA + 51, [128])
    dst_ = sb("dstat", DA + 51.5, [16])
    v_pending = {}
    dab = [bank[6], bank[7]]
    da_done = []

    def by_residue(ap):
        return ap.rearrange("p (l r) -> p r l", r=4)

    def da_evac(kind, h, g):
        def evac(bks, done):
            ps = by_residue(bks[0].ap)
            if kind == "v":
                c = dvT.next()
                a = act(c.ap[:].rearrange("p (r l) -> p r l", r=4), ps, ACT.Copy, [done, c.free])
                v_pending[h, g] = (c, a)
            else:
                c = (dqc if kind == "q" else dkc)[h % 2][g]
                o = c.ap.rearrange("p (r l) -> p r l", r=4)
                if kind == "q":
                    a = act(o, ps, ACT.Copy, [done, c.free], scale=128.0 ** -0.5)
                else:
                    a = copy(o, ps, [done, c.free])
                c.ready, c.free = [a], []
            bks[0].done(a)
        return evac

    for h in range(4):
        for kind, base in (("q", 17), ("k", 29), ("v", 41)):
            for g in range(3):
                u_da.append(Unit(io["w_in"][base + 4 * g + h], h_rhs, da_evac(kind, h, g)))

    def dilated():
        A, B = dab
        s_free, pv, out_done = list(msb_free), [], []
        for h in range(4):
            vt = []
            for g in range(3):
                while (h, g) not in v_pending:
                    yield POLL
                c, a = v_pending[h, g]
                b = (A, B)[g % 2]
                yield [a, b.free]
                for r in range(4):
                    m = tr(b.ap[:, 128 * r:128 * r + 128], c.ap[:, 128 * r:128 * r + 128], ident, [a, b.free])
                w = act(dv[:, g], heads(b.ap), ACT.Copy, [m, pv])
                c.done(m)
                b.free = [w]
                vt.append(w)
            q, k = dq[h % 2], dk[h % 2]
            qk_ready = [c.ready for c in dqc[h % 2] + dkc[h % 2]]
            for r in range(4):
                ld = P.dma("gpsimd", dB.ap[:], io["da_bias"][h, r], "dabias", dB.free)
                yield [qk_ready, A.free, B.free]
                t = slice(128 * r, 128 * r + 128)
                mm(A.ap, q[:, 0, t], k[:, 0, :], after=[qk_ready, A.free])
                mm(B.ap[:, 0:128], q[:, 1, t], k[:, 1, t], after=[B.free])
                m = mm(B.ap[:, 128:256], q[:, 2, t], k[:, 2, t])
                s2 = psum[:, 6:8, :].rearrange("p a b -> p (a b)")[:, 0:768]
                mx = P.op("vector", lambda e, s2=s2: e.tensor_tensor_reduce(
                    dS[:], s2, dB.ap[:], 1.0, -3e38, ALU.add, ALU.max, dst_[:, 0:1]), [m, ld, s_free])
                A.free, B.free, dB.free = [mx], [mx], [mx]
                nm = ts(dst_[:, 1:2], dst_[:, 0:1], -1.0, ALU.mult, [mx])
                ex = act(dS[:], dS[:], ACT.Exp, [nm], bias=dst_[:, 1:2], accum=dst_[:, 2:3])
                rc = P.op("vector", lambda e: e.reciprocal(dst_[:, 3:4], dst_[:, 2:3]), [ex])
                yield [ex]
                for i in range(6):
                    b = A if i < 4 else B
                    m = tr(b.ap[:, 128 * (i % 4):128 * (i % 4) + 128], dS[:, 128 * i:128 * i + 128], ident,
                           [ex, b.free])
                    if i == 3:
                        p1 = act(dPT[:, 0:4], heads(A.ap), ACT.Copy, [m, pv])
                s_free = [m]
                p2 = copy(dPT[:, 4:6], B.ap[:, 0:256].rearrange("p (a b) -> p a b", a=2), [m, pv])
                A.free, B.free = [p1], [p2]
                yield [p1, p2, vt]
                for i in range(6):
                    g, rr = (0, i) if i < 4 else (i - 3, r)
                    m = mm(A.ap[:, 0:128], dPT[:, i], dv[:, g, rr], i == 0, i == 5, [p1, p2, vt, A.free])
                pv = [m]
                o1 = act(dO[:], A.ap[:, 0:128], ACT.Copy, [m, rc, out_done], scale=dst_[:, 3:4])
                A.free = [o1]
                yield [o1, B.free]
                m = tr(B.ap[:, 0:128], dO[:], ident, [o1, B.free])
                w = copy(oda[:, h].rearrange("p (l r) -> p r l", r=4)[:, r], B.ap[:, 0:128], [m, oda_idle])
                out_done = [m]
                B.free = [w]
                da_done.append(w)
            for c in dqc[h % 2] + dkc[h % 2]:
                c.free = pv

    zs = sb("zs", DA, [4, T])
    zsc = [Cell(zs[:, h, :]) for h in range(4)]

    def z_evac(h):
        def evac(bks, done):
            w = act(zsc[h].ap, bks[0].ap, ACT.Silu, [done, [c.free for c in dqc[0] + dkc[0]]])
            bks[0].done(w)
            zsc[h].ready = [w]
        return evac

    for h in range(4):
        u_z.append(Unit(io["w_in"][12 + h], h_rhs, z_evac(h)))

    odn_hi, odn_lo = sb("odn_hi", WK + 16, [4, T], F32R), sb("odn_lo", WK + 24, [4, T], F32R)
    oda_hi, oda_lo = sb("oda_hi", WK + 40, [4, T], F32R), sb("oda_lo", WK + 48, [4, T], F32R)
    odn_c = [(Cell(odn_hi[:, h]), Cell(odn_lo[:, h])) for h in range(4)]
    oda_c = [(Cell(oda_hi[:, h]), Cell(oda_lo[:, h])) for h in range(4)]
    osq = Ring([Cell(sb(f"osq{i}", WK + 64 - 4 * i, [T])) for i in range(2)])
    of = Ring([Cell(sb(f"of{i}", WK + 66 - 4 * i, [T])) for i in range(2)])
    orr = sb("orr", WK + 68, [16])

    def finish_mixers(chain_end):
        sums = []
        for n in range(4):
            q = osq.next()
            a = tt(heads(q.ap[:]), oacc[:, n], oacc[:, n], ALU.mult, [o_ready[n], chain_end, q.free])
            q.done(dve(lambda e, n=n, q=q: e.tensor_reduce(orr[:, 4 * n:4 * n + 4], heads(q.ap[:]), AX.X, ALU.add), [a], T))
            sums += q.free
        yield
        c = act(orr[:], orr[:], ACT.Ln, sums, bias=EPS, scale=1.0 / 128)
        d_ = act(orr[:], orr[:], ACT.Exp, [c], scale=-0.5)
        for n in range(4):
            q, f, bk = osq.next(), of.next(), dnb.next()
            e_ = tt(heads(q.ap[:]), oacc[:, n], along(orr[:, 4 * n:4 * n + 4]), ALU.mult, [d_, q.free])
            yield [e_, bk.free]
            for h in range(4):
                m = tr(bk.ap[:, 128 * h:128 * h + 128], q.ap[:, 128 * h:128 * h + 128], ident, [e_, bk.free])
            q.done(m)
            w = stt(heads(f.ap[:]), heads(bk.ap), cv(ONORM), zs[:, :, 128 * n:128 * n + 128], ALU.mult, ALU.mult,
                    [m, f.free, [z.ready for z in zsc]])
            bk.done(w)
            hi = act(odn_hi[:, :, 128 * n:128 * n + 128], heads(f.ap[:]), ACT.Copy, [w])
            lo = tt(odn_lo[:, :, 128 * n:128 * n + 128], heads(f.ap[:]),
                    odn_hi[:, :, 128 * n:128 * n + 128].bitcast(F32), ALU.subtract, [hi])
            f.done(lo)
            for h in range(4):
                odn_c[h][0].ready.append(hi)
                odn_c[h][1].ready.append(lo)
            yield
            hi = act(oda_hi[:, n], oda[:, n], ACT.Copy, [da_done, chain_end])
            lo = tt(oda_lo[:, n], oda[:, n], oda_hi[:, n].bitcast(F32), ALU.subtract, [hi])
            oda_c[n][0].ready, oda_c[n][1].ready = [hi], [lo]

    gates = Ring([Cell(sb(f"gate{i}", WK + 82 + 2 * i, [T])) for i in range(6)])
    gate_of = {}
    mg_hi, mg_lo = sb("mg_hi", WK + 56, [KC, T], F32R), None
    mg_lo = sb("mg_lo", WK + 98, [KC, T], F32R)
    mgc = [(Cell(mg_hi[:, c]), Cell(mg_lo[:, c])) for c in range(KC)]

    def gate_evac(which, o):
        def evac(bks, done):
            c = gates.next()
            a = act(c.ap[:], bks[0].ap, ACT.Sigmoid, [done, c.free, da_done, [x.free for x in dqc[0] + dkc[0]]])
            bks[0].done(a)
            gate_of[which, o] = (c, a)
        return evac

    xres = sb("xres", WK, [KC, T])
    xr = [Cell(xres[:, c, :]) for c in range(KC)]

    def merge_evac(o):
        def evac(bks, done):
            (c1, r1), (c2, r2) = gate_of["dn", o], gate_of["da", o]
            a = tt(c1.ap[:], bks[0].ap, c1.ap[:], ALU.mult, [done, r1])
            b = tt(c2.ap[:], bks[1].ap, c2.ap[:], ALU.mult, [done, r2])
            bks[0].done(a)
            bks[1].done(b)
            s = tt(c1.ap[:], c1.ap[:], c2.ap[:], ALU.add, [a, b])
            hi = act(mgc[o][0].ap, c1.ap[:], ACT.Copy, [s])
            lo = tt(mgc[o][1].ap, c1.ap[:], mgc[o][0].ap.bitcast(F32), ALU.subtract, [hi])
            c1.done(lo)
            c2.done(s)
            mgc[o][0].ready, mgc[o][1].ready = [hi], [lo]
        return evac

    late_banks = Ring(bank[2:6])
    GL = 3
    for o in range(KC + GL):
        if o >= GL:
            u_merge.append(Unit(io["w_br"][o - GL], lambda: whole(odn_c, oda_c), merge_evac(o - GL), late_banks))
        if o < KC:
            u_merge.append(Unit(io["w_in"][53 + o], h_rhs, gate_evac("dn", o)))
            u_merge.append(Unit(io["w_in"][61 + o], h_rhs, gate_evac("da", o)))

    norm = Norm("n", WK + 116, T, xr, late_banks)

    def wout_evac(o):
        def evac(bks, done):
            w = tt(xr[o].ap, xr[o].ap, bks[0].ap, ALU.add, [done, xr[o].ready])
            bks[0].done(w)
            xr[o].ready = [w]
            norm.add(o, [w], da_done)
        return evac

    for o in range(KC):
        u_out.append(Unit(io["w_out"][o], lambda: whole(mgc), wout_evac(o), late_banks))

    pq = Ring([Cell(sb(f"pq{i}", kb, [T])) for i, kb in enumerate((136, 138, 205))])
    keys = Ring([Cell(sb(f"keys{i}", kb, [128])) for i, kb in enumerate((125, 125.5, 207))])
    rest = sb("rest", 195, [4, 128])
    sv, siu = sb("sv", 126, [4, 16, 16]), sb("siu", 130, [4, 16, 16], U32)
    cand, eqv, eqg = sb("cand", 49, [2048]), sb("eqv", 57, [2048]), sb("eqg", 65, [2048])
    sif = sb("sif", 73, [16, 16])
    cvl, ciu = sb("cvl", 74, [8, 16]), sb("ciu", 74.5, [8, 16], U32)
    su = sb("su", 75, [3, 128], U32)
    af, bf, tf = [sb(f"rank{i}", 76.5 + i / 2, [128]) for i in range(3)]
    i1f, i2f, gtf = [sb(f"chosen{i}", 78 + i / 2, [128]) for i in range(3)]
    ksm = sb("ksm", 79.5, [32])
    i1T, i2T, gT = sb("i1T", 197, [TD]), sb("i2T", 198.5, [TD]), sb("gT", 200, [TD])
    rows, rgate, ract = sb("rows", 201.5, [128], I32), sb("rgate", 202, [128]), sb("ract", 202.5, [128])
    NEGF = -3.0e38
    wq_idle = []
    pq_of = {}

    def wq_evac(i):
        def evac(bks, done):
            c = pq.next()
            a = act(c.ap[:], bks[0].ap, ACT.Copy, [done, c.free, wq_idle])
            bks[0].done(a)
            pq_of[i] = (c, a)
        return evac

    for i in range(16):
        u_wq.append(Unit(io["peer_wq"][i], h_rhs, wq_evac(i), spine_banks, lo="any"))
        u_wq[i].guard = lambda: not all(c.held for c in pq.cells)

    keyb = Ring(bank[6:8])
    tile_keys, rows_ready = [], []

    def vmax(out, in_, after):
        return dve(lambda e: e.max(out, in_), after, width(in_))

    def vindex(out, vals, in_, after):
        return dve(lambda e: e.max_index(out, vals, in_), after, width(in_))

    def vreplace(out, vals, in_, after):
        return dve(lambda e: e.match_replace(out, vals, in_, NEGF), after, width(in_))

    def top_keys():
        loaded = []

        def load(i):
            if i < 16:
                c = keys.next()
                c.ready = [P.dma("gpsimd", c.ap[:], io["peer_keys"][:, i, :], f"keys{i % 3}", [c.free, wq_idle])]
                loaded.append(c)
        for i in range(3):
            load(i)
        x2, r1 = [], []
        for i in range(16):
            while i not in pq_of:
                yield POLL
            c, a = pq_of[i]
            k, b = loaded[i], keyb.next()
            yield [a, k.ready, b.free]
            src = [b.ap[:, 128 * n:128 * n + 128] for n in range(4)]
            for n in range(4):
                m = mm(src[n], c.ap[:, 128 * n:128 * n + 128], k.ap[:], after=[a, k.ready, b.free])
            c.done(m)
            k.done(m)
            load(i + 3)
            m1 = [vmax(sv[:, n, i, 0:8], src[n], [m, wq_idle]) for n in range(4)]
            yield
            r1 = [vreplace(rest[:, n, :], sv[:, n, i, 0:8], src[n], [m1[n], x2]) for n in range(4)]
            x1 = [vindex(siu[:, n, i, 0:8], sv[:, n, i, 0:8], src[n], [m1[n]]) for n in range(4)]
            b.done(x1)
            yield
            m2 = [vmax(sv[:, n, i, 8:16], rest[:, n, :], [r1[n]]) for n in range(4)]
            x2 = [vindex(siu[:, n, i, 8:16], sv[:, n, i, 8:16], rest[:, n, :], [m2[n]]) for n in range(4)]
            yield
        return [m2, x2]

    NC = 72

    def top_pairs(sel):
        free = {"sel": [], "cand": flat([[c.free for c in hhi + hlo], norm.summed]), "i": []}
        for n in range(4):
            t = slice(128 * n, 128 * n + 128)
            s4 = sv[:, n].rearrange("p (h c) k -> p h c k", c=2)
            s5 = sif[:].rearrange("p (h c) k -> p h c k", c=2)
            c4 = cand[:, 0:8 * NC].rearrange("p (h j) -> p h j", h=8)
            w = []
            for at, a0, a1, nb in ((0, 0, 2, 16), (32, 2, 4, 8), (48, 4, 8, 4), (64, 8, 16, 1)):
                na = a1 - a0
                w.append(tt(c4[:, :, at:at + na * nb].rearrange("p h (a b) -> p h a b", a=na),
                            s4[:, :, 0, a0:a1].unsqueeze(3).broadcast_to([128, 8, na, nb]),
                            s4[:, :, 1, 0:nb].unsqueeze(2).broadcast_to([128, 8, na, nb]), ALU.add, [sel, free["cand"]]))
            fi = copy(sif[:], siu[:, n], [sel, free["sel"], w])
            yield
            ch = [c4[:, h] for h in range(8)]
            rh = [eqv[:, NC * h:NC * h + NC] for h in range(8)]
            m1 = [vmax(cvl[:, h, 0:8], ch[h], [w, free["i"]]) for h in range(8)]
            r1, x1 = [], []
            for h in range(8):
                if h % 4 == 0:
                    yield
                r1.append(vreplace(rh[h], cvl[:, h, 0:8], ch[h], [m1[h], free["cand"]]))
                x1.append(vindex(ciu[:, h, 0:8], cvl[:, h, 0:8], ch[h], [m1[h]]))
            yield
            m2 = [vmax(cvl[:, h, 8:16], rh[h], [r1[h]]) for h in range(8)]
            yield
            x2 = [vindex(ciu[:, h, 8:16], cvl[:, h, 8:16], rh[h], [m2[h]]) for h in range(8)]
            yield
            cf = ciu[:].rearrange("p h k -> p (h k)")
            s1 = [ts(su[:, j], cf, 4 - j, ALU.logical_shift_right, [x1, x2]) for j in range(3)]
            a = stt(af[:], su[:, 1], -2.0, su[:, 0], ALU.add, ALU.max, s1)
            a = stt(af[:], su[:, 2], -8.0, af[:], ALU.add, ALU.max, [a])
            a = stt(af[:], cf, -56.0, af[:], ALU.add, ALU.max, [a])
            b1 = ts(bf[:], af[:], 8.0, ALU.mult, [a], 16.0, ALU.add)
            b2 = ts(tf[:], af[:], 4.0, ALU.mult, [a], 32.0, ALU.add)
            b1 = stt(bf[:], af[:], 16.0, bf[:], ALU.mult, ALU.min, [b1])
            b2 = stt(tf[:], af[:], 56.0, tf[:], ALU.add, ALU.min, [b2])
            b1 = tt(bf[:], bf[:], tf[:], ALU.min, [b1, b2])
            b = tt(bf[:], cf, bf[:], ALU.subtract, [b1])
            i16 = cst[:, IOTA:IOTA + 16].unsqueeze(1).broadcast_to([128, 128, 16])
            e3, g3 = eqv[:].rearrange("p (q j) -> p q j", j=16), eqg[:].rearrange("p (q j) -> p q j", j=16)

            def table(c):
                return s5[:, :, c, :].unsqueeze(2).broadcast_to([128, 8, 16, 16])

            def look_up(eq, c, ready):
                e4 = eq[:].rearrange("p (h k j) -> p h k j", h=8, j=16)
                return tt(e4, e4, table(c), ALU.mult, [ready, fi], eng="gpsimd")
            yield
            v1 = tt(e3, along(af[:], 16), i16, ALU.is_equal, [a, x2, m2, ld_c])
            v2 = look_up(eqv, 0, v1)
            yield
            p1 = tt(g3, along(bf[:], 16), i16, ALU.is_equal, [b, free["cand"]])
            p2 = look_up(eqg, 1, p1)
            d0 = tt(gtf[:].rearrange("p (h k) -> p h k", h=8), cvl[:], cvl[:, :, 0:1].broadcast_to([128, 8, 16]),
                    ALU.subtract, [m1, m2, free["i"]])
            d1 = act(gtf[:], gtf[:], ACT.Exp, [d0])
            yield [d1]
            d2 = dve(lambda e: e.tensor_reduce(ksm[:, 0:8], gtf[:].rearrange("p (h k) -> p h k", h=8),
                                               AX.X, ALU.add), [d1], 128)
            d3 = dve(lambda e: e.reciprocal(ksm[:, 8:16], ksm[:, 0:8]), [d2], 8)
            d4 = tt(gtf[:].rearrange("p (h k) -> p h k", h=8), gtf[:].rearrange("p (h k) -> p h k", h=8),
                    ksm[:, 8:16].unsqueeze(2).broadcast_to([128, 8, 16]), ALU.mult, [d3])
            yield [v2]
            v3 = dve(lambda e: e.tensor_reduce(i1f[:], e3, AX.X, ALU.add), [v2, free["i"]], 2048)
            yield [p2]
            p3 = dve(lambda e: e.tensor_reduce(i2f[:], g3, AX.X, ALU.add), [p2, free["i"]], 2048)
            if n == TD // 128:
                r1 = stt(rows[:], i1f[:], 128.0, i2f[:], ALU.mult, ALU.add, [v3, p3])
                rows_ready.extend([r1, copy(rgate[:], gtf[:], [d4])])
                free["cand"] = [x1, p3, v3]
                continue
            bk = keyb.next()
            yield [v3, p3, d4, bk.free]
            q = [tr(bk.ap[:, 0:128], i1f[:], ident, [v3, bk.free]), tr(bk.ap[:, 128:256], i2f[:], ident, [p3]),
                 tr(bk.ap[:, 256:384], gtf[:], ident, [d4])]
            k = [copy(i1T[:, t], bk.ap[:, 0:128], q), copy(i2T[:, t], bk.ap[:, 128:256], q),
                 copy(gT[:, t], bk.ap[:, 256:384], q)]
            bk.done(k)
            tile_keys.append(k)
            free = {"sel": [v2, p2], "cand": [x1, p3, v3], "i": [q, d0]}
        for c in hhi + hlo:
            c.free = flat(list(free.values()))

    NG = TD // 16
    gate_dram = nc.dram_tensor("gate_dram", [NG, 128, 128, 16], F32, kind="Internal").ap()
    GT = 4
    ea = Ring([Cell(sb(f"ea{i}", kb, [GT, 128])) for i, kb in enumerate((185, 187, 189, 136))])
    eb = Ring([Cell(sb(f"eb{i}", kb, [GT, 128])) for i, kb in enumerate((191, 193, 195, 138))])
    stage = Ring([Cell(sb(f"stage{i}", 152 + 8 * i, [128, 16])) for i in range(2)])
    g_written, g_idle = [], []

    def dense_gates():
        io_b = cst[:, IOTA:IOTA + 128].unsqueeze(1).broadcast_to([128, GT, 128])

        def one_hots(n):
            t = slice(GT * n, GT * n + GT)
            k = tile_keys[GT * n // 128]
            A, B = ea.next(), eb.next()
            idle = [g_idle, [c.free for c in pq.cells]]
            a1 = tt(A.ap[:], io_b, along(i1T[:, t]), ALU.is_equal, [k, A.free, idle])
            a2 = tt(A.ap[:], A.ap[:], along(gT[:, t]), ALU.mult, [a1], eng="gpsimd")
            b1 = tt(B.ap[:], io_b, along(i2T[:, t]), ALU.is_equal, [k, B.free, idle])
            return A, B, [a2, b1]
        while not g_idle or not tile_keys:
            yield POLL
        ahead, made = [], 0
        for n in range(TD // GT):
            while made < TD // GT and len(ahead) < 3:
                if len(tile_keys) <= GT * made // 128:
                    if ahead:
                        break
                    yield POLL
                    continue
                yield
                ahead.append(one_hots(made))
                made += 1
            A, B, ab = ahead.pop(0)
            if n % 4 == 0:
                S, ws = stage.next(), []
            b = keyb.next()
            yield [ab, b.free]
            for v in range(GT):
                m = mm(b.ap[:, 128 * v:128 * v + 128], A.ap[:, v, :], B.ap[:, v, :], after=[ab, b.free])
            c = GT * (n % 4)
            w = act(S.ap[:, :, c:c + 4], b.ap.rearrange("p (v j) -> p j v", v=4), ACT.Copy, [m, S.free, g_idle])
            b.done(w)
            ws.append(w)
            A.done(m)
            B.done(m)
            if n % 4 == 3:
                g = n // 4
                d = P.dma("sync", gate_dram[g].rearrange("p j t -> p (j t)"), S.ap[:].rearrange("p j t -> p (j t)"),
                          f"stage{g % 2}", ws)
                S.done(d)
                g_written.append(d)
        while not gin[0].free:
            yield POLL
        load_gates(0)

    GJ = 8
    gin = [Cell(sb(f"gin{i}", kb, [NG, GJ, 16])) for i, kb in enumerate((145, 157))]
    ag_hi = [sb(f"ag_hi{i}", kb, [GJ, TD], F32R) for i, kb in enumerate((97, 169))]
    ag_lo = [sb(f"ag_lo{i}", kb, [GJ, TD], F32R) for i, kb in enumerate((109, 181))]
    agc = [[(Cell(ag_hi[i][:, j]), Cell(ag_lo[i][:, j])) for j in range(GJ)] for i in range(2)]
    uact = Ring([Cell(sb(f"uact{i}", 193 + 1.5 * i, [TD])) for i in range(2)])
    hd = [(Cell(hhi[c].ap[:, 0:TD]), Cell(hlo[c].ap[:, 0:TD])) for c in range(KC)]

    def load_gates(g):
        c = gin[g % 2]
        c.ready = [P.dma("sync", c.ap[:].rearrange("p n j t -> p n (j t)"),
                         gate_dram[:, :, GJ * g:GJ * g + GJ, :].rearrange("n p j t -> p n (j t)"),
                         f"gin{g % 2}", [g_written, c.free])]
        c.free = []

    def u_evac(j):
        g, jj = divmod(j, GJ)

        def evac(bks, done):
            c, gc_ = uact.next(), gin[g % 2]
            hi, lo = agc[g % 2][jj]
            a = act(c.ap[:], bks[0].ap[:, 0:TD], ACT.Gelu_apprx_tanh, [done, c.free])
            bks[0].done(a)
            t3 = c.ap[:].rearrange("p (n t) -> p n t", t=16)
            w = tt(t3, t3, gc_.ap[:, :, jj, :], ALU.mult, [a, gc_.ready])
            gc_.free = gc_.free + [w]
            h = act(hi.ap, c.ap[:], ACT.Copy, [w, hi.free])
            l = tt(lo.ap, c.ap[:], hi.ap.bitcast(F32), ALU.subtract, [h, lo.free])
            c.done(l)
            hi.ready, lo.ready = [h], [l]
        return evac

    def v_evac(g, dt):
        def evac(bks, done):
            w = tt(xr[dt].ap[:, 0:TD], xr[dt].ap[:, 0:TD], bks[0].ap[:, 0:TD], ALU.add, [done, xr[dt].ready])
            bks[0].done(w)
            xr[dt].ready = [w]
            if g == 128 // GJ - 1:
                xr[dt].ready = [w] + row_sums
                chain_norm.add(dt, xr[dt].ready, gain=gchain[:, dt:dt + 1])
                norm.add(dt, xr[dt].ready)
        return evac

    NGR = 128 // GJ
    u_units = [[Unit(io["peer_u"][GJ * g + j], lambda: whole(hd), u_evac(GJ * g + j), spine_banks, lo="any") for j in range(GJ)]
               for g in range(NGR)]
    v_units = [[Unit(io["peer_v"][8 * g + d], lambda g=g: whole(agc[g % 2]), v_evac(g, d), late_banks, lo="any") for d in range(8)]
               for g in range(NGR)]
    u_peer += u_units[0]
    for g in range(NGR):
        for j in range(8):
            if g + 1 < NGR:
                u_peer.append(u_units[g + 1][j])
            u_peer.append(v_units[g][j])

    xtok = sb("xtok", 126, [D])
    fetched = [Cell(sb(f"fetched{i}", kb, [D])) for i, kb in enumerate((130, 134, 138, 121, 196))]
    row_sums, x_tok = [], []
    chain_norm = Norm("ch", 126, T, xr, late_banks)

    def to_tokens(c, h, ready):
        b = keyb.next()
        t = tr(b.ap[:, 0:128], h[:, TD:T], ident, [ready, b.free])
        w = copy(xtok[:, 128 * c:128 * c + 128], b.ap[:, 0:128], [t, rows_ready])
        b.done(w)
        x_tok.append(w)
        return t

    def chosen_experts(idle):
        R = len(fetched)

        def fetch(i):
            if i < 256:
                c = fetched[i % R]
                c.ready = [P.gather(c.ap[:], io["peer_v_rows" if i >= 128 else "peer_u_rows"],
                                    rows[:, i % 128:i % 128 + 1], f"fetched{i % R}", [c.free, rows_ready, idle])]
        for i in range(R - 1):
            fetch(i)
        ws = []
        for i in range(128):
            c = fetched[i % R]
            yield [c.ready, x_tok]
            w = dve(lambda e, c=c, i=i: e.tensor_tensor_reduce(c.ap[:], c.ap[:], xtok[:], 1.0, 0.0, ALU.mult, ALU.add,
                                                              ract[:, i:i + 1]), [c.ready, x_tok, idle], D + 120)
            c.free = [w]
            ws.append(w)
            fetch(i + R - 1)
        yield [ws]
        a = act(ract[:], ract[:], ACT.Gelu_apprx_tanh, [ws])
        b = tt(ract[:], ract[:], rgate[:], ALU.mult, [a, rows_ready])
        for i in range(128):
            c = fetched[(i + 128) % R]
            yield [c.ready, b]
            if i == 0:
                w = ts(xtok[:], c.ap[:], ract[:, 0:1], ALU.mult, [c.ready, b, ws])
            else:
                w = stt(xtok[:], c.ap[:], ract[:, i:i + 1], xtok[:], ALU.mult, ALU.add, [c.ready, w])
            c.free = [w]
            fetch(i + 128 + R - 1)
        for x in range(2):
            b = keyb.next()
            yield [w, b.free]
            for c in range(4):
                t = tr(b.ap[:, 128 * c:128 * c + 128], xtok[:, 512 * x + 128 * c:512 * x + 128 * c + 128], ident,
                       [w, b.free])
            us = [tt(xr[4 * x + c].ap[:, TD:T], xr[4 * x + c].ap[:, TD:T], b.ap[:, 128 * c:128 * c + 128], ALU.add,
                     [t, xr[4 * x + c].ready]) for c in range(4)]
            b.done(us)
            row_sums.extend(us)

    M0 = 97
    svec = sb("svec", 4.25, [46])
    mod_ready = [[], []]
    svec_ready, mod_pending = [], []
    msb = [sb(f"msb{i}", kb, [512]) for i, kb in enumerate((DA + 34, DA + 36, WK + 94, 134, 158, 199))]

    def start_mod():
        a = memset(svec[:], 0.0)
        sv_ = svec[:, 0:16].rearrange("p (k v) -> p v k", v=2)
        svec_ready.append(act(sv_, cv(CVEC, 16).rearrange("p (v k) -> p v k", v=2), ACT.Silu, [a, ld_c]))

    def mod_finish():
        for l, r, bk, m, w in mod_pending:
            if w.eng == "tensor":
                w = mod_copy(bk, m, w)
            for x in range(4):
                t = tr(bk.ap[:, 128 * x:128 * x + 128], m[:, 128 * x:128 * x + 128], ident, [w])
            msb_free[:] = [t]
            src = bk.ap.rearrange("p (x j v) -> p j x v", x=4, j=4)[:, :, :, 0:2]
            dst = mod[:, l, :, 16 * r:16 * r + 16].rearrange("p v (j x) -> p j x v", x=4)
            for v in range(2):
                w = tt(dst[:, :, :, v], src[:, :, :, v],
                       cv(BMOD + 48 * l + 16 * r, 16).rearrange("p (j x) -> p j x", x=4), ALU.add, [t, ld_c])
                mod_ready[l].append(w)
            bk.done(w)
            if r != 1:
                x, nrm, sc = ((0, N2MIX, 8), None, (1, N2FFN, 32))[r]
                for v in range(2):
                    mod_ready[l].append(stt(amod[:, l, v, x], mod[:, l, v, sc:sc + 8], 1.0,
                                            cv(nrm + 8 * l, 8), ALU.add, ALU.mult, [mod_ready[l], ld_c]))
        mod_pending.clear()

    msb_free = []

    def mod_unit(l, r, k, half, bk, m):
        def run(rawc):
            if k == 2 and half == 0:
                mod_finish()
            for j in (2 * half, 2 * half + 1):
                t = mm(bk.ap[32 * j:32 * j + 32, :], svec[:, 2 * k:2 * k + 32],
                       rawc.ap[:, 512 * (j % 2):512 * (j % 2) + 512], k == 0, k == KC - 1,
                       [rawc.ready, svec_ready, bk.free], (0, 32 * j))
            if k == KC - 1 and half == 1:
                mod_pending.append([l, r, bk, m, t])
                if (l, r) != (1, 2):
                    mod_pending[-1][4] = mod_copy(bk, m, t)
            return t
        return run

    def mod_copy(bk, m, t):
        return act(m[:], bk.ap, ACT.Copy, [t, msb_free, after_l[0]])

    place = {(0, 0): (bank[6], msb[0]), (0, 1): (bank[7], msb[1]), (0, 2): (bank[6], msb[2]),
             (1, 0): (bank[5], msb[3]), (1, 1): (bank[6], msb[4]), (1, 2): (bank[7], msb[5])}
    mod_units = [[Unit(io["w_mod"][((3 * l + r) * 8 + k) * 2 + h], None, mod_unit(l, r, k, h, *place[l, r]), None, False)
                  for r in range(3) for k in range(8) for h in range(2)] for l in range(2)]

    def modv(l, v, chunk):
        return mod[:, l, v, chunk:chunk + 1]

    c2, c2c = sb("c2", M0, [NC2]), sb("c2c", 140, [NC2C])
    wa2, wa2c = sb("wa2", M0 + 9.5, [2, 256]), sb("wa2c", 143, [2, 256])
    res_dram = nc.dram_tensor("ctx_res", [2, 128, 2560], F32, kind="Internal").ap()
    res_written = [None, None]

    class Mixer:
        pass

    lat_in, ctx_in = Mixer(), Mixer()
    lat_in.reset = [c2[:, RSTF:RSTF + T], c2[:, RSTB:RSTB + T][:, ::-1]]
    lat_in.onesbd, lat_in.bmask = c2[:, ONESBD:ONESBD + 128], c2[:, BMASK:BMASK + 128]
    lat_in.wa, lat_in.ready = Cell(wa2[:]), []
    lat_in.out = [(bank[2], bank[2].ap), (bank[3], bank[3].ap)]
    lat_in.work = Ring(bank[4:6])
    ctx_in.reset = [c2c[:, 0:256], c2c[:, 256:512][:, ::-1]]
    ctx_in.onesbd, ctx_in.bmask = c2c[:, 512:640], c2c[:, 640:768]
    ctx_in.wa, ctx_in.ready = Cell(wa2c[:]), []
    ctx_in.out = [(bank[2], bank[2].ap[:, 0:256]), (bank[2], bank[2].ap[:, 256:512])]
    ctx_in.work = Ring(bank[3:5])

    def make_mixer(l, v, N, base, hin, full, idle, shared):
        m = Mixer()
        m.l, m.v, m.N, m.full, m.hin = l, v, N, full, hin
        NT, z = N // 128, N / 512
        nm = f"{'cl'[v == 0]}{l}"
        lat = v == 0
        lay = (dict(gq=0, gk=4, gvT=8, gvtok=12, gg=16, za=20, C=22, qin=26, kin=30, ktok=34, Sen=38, aT=46, tmp=50,
                    S0=54, nq=56, nk=62, nvT=68, sq=74, sk=80, svT=82, svtok=84, rope=86, nvtok=0, swm=18,
                    res=197 - base) if lat else
               dict(gq=0, gk=2, gvT=4, gvtok=6, gg=8, za=10, C=11, qin=13, kin=15, ktok=17, Sen=19, aT=23, tmp=27,
                    S0=29, nq=30, nvT=33, sq=36, svT=39, pipe=0, res=40) if full else
               dict(gk=0, gvT=2, gvtok=4, C=8, ktok=10, tmp=17, S0=19, svT=20, za=21, res=55, Sen=65, nvT=69))

        def buf(key, shape, dt=F32, off=0.0, name=None):
            if key not in lay:
                return None
            return sb(f"{nm}_{name or key}", base + lay[key] + off, shape, dt)
        res = buf("res", [2560])
        r_nk = res[:, 0:768].rearrange("p (i t) -> p i t", i=3)
        r_nv = res[:, 768:1536].rearrange("p (n f) -> p n f", n=2)
        r_sk = res[:, 1536:1792]
        r_sv = res[:, 1792:2048].rearrange("p (n f) -> p n f", n=2)
        r_S = res[:, 2048:2560].rearrange("p (d i f) -> p d i f", d=2, i=2)
        gq, gk, gvT, gvtok, gg = [buf(k, [2, N]) for k in ("gq", "gk", "gvT", "gvtok", "gg")]
        za, C, qin, kin, ktok, tmp = buf("za", [N]), *[buf(k, [2, N]) for k in ("C", "qin", "kin", "ktok", "tmp")]
        NCH = N // 64
        Sen = buf("Sen", [NCH, 2, 128])
        aT = [buf("aT", [4, 128], F32, 2 * i, f"aT{i}") for i in range(2)]
        dec = sb(f"{nm}_dec", 8.5 if lat else 8.75, [2, NCH])
        S0 = buf("S0", [2, 2, 128] if lat else [2, 128])
        nq, nvT, sq_, svT = buf("nq", [3, N]), buf("nvT", [3, N]), buf("sq", [3, N]), buf("svT", [N])
        nk = buf("nk", [3, N]) if lat else r_nk
        sk = buf("sk", [N]) if lat else r_sk
        ready = {}

        def plain(dst, key, scale=None, perm=False):
            def evac(bks, done):
                ps, o = bks[0].ap[:, 0:N], dst
                if perm:
                    if perm == "query":
                        ps = ps.rearrange("p (r b c) -> p b r c", r=8, b=4)
                        o = dst.rearrange("p (b r c) -> p b r c", b=4, r=8)
                    else:
                        ps = ps.rearrange("p (x r w) -> p x w r", x=2, r=4)
                        o = dst.rearrange("p (x w r) -> p x w r", x=2, r=4)
                    if scale is not None:
                        w = ts(o, ps, scale, ALU.mult, [done, idle])
                    else:
                        w = copy(o, ps, [done, idle])
                elif scale is not None:
                    w = act(o, ps, ACT.Copy, [done, idle], scale=scale)
                else:
                    w = act(o, ps, ACT.Copy, [done, idle])
                bks[0].done(w)
                ready[key] = [w]
            return evac

        def silu_evac(dst, i):
            def evac(bks, done):
                w = act(dst, bks[0].ap[:, 0:N], ACT.Silu, [done, idle])
                bks[0].done(w)
                ready["gg"] = ready.get("gg", []) + [w]
            return evac

        proj = []
        for i in range(2):
            proj.append((4 + i, plain(gvT[:, i], f"gv{i}")))
        proj.append((8, plain(za[:], "za")))
        for i in range(2):
            proj.append((2 + i, plain(gk[:, i], f"gk{i}")))
        if full:
            for i in range(2):
                proj.append((i, plain(gq[:, i], f"gq{i}", 0.125)))
            for i in range(2):
                proj.append((6 + i, silu_evac(gg[:, i], i)))
        for i in range(3):
            if full:
                proj.append((9 + i, plain(nq[:, i], f"nq{i}", 0.125 if lat else -0.125, lat and "query")))
            proj.append((12 + i, plain(nk[:, i], f"nk{i}", None, lat and "key")))
            proj.append((15 + i, plain(nvT[:, i], f"nv{i}", None, lat and "key")))
        if full:
            for i in range(3):
                proj.append((18 + i, plain(sq_[:, i], f"sq{i}", 0.125 if lat else -0.125)))
        proj.append((21, plain(sk[:] if lat else sk, "sk")))
        proj.append((22, plain(svT[:], "sv")))
        m.units = [Unit(io["w_in2"][l * 23 + t], lambda: whole(hin), ev, lo="any") for t, ev in proj]
        m.proj_done = False
        ob, g4 = shared.out, shared.work
        one_bank = ob[0][0] is ob[1][0]
        hs = [slice(0, 64), slice(64, 128)]

        def wait_for(*keys):
            while not all(k in ready for k in keys):
                yield POLL
            return [ready[k] for k in keys]

        def begin():
            m.w_wa = P.dma("sync", shared.wa.ap, io["wa2"][l], f"wa2{v}", [shared.wa.free, shared.ready])
            if lat:
                m.s_init = P.dma("sync", S0[:].rearrange("p d i f -> p (d i f)"), res_dram[l][:, 2048:2560], "S0",
                                 [idle, res_written[l]])
            else:
                m.s_init = memset(S0[:], 0.0, [idle])
        m.begin = begin

        def gla():
            wa, w_wa, s_init = shared.wa.ap, m.w_wa, m.s_init
            vt = []
            for i in range(2):
                rd = yield from wait_for(f"gv{i}")
                b = g4.next()
                yield [rd, b.free]
                for n in range(NT):
                    t = tr(b.ap[:, 128 * n:128 * n + 128], gvT[:, i, 128 * n:128 * n + 128], ident, [rd, b.free])
                w = copy(gvtok[:, i], b.ap[:, 0:N], [t, idle])
                b.done(w)
                vt.append(w)
            r_za = yield from wait_for("za")
            yield [r_za]
            o_begun = set()
            q_done, k_done, kt_done, sen_done, at_done, wa_done = [], [], [], [], [], []
            tmp_done = []
            for d in range(2):
                zb = []
                for i in range(2):
                    b = g4.next()
                    t = mm(b.ap[:, 0:N], wa[:, d, 128 * i:128 * i + 128], za[:], after=[w_wa, r_za, b.free])
                    w = ts(tmp[:, i], b.ap[:, 0:N], cv(GBA + 4 * l + 2 * d + i), ALU.add,
                           [t, ld_c, idle, tmp_done], -1.0, ALU.mult)
                    b.done(w)
                    zb.append(w)
                wa_done.append(t)
                yield
                a = act(C[:], tmp[:], ACT.Abs, [zb, idle, q_done, k_done])
                a = act(C[:], C[:], ACT.Exp, [a], scale=-1.0)
                yield
                a = act(C[:], C[:], ACT.Ln, [a], bias=1.0)
                w = stt(tmp[:], tmp[:], 0.0, C[:], ALU.max, ALU.add, [a])
                sc = []
                for i in range(2):
                    rst = shared.reset[d]
                    o_, i_ = (C[:, i], tmp[:, i]) if d == 0 else (C[:, i][:, ::-1], tmp[:, i][:, ::-1])
                    sc.append(P.op("vector", lambda e, o_=o_, i_=i_, rst=rst: e.tensor_tensor_scan(
                        o_, rst, i_, 0.0, ALU.mult, ALU.add), [w, shared.ready]))
                yield
                C4 = C[:].rearrange("p i (c s) -> p i c s", s=64)
                cl = C4[:, :, :, 63 if d == 0 else 0]
                r_k = yield from wait_for("gk0", "gk1")
                dc = act(dec[:], cl, ACT.Exp, [sc, idle, sen_done], scale=-1.0 / 16)
                if full:
                    r_q = yield from wait_for("gq0", "gq1")
                    qa = act(qin[:], C[:], ACT.Exp, [sc, idle, q_done], scale=-1.0 / 16)
                    q_ = tt(qin[:], qin[:], gq[:], ALU.mult, [qa, r_q])
                    yield
                    ka = act(kin[:], C[:], ACT.Exp, [sc, idle, k_done], scale=1.0 / 16)
                    k_ = tt(kin[:], kin[:], gk[:], ALU.mult, [ka, r_k], eng="gpsimd")
                yield
                t4 = tmp[:].rearrange("p i (c s) -> p i c s", s=64)
                e = tt(t4, C4, cl.unsqueeze(3).broadcast_to([128, 2, NCH, 64]), ALU.subtract, [sc])
                e = act(tmp[:], tmp[:], ACT.Exp, [e], scale=1.0 / 16)
                e = tt(tmp[:], tmp[:], gk[:], ALU.mult, [e, r_k])
                if d == 1:
                    m.qk_used = [q_, k_, e, vt] if full else [e, vt]
                kt = []
                for i in range(2):
                    b = g4.next()
                    yield [e, b.free]
                    for n in range(NT):
                        t = tr(b.ap[:, 128 * n:128 * n + 128], tmp[:, i, 128 * n:128 * n + 128], ident, [e, b.free])
                    w = act(ktok[:, i], b.ap[:, 0:N], ACT.Copy, [t, idle, kt_done])
                    b.done(w)
                    kt.append(w)
                tmp_done = [t]
                cs = [None] * NCH
                for c0 in range(0, NCH, 4):
                    for p in range(2):
                        b = g4.next()
                        yield [kt, vt, b.free]
                        for x in range(2):
                            c = c0 + 2 * x + p
                            n = c // 2
                            for i in range(2):
                                t = mm(b.ap[:, 256 * x + 128 * i:256 * x + 128 * i + 128],
                                       ktok[hs[p], i, 128 * n:128 * n + 128], gvtok[hs[p], i, 128 * n:128 * n + 128],
                                       after=[kt, vt, b.free])
                        c = c0 + p
                        w = tt(Sen[:, c:c + 3:2], b.ap.rearrange("p (x i f) -> p x i f", x=2, i=2),
                               shared.bmask.unsqueeze(1).unsqueeze(1).broadcast_to([128, 2, 2, 128]),
                               ALU.mult, [t, idle, sen_done, shared.ready])
                        b.done(w)
                        cs[c] = cs[c + 2] = w
                kt_done = [t]
                order = list(range(NCH)) if d == 0 else list(range(NCH - 1, -1, -1))
                enter, e_ready = {}, {}
                cur, cr = (S0[:, d] if lat else S0[:]), [s_init]
                for c in order:
                    enter[c], e_ready[c] = cur, cr
                    cr = [stt(Sen[:, c, i], cur[:, i], dec[:, i, c:c + 1], Sen[:, c, i], ALU.mult, ALU.add,
                              [cr, dc, cs[c]]) for i in range(2)]
                    cur = Sen[:, c]
                if not lat:
                    m.S_out = m.S_out + [copy(r_S[:, d], cur, [cr, idle], eng="gpsimd")]
                    sen_done = [m.S_out]
                if not full:
                    continue
                for c in order:
                    yield [e_ready[c], q_, ob[0][0].free, ob[1][0].free]
                    for i in range(2):
                        t = mm(ob[i][1][:, 64 * c:64 * c + 64], enter[c][:, i], qin[:, i, 64 * c:64 * c + 64],
                               ob[i][0] not in o_begun, False, [e_ready[c], q_, ob[i][0].free])
                        o_begun.add(ob[i][0])
                sen_done = sen_done + [t]
                for x in range(2):
                    z_ = memset(aT[x][:], 0.0, [idle, at_done])
                    at_done = at_done + [z_]
                for n0 in range(0, NT, 2):
                    bh = [g4.next(), g4.next()]
                    yield [k_, q_, bh[0].free, bh[1].free]
                    cp = []
                    for h in range(2):
                        for x in range(2):
                            for i in range(2):
                                tk = slice(128 * (n0 + x), 128 * (n0 + x) + 128)
                                t = mm(bh[h].ap[:, 256 * x + 128 * i:256 * x + 128 * i + 128], kin[hs[h], i, tk],
                                       qin[hs[h], i, tk], after=[k_, q_, bh[h].free])
                        w = cpred(aT[h][:], over(tri[:, d]), heads(bh[h].ap), [t, at_done, ld_c])
                        bh[h].done(w)
                        cp.append(w)
                    yield [cp, vt]
                    for x in range(2):
                        for i in range(2):
                            for h in range(2):
                                tk = slice(128 * (n0 + x), 128 * (n0 + x) + 128)
                                t = mm(ob[i][1][hs[h], tk],
                                       gvtok[:, i, 128 * (n0 + x) + 64 * h:128 * (n0 + x) + 64 * h + 64],
                                       aT[h][:, 2 * x + i], False,
                                       d == 1 and n0 + x == NT - 1 and (i == 1 or not one_bank), [cp, vt])
                    at_done = [t]
                q_done, k_done = [t], [t]
            shared.wa.free = wa_done
            if not full:
                return
            m.mixed = [t]
            r_g = ready["gg"]
            squares = [act(tmp[:, i], ob[i][1][:, 0:N], ACT.Square, [t, tmp_done]) for i in range(2)]
            ends, ls = [], []
            for i in range(2):
                b = g4.next()
                yield [squares[i], b.free]
                x = mm(b.ap[:, 0:N], shared.onesbd, tmp[:, i], after=[squares[i], b.free])
                ls.append(act(C[:, i], b.ap[:, 0:N], ACT.Ln, [x], bias=EPS, scale=1.0 / 64))
                b.done(ls[-1])
            rs = act(C[:], C[:], ACT.Exp, ls, scale=-0.5)
            ws = []
            for i in range(2):
                w = tt(tmp[:, i], ob[i][1][:, 0:N], C[:, i], ALU.mult, [rs, x, squares])
                ends.append(w)
                ws.append(stt(tmp[:, i], tmp[:, i], cv(GNORM + 2 * l + i), gg[:, i], ALU.mult, ALU.mult, [w, r_g]))
            m.normed = ws
            for i in range(2):
                ob[i][0].free = ends
            while not m.proj_done:
                yield POLL
            ha = []
            for i in range(2):
                hi, lo = hin[i]
                hi.ready = [act(hi.ap, tmp[:, i], ACT.Copy, [ws[i], hi.free])]
                ha += hi.ready
            es = []
            for i in range(2):
                hi, lo = hin[i]
                lo.ready = [tt(lo.ap, tmp[:, i], hi.ap.bitcast(F32), ALU.subtract, [ha[i], lo.free])]
                es += lo.ready
            m.gla_end = ha + es

        m.S_out, m.gla_end, m.qk_used, m.mixed, m.normed = [], [], [], [], []
        m.gla = gla

        def store_ctx():
            ws = []
            yield from wait_for("nv0", "nv1", "nv2", "sv", "nk0", "nk1", "nk2", "sk")
            for i in range(3):
                b = g4.next()
                yield [ready[f"nv{i}"], b.free]
                for n in range(2):
                    t = tr(b.ap[:, 128 * n:128 * n + 128], nvT[:, i, 128 * n:128 * n + 128], ident,
                           [ready[f"nv{i}"], b.free])
                w = copy(r_nv[:, :, 128 * i:128 * i + 128], b.ap[:, 0:256].rearrange("p (n f) -> p n f", n=2), [t, idle])
                b.done(w)
                ws.append(w)
            b = g4.next()
            yield [ready["sv"], b.free]
            for n in range(2):
                t = tr(b.ap[:, 128 * n:128 * n + 128], svT[:, 128 * n:128 * n + 128], ident, [ready["sv"], b.free])
            w = copy(r_sv, b.ap[:, 0:256].rearrange("p (n f) -> p n f", n=2), [t, idle])
            b.done(w)
            ws.append(w)
            m.v_ready = ws
            keys = [ready[k] for k in ("nk0", "nk1", "nk2", "sk")]
            res_written[l] = P.dma("sync", res_dram[l], res[:], "res", [ws, keys, m.S_out])
        m.store_ctx = store_ctx

        class Pairs:

            def __init__(self, ch, cell, arrange=None):
                self.ch, self.cell, self.arrange, self.ws = ch, cell, arrange, []

        class Pair:

            def __init__(self, out, tile, n, scores, vals, ready, bias=None, sink=None, readers=None):
                self.out, self.tile, self.n, self.scores, self.vals, self.ready = out, tile, n, scores, vals, ready
                self.bias, self.sink, self.readers = bias, sink, [] if readers is None else readers

        def soonest(after, **costs):
            ready_at = max([0] + [o.end + 130 for o in flat(after)])
            return min(costs, key=lambda e: max(P.clock[e], ready_at) + costs[e])

        def quick(out, in_, after):
            n = width(out)
            slow = in_.tensor is psum
            eng = soonest(after, scalar=60 + 0.87 * n, vector=65 + (1.05 if slow else 0.53) * n)
            return (acopy if eng == "scalar" else copy)(out, in_, after)

        def scaled(x, by, after):
            n = width(x)
            eng = soonest(after, scalar=160 + 0.87 * n, vector=120 + 0.53 * n, gpsimd=150 + 2.1 * n)
            if eng == "scalar":
                return act(x, x, ACT.Copy, after, scale=by)
            if eng == "vector":
                return ts(x, x, by, ALU.mult, after)
            return tt(x, x, by.broadcast_to([128, n]), ALU.mult, after, eng)

        def rest_of(out, a, b, after):
            eng = soonest(after, vector=65 + 1.05 * width(out), gpsimd=100 + 2.2 * width(out))
            return tt(out, a, b, ALU.subtract, after, eng)

        def twice(x, dup, low, after):
            ws = []
            for p in range(2):
                own = quick(dup[hs[p], p], x[hs[p]], after)
                ws += [own, quick(dup[hs[1 - p], p], x[hs[p]], after),
                       tt(low[hs[p]], x[hs[p]], dup[hs[p], p].bitcast(F32), ALU.subtract, [own, after])]
            return ws

        def stacked(x, both, after):
            ws = []
            for p in range(2):
                own = quick(both[hs[p], p], x[hs[p]], after)
                ws += [own, tt(both[hs[1 - p], p], x[hs[p]], both[hs[p], p].bitcast(F32), ALU.subtract, [own, after])]
            return ws

        def split_pairs(out):
            while lat and not (m.na_done if out.ch > 4 else m.proj_done):
                yield POLL
            yield [out.ws]
            hi, lo = hin[out.ch]
            o, h_, l_ = out.cell.ap, hi.ap, lo.ap
            if out.arrange:
                o, h_, l_ = out.arrange[0](o), out.arrange[1](h_), out.arrange[1](l_)
            idle3 = m.na_end if out.ch > 4 else []
            a = act(h_, o, ACT.Copy, [out.ws, hi.free, idle3])
            b = rest_of(l_, o, h_.bitcast(F32), [a, lo.free, idle3])
            out.cell.done(b)
            hi.ready, lo.ready = [a], [b]
            m.end = m.end + [a, b]
            m.split.add(out.ch)

        def take(groups, count):
            while True:
                free = [g[:count] for g in groups if not any(bank[b].held for b in g[:count])]
                if free:
                    break
                yield POLL
            g = min(free, key=lambda g: max([0] + [o.end for b in g for o in flat(bank[b].free)]))
            for b in g:
                bank[b].held = True
            return [bank[b] for b in g], psum[:, g[0]:g[0] + count, :].rearrange("p a b -> p (a b)")

        def attend(items, sides, groups, S, x, after, bb=None):
            st = sb(f"{nm}_st{x}", (8.5 if lat else 8.75) + (x + 1) / 32, [8])
            least, sums, rc, es = [st[:, 2 * j:2 * j + 2] for j in range(4)]
            col = [slice(p, p + 1) for p in range(2)]
            used = [after]
            m.open += 1

            def following():
                if items and bb:
                    bb.ready = [P.dma("gpsimd", bb.ap.rearrange("p (x w) -> p x w", w=256)[:, 0:3:2], items[0].bias,
                                      f"nab{x}", [bb.free, after]), bb.zero]
                return items.pop(0) if items else None
            coming = following()
            while coming:
                it = coming
                n, out, count = it.n, it.out, -(-it.n // 256)
                at = [slice(n * p, n * p + n) for p in range(2)]
                while not it.ready():
                    yield POLL
                yield [it.ready()]
                cells, sp = yield from take(groups, count)
                free = [c.free for c in cells]
                yield [it.ready(), free, bb.ready if bb else it.bias and it.bias[0][1]]
                done, wrote = [], {}
                for p in range(2):
                    if p and count == 1:
                        yield done
                    for c0, c1, parts_ in it.scores[p]:
                        other = wrote.get(c0 // 512) if p else None
                        for k, (q, key) in enumerate(parts_):
                            t = mm(sp[:, c0:c1], q, key, k == 0, k == len(parts_) - 1, [it.ready(), free, other])
                        if not p:
                            wrote[c0 // 512] = t
                    done.append(t)
                it.readers.append(t)
                apart = n == 512
                if state["drain"]:
                    yield done
                if it.bias is not None:
                    ws = []
                    for p in range(2):
                        mk, got = (bb.ap[:, 256 * p:256 * p + 512], bb.ready) if bb else it.bias[p]
                        init = 3e38 if it.sink is None else it.sink[:, col[p]]
                        ws.append(dve(lambda e, mk=mk, n=n, init=init, p=p, at=at, sp=sp: e.tensor_tensor_reduce(
                            S[:, at[p]], sp[:, at[p]], mk, -1.0, init, ALU.add, ALU.min, least[:, col[p]]),
                            [done[p] if apart else done, got, nsink_ready, used], n + 120))
                    if bb:
                        bb.free = ws
                    for c in cells:
                        c.done(ws)
                    src = S
                else:
                    w = dve(lambda e, n=n, sp=sp: e.tensor_reduce(least, sp[:, 0:2 * n].rearrange("p (h k) -> p h k", h=2),
                                                                  AX.X, ALU.min), [done, used], 2 * n)
                    if it.sink is not None:
                        w = tt(least, least, it.sink, ALU.min, [w, nsink_ready])
                    src, ws = sp, [w, w]
                coming = following()
                if state["drain"]:
                    yield ws
                ex = [act(S[:, at[p]], src[:, at[p]], ACT.Exp, [ws[p], used], bias=least[:, col[p]], scale=-1.0,
                          accum=sums[:, col[p]]) for p in range(2)]
                if it.bias is None:
                    for c in cells:
                        c.done(ex)
                total = ex
                if it.sink is not None:
                    d = tt(es, least, it.sink, ALU.subtract, ws)
                    e2 = act(es, es, ACT.Exp, [d])
                    total = [tt(sums[:, col[p]], sums[:, col[p]], es[:, col[p]], ALU.add, [ex[p], e2]) for p in range(2)]
                sc = []
                for p in range(2):
                    if p == 0:
                        yield total
                    r = dve(lambda e, p=p: e.reciprocal(rc[:, col[p]], sums[:, col[p]]), [total[p]], 1)
                    sc.append(scaled(S[:, at[p]], rc[:, col[p]], [r, ex[p]]))
                yield [sc[0]]
                cells, sp = yield from take(groups, count)
                cp = []
                for k, c in enumerate(cells):
                    blocks = range(4 * k, min(4 * k + 4, 2 * n // 128))
                    last = sc[1 if 128 * blocks[-1] >= n else 0]
                    yield [last, c.free]
                    for b in blocks:
                        t = tr(sp[:, 128 * b:128 * b + 128], S[:, 128 * b:128 * b + 128], ident, [last, sc[0], c.free])
                    cols = slice(128 * blocks[0], 128 * blocks[-1] + 128)
                    cp.append(quick(S[:, cols], sp[:, cols], [t]))
                yield [cp, m.v_ready]
                for j in range(n // 128):
                    for p in range(2):
                        t = mm(sp[hs[p], 0:128], it.vals[p][j], S[:, n * p + 128 * j:n * p + 128 * j + 128], j == 0,
                               j == n // 128 - 1, [cp, m.v_ready])
                used = [t]
                o = out.cell
                if not out.ws:
                    while o.held:
                        yield POLL
                    o.held = True
                w = quick(o.ap[:, 128 * it.tile:128 * it.tile + 128], sp[:, 0:128], [t, o.free])
                for c in cells:
                    c.done(w)
                out.ws.append(w)
                m.end = m.end + [t, w]
                if len(out.ws) == NT:
                    sides.insert(0, Side(split_pairs(out), 2.0))
                yield
            m.open -= 1

        m.open, m.end, m.last, m.split, m.na_end = 0, [], [], set(), []

        def ctx_attention(sides):
            items = []
            turn = [Cell(buf("nvT", [N], F32, x, f"o{x}")[:]) for x in range(3)]
            k_ready = [ready[k] for k in ready if k[:2] in ("nk", "nq", "sq", "sk")]
            for i in range(6):
                out = Pairs(2 + i, turn[i % 3])
                for n in range(NT):
                    tile, scores, vals = slice(128 * n, 128 * n + 128), [], []
                    for p in range(2):
                        h = 2 * i + p
                        q, k = (nq[hs[p], i, tile], r_nk[hs[p], i]) if i < 3 else (sq_[hs[p], i - 3, tile], r_sk[hs[p], :])
                        scores.append([(256 * p, 256 * p + 256, [(q, k)])])
                        vals.append([r_nv[:, x, 64 * h:64 * h + 64] if i < 3 else r_sv[:, x, 64 * p:64 * p + 64]
                                     for x in range(2)])
                    sink = None if i < 3 else nsink[:, 6 * l + i - 3:6 * l + i + 1:3]
                    items.append(Pair(out, n, 256, scores, vals, lambda: k_ready, None, sink))
            for x in range(4):
                S = sb(f"{nm}_S{x}", base + 2 * x, [512])
                sides.insert(x, Side(attend(items, sides, [(2,), (3,), (4,)], S, x, m.gla_end), 2.0))
            while m.open or items or len(m.split) < 6:
                yield POLL

        def lat_attention(sides):
            nvtok, svtok = buf("nvtok", [4, 2, 3, 128]), buf("svtok", [4, 128])
            ld = P.dma("sync", res[:, 0:2048], res_dram[l][:, 0:2048], f"res{l}", [m.res_idle, res_written[l]])
            m.v_ready = [ld]
            turn = [Cell(sb(f"{nm}_o{x}", base + kb, [N])[:]) for x, kb in enumerate((96, 68, 70, 72))]

            def at(name, kb, shape, dt=F32R):
                return sb(f"{nm}_{name}", base + kb, shape, dt)
            slots = [[at(f"{a}{x}", kb, sh) for a, kb, sh in zip(("nqd", "nql", "nks", "rks"), kbs,
                                                                  ([2, T], [T], [2, T], [2, 256]))]
                     for x, kbs in enumerate(((26, 20, 30, 54), (34, 42, 38, 44)))]
            made, swept = [[], [], []], [[], [], []]

            def values(i, ring):
                rd = yield from wait_for(f"nv{i}")
                while not m.qk_used or (i and not m.mixed):
                    yield POLL
                for y in range(2):
                    b = ring.next()
                    yield [b.free, rd, m.qk_used]
                    for k in range(4):
                        c0 = min(max(16 * (2 * y + k // 2) - 8, 0), 32)
                        src = nvT[:, i, 256 * (k % 2) + 4 * c0:256 * (k % 2) + 4 * c0 + 128]
                        t = tr(b.ap[:, 128 * k:128 * k + 128], src, ident, [rd, b.free])
                    w = quick(nvtok[:, 2 * y:2 * y + 2, :, i], b.ap.rearrange("p (c x f) -> p c x f", c=2, x=2),
                              [t, m.qk_used])
                    b.done(w)
                    m.v_ready.append(w)
                turn[1 + i].free = [t]

            def operands(i):
                rd = yield from wait_for(f"nq{i}", f"nk{i}")
                while not m.mixed or (i == 2 and len(swept[0]) < NT):
                    yield POLL
                idle4 = [rd, m.mixed, swept[0] if i == 2 else [], ld]
                yield idle4
                nqd, nql, nks, rks = slots[i % 2]
                made[i] = twice(nq[:, i], nqd, nql, idle4)
                yield
                made[i] = made[i] + stacked(nk[:, i], nks, idle4) + stacked(r_nk[:, i], rks, idle4)

            def by_rows(ap):
                return ap.rearrange("p (r b c) -> p b r c", r=8, b=4)

            def by_blocks(ap):
                return ap.rearrange("p (b r c) -> p b r c", r=8, b=4)
            na, swa, na_sides = [], [], []
            for i in range(3):
                out = Pairs(2 + i, turn[i], (by_blocks, by_rows))
                nqd, nql, nks, rks = slots[i % 2]
                for n in range(NT):
                    c0, tile, scores, vals = min(max(16 * n - 8, 0), 32), slice(128 * n, 128 * n + 128), [], []
                    for p in range(2):
                        h = 2 * i + p
                        kw = nks[:, p].rearrange("p (x w) -> p x w", x=2)[:, :, 4 * c0:4 * c0 + 128]
                        near = [(nqd[:, p, tile], kw), (nql[hs[p], tile], kw[hs[p]])]
                        far = [(nqd[:, p, tile], rks[:, p]), (nql[hs[p], tile], rks[hs[p], p])]
                        vn = [nvtok[:, n, x, i, hs[p]] for x in range(2)]
                        vf = [r_nv[:, x, 64 * h:64 * h + 64] for x in range(2)]
                        o = 512 * p
                        both = [(near, vn), (far, vf)] if p == 0 else [(far, vf), (near, vn)]
                        scores.append([(o + 256 * x, o + 256 * x + 256, both[x][0]) for x in range(2)])
                        vals.append(both[0][1] + both[1][1])
                    na.append(Pair(out, n, 512, scores, vals, lambda i=i: made[i],
                                   io["na_bias"][l, 2 * i:2 * i + 2, n].rearrange("h p w -> p h w"), None, swept[i]))

            groups = [(6, 7)]

            def grid(x, S, bias, after):
                bb = Cell(bias[:])
                bb.zero = memset(bb.ap[:, 256:512], 0.0, [after])
                m.end = m.end + [bb.zero]
                na_sides.append(Side(attend(na, sides, groups, S, x, after, bb), 2.0))
                sides.insert(0, na_sides[-1])

            yield from values(0, Ring(bank[6:8]))
            yield from operands(0)
            grid(0, at("NS0", 12, [1024], F32), at("NB0", 46, [768], F32), m.mixed)
            yield from values(1, g4)
            yield from operands(1)
            yield from values(2, g4)
            sides.append(Side(operands(2)))
            while not m.normed:
                yield POLL
            groups.append((2, 3))
            grid(1, at("NS1", 16, [1024], F32), at("NB1", 22, [768], F32), m.normed)
            sqs = [at(f"sqs{i}", kb, [2, T]) for i, kb in enumerate((56, 62, 74))]
            skd, skl, rskl, swm = [sb(f"{nm}_{a}", kb, sh, dt) for a, kb, sh, dt in
                                   (("skd", M0, [2, T], F32R), ("skl", M0 + 9, [T], F32R), ("rskl", M0 + 11, [256], F32R),
                                    ("swm", M0 + 4.5, [896], F32))]
            rskd = at("rskd", 82, [2, 256])
            ldm = [P.dma("sync", swm[:], io["swa_mask"], "swm", m.mixed)]
            s_made, turned = [], []
            for i in range(3):
                w = yield from rope(sq_[:, i], f"sq{i}", turned)
                s_made += stacked(sq_[:, i], sqs[i], [w, made[0], made[1], s_made])
            w = yield from rope(sk[:], "sk", turned)
            yield from wait_for("sv")
            b = g4.next()
            yield [b.free, ready["sv"]]
            for n in range(4):
                t = tr(b.ap[:, 128 * n:128 * n + 128], svT[:, 128 * n:128 * n + 128], ident, [ready["sv"], b.free])
            v_ = copy(svtok[:].rearrange("p n f -> p (n f)"), b.ap, [t, idle])
            b.done(v_)
            s_made += twice(sk[:], skd, skl, [w, m.mixed]) + twice(r_sk, rskd, rskl, [ld, w, v_])
            for i in range(3):
                out = Pairs(5 + i, turn[(3 + i) % 4])
                for n in range(NT):
                    lo, hi = max(n - 1, 0), min(n + 2, 4)
                    w, tile, scores, vals, bias = 128 * (hi - lo), slice(128 * n, 128 * n + 128), [], [], []
                    for p in range(2):
                        o, first = (w + 256) * p, n == 0 or (p == 1 and n < 3)
                        far, near = (o + w, o) if first else (o, o + 256)
                        cuts = [c for c in (near, 512, near + w) if near <= c <= near + w]
                        pieces = [(a, b, skd[:, p, 128 * lo + a - near:128 * lo + b - near],
                                   skl[hs[p], 128 * lo + a - near:128 * lo + b - near])
                                  for a, b in zip(cuts, cuts[1:]) if b > a]
                        pieces.append((far, far + 256, rskd[:, p], rskl[hs[p]]))
                        pieces.sort(reverse=True, key=lambda x: x[0] if p else x[0] // 512)
                        q = sqs[i][:, p, tile]
                        scores.append([(a, b, [(q, k2), (q[hs[p]], k1)]) for a, b, k2, k1 in pieces])
                        v = [[svtok[:, x, 64 * p:64 * p + 64] for x in range(lo, hi)],
                             [r_sv[:, x, 64 * p:64 * p + 64] for x in range(2)]]
                        vals.append(v[0] + v[1] if first else v[1] + v[0])
                        c = 384 if n == 0 else 256 if first else 0
                        bias.append((swm[:, c:c + w + 256], ldm))
                    swa.append(Pair(out, n, w + 256, scores, vals, lambda: s_made, bias,
                                    nsink[:, 6 * l + i:6 * l + i + 4:3]))
            while not m.proj_done:
                yield POLL
            groups += [(0, 1), (4, 5)]
            grid(2, sb(f"{nm}_NS2", 61, [1024]), sb(f"{nm}_NB2", 75, [768]), [x.free for c in range(5, 8) for x in hin[c]])
            def window(x, kb, after):
                return Side(attend(swa, sides, [(2, 3, 4), (5, 6, 7)], at(f"SS{x}", kb, [1280], F32), 3 + x, after), 2.0)
            while na:
                yield POLL
            while not m.gla_end:
                yield POLL
            sides.insert(3, window(0, 49, m.gla_end))
            while any(x.alive for x in na_sides) or len(m.split) < 3:
                yield POLL
            m.na_end = m.end
            m.na_done = True
            sides[0:0] = [window(x, 21 + 5 * x, m.na_end) for x in range(1, 5)]
            yield
            while m.open or swa or len(m.split) < 6:
                yield POLL
            lat_in.ready.append(P.dma("sync", c2[:], io["consts2"][:, 0:NC2], "c2", m.end))
            shared.wa.free = m.end
        m.na_done = False

        def rope(x, key, done):
            rt = buf("rope", [T], F32, 0.0, f"rope_{key}")
            r = yield from wait_for(key)
            b = g4.next()
            yield [r, b.free]
            t = mm(b.ap, c2[:, PERM:PERM + 128], x, after=[r, b.free, shared.ready])
            w = tt(rt[:], b.ap, c2[:, SIN:SIN + T], ALU.mult, [t, done, idle])
            b.done(w)
            w2 = tt(x, x, c2[:, COS:COS + T], ALU.mult, [t], eng="gpsimd")
            w = tt(x, x, rt[:], ALU.add, [w, w2])
            done[:] = [w]
            return w
        m.attention = lat_attention if lat else ctx_attention
        return m

    def out_units(l, v, N, pairs, x, nrm, after=(), ring=None):
        def evac(part, o):
            def run(bks, done):
                w = stt(x[o[0]].ap, bks[0].ap[:, 0:N], modv(l, v, 16 + o[0]), x[o[0]].ap, ALU.mult, ALU.add,
                        [done, x[o[0]].ready, mod_ready[l]])
                bks[0].done(w)
                x[o[0]].ready = [w]
                if part:
                    nrm.add(o[0], [w], after)
                o.pop(0)
            return run
        units = []
        for part in range(2):
            for s in range(4):
                u = Unit(io["w_out2"][l * 8 + 4 * part + s], lambda part=part: whole(*[pairs[4 * part:4 * part + 4]] * 2),
                         evac(part, [2 * s, 2 * s + 1]), ring, lo="any")
                u.each = True
                units.append(u)
        return units

    def ffn_units(l, v, N, pairs, x, nrm, places, ring, after):
        nm = f"f{v}{l}"
        hid = [tuple(Cell(sb(f"{nm}h{k}{y}", places[2 * k + y], [N], F32R)[:]) for y in range(2)) for k in range(HALF)]
        sg = Ring([Cell(sb(f"{nm}sg{i}", places[2 * HALF + i], [N])) for i in range(2)])
        held = {}
        units = []
        lo_eng = "any" if v else "vector"

        def gate(k):
            def run(bks, done):
                c = held[k] = sg.next()
                a = act(c.ap[:], bks[0].ap[:, 0:N], ACT.Silu, [done, c.free, after])
                bks[0].done(a)
                c.ready = [a]
            return run

        def up(k):
            def run(bks, done):
                c = held.pop(k)
                hi, lo = hid[k % HALF]
                w = tt(c.ap[:], bks[0].ap[:, 0:N], c.ap[:], ALU.mult, [done, c.ready])
                bks[0].done(w)
                a = act(hi.ap, c.ap[:], ACT.Copy, [w, hi.free, after])
                b = tt(lo.ap, c.ap[:], hi.ap.bitcast(F32), ALU.subtract, [a, lo.free, after])
                c.done(b)
                hi.ready, lo.ready = [a], [b]
            return run

        def down_groups(s):
            def run():
                out = []
                for b in range(8 * s, 8 * s + 8):
                    o, k = divmod(b, HALF)
                    if not out or out[-1][0] != (nm, o):
                        out.append([(nm, o), [], k == 0, False])
                    out[-1][1].append(hid[k])
                    out[-1][3] = k == HALF - 1
                return out
            return run

        def down(half, s):
            ends = [b // HALF for b in range(8 * s, 8 * s + 8) if b % HALF == HALF - 1]

            def run(bks, done):
                for o, bk, t in zip(ends, bks, done):
                    w = stt(x[o].ap, bk.ap[:, 0:N], modv(l, v, 40 + o), x[o].ap, ALU.mult, ALU.add, [t, x[o].ready])
                    bk.done(w)
                    x[o].ready = [w]
                    if half:
                        nrm.add(o, [w])
            return run

        for half in range(2):
            for k in range(HALF * half, HALF * half + HALF):
                units.append(Unit(io["w_gate2"][l * 22 + k], lambda: whole(pairs), gate(k), ring, lo=lo_eng))
                units.append(Unit(io["w_up2"][l * 22 + k], lambda: whole(pairs), up(k), ring, lo=lo_eng))
            for s in range(HALF):
                units.append(Unit(io["w_down2"][(l * 2 + half) * HALF + s], down_groups(s), down(half, s), ring,
                                  lo=lo_eng))
        return units

    TC = 256
    xct = sb("xct", 113, [KC, TC])
    xc = [Cell(xct[:, c, :]) for c in range(KC)]
    hct = [sb("hchi", 97, [KC, TC], F32R), sb("hclo", 105, [KC, TC], F32R)]
    hct_plain = sb("hct_plain", 105, [KC, TC])
    hc = [(Cell(hct[0][:, c]), Cell(hct[1][:, c], hct_plain[:, c])) for c in range(KC)]
    ctx_late = Ring(bank[0:5])
    cnorm = Norm("cn", 121, TC, xc, ctx_late)
    idle_c, idle_l = [[], []], [[], []]
    cm = [make_mixer(l, 1, TC, kb, hc, l == 0, idle_c[l], ctx_in) for l, kb in ((0, 145), (1, 113))]
    lm = [make_mixer(l, 0, T, M0 + 12, hl, True, idle_l[l], lat_in) for l in range(2)]
    after_c, after_l = [], [[], []]
    u_cout = out_units(0, 1, TC, hc, xc, cnorm, (), ctx_late)
    u_cffn = ffn_units(0, 1, TC, hc, xc, cnorm, list(range(145, 152)) + list(range(168, 185)), ctx_late, after_c)
    u_lout = [out_units(l, 0, T, hl, xr, norm, lm[l].last) for l in range(2)]
    u_lffn = [ffn_units(l, 0, T, hl, xr, norm, [M0 + 12 + 2 * i for i in range(24)], late_banks, after_l[l])
              for l in range(2)]

    def mixed(main, other):
        out, n = [], 0
        for i, u in enumerate(main):
            upto = -(-len(other) * (i + 1) // len(main))
            out += other[n:upto] + [u]
            n = upto
        return out

    def frontier():
        return [P.queues[e][-1] for e in ("tensor", "vector", "scalar", "gpsimd")]

    NWQ = 3
    m0, m1 = mod_units
    spine += u_dn[:2] + mixed(u_dn[2:], m0[:32]) + u_da + u_z + u_merge[:2] + mixed(u_merge[2:], m0[32:]) + u_out
    w1 = cm[0].units[:6] + mixed(cm[0].units[6:], u_wq[:NWQ])
    for u in m1[8:20] + m1[44:]:
        u.early = True
    spine += mixed(w1 + u_wq[NWQ:], m1[:8]) + u_cout[:2] + m1[8:12] + u_cout[2:]
    spine += u_cffn[:2] + m1[12:16] + u_cffn[2:] + cm[1].units + u_peer
    spine += lm[0].units + u_lout[0]
    spine += u_lffn[0][:2] + m1[16:20] + mixed(u_lffn[0][2:], m1[20:44])
    spine += lm[1].units[:2] + m1[44:] + lm[1].units[2:] + u_lout[1] + u_lffn[1]

    def mixers(m):
        m.res_idle = frontier()
        sides = []
        sides += [Side(m.gla(), 2.0), Side(m.attention(sides))]
        run_spine(len(m.units) - 2, sides)
        m.proj_done = True
        drain(sides, lambda: m.na_done)
        run_spine(4, sides)
        drain(sides)
        m.last += m.end
        run_spine(4, sides)

    def ctx_mixers(m, sides):
        yield from m.gla()
        yield from m.store_ctx()
        if m.full:
            yield from m.attention(sides)

    def choose():
        sel = yield from top_keys()
        yield from top_pairs(sel)
        yield from norm.apply(lambda c: cv(G_FFN + c), hl, None, to_tokens)
        for p, q in zip(hd, hl):
            for x, y in zip(p, q):
                x.ready = y.ready

    first_norm()
    start_mod()
    start_conv([c.ready for c in hlo])
    run_pair([], False)
    load_masks()
    run_spine(11, [])
    mod_finish()
    w = tt(gchain[:], cv(G_FIN, 8), cv(G_FIN, 8), ALU.mult, ld_c)
    act(gchain[:], gchain[:], ACT.Sqrt, [w], bias=EPS)
    sides = [Side(dilated())]
    sides.insert(0, Side(delta(sides)))
    run_spine(36, sides)
    run_spine(6, sides)
    drain(sides)
    chain_end = [S_ready, o_ready]
    for c in range(KC):
        xr[c].ready = [P.dma("sync", xr[c].ap, io["xT"][:, c, :], f"x{c}", [chain_end] + [a.ready for a in odn_c[3]])]
    sides = [Side(finish_mixers(chain_end))]
    run_spine(2 * GL - 2, sides)
    drain(sides)
    msb_free[:] = frontier()
    run_spine(24 - 2 * GL, [])
    mod_finish()

    def ctx_norm():
        for c in range(KC):
            xc[c].ready = [P.dma("sync", xc[c].ap, io["ctxT"][:, c, :], f"c{c}", idle)]
        for c in range(KC):
            yield [xc[c].ready, cnorm.summed]
            cnorm.add(c, xc[c].ready, idle)
        for p in hc:
            for x in p:
                x.free = idle
        yield from cnorm.apply(lambda c: amod[:, 0, 1, 0, c:c + 1], hc, lambda c: modv(0, 1, c), needs=mod_ready[0])
    idle = frontier()
    sides = [Side(ctx_norm())]
    run_spine(8, sides)
    drain(sides)
    norm.rs()
    idle_c[0] += frontier()
    ctx_in.ready.append(P.dma("sync", c2c[:], io["consts2"][:, NC2:], "c2c", idle_c[0]))
    cm[0].begin()
    wq_idle += idle_c[0]
    msb_free[:] = idle_c[0]

    sides = [Side(norm.apply(lambda c: cv(G_FFN + c), hl))]
    run_spine(6, sides)
    drain(sides)
    sides.append(Side(ctx_mixers(cm[0], sides), 2.0))
    sides.append(Side(dense_gates()))
    sides.append(Side(choose()))
    run_spine(17 + NWQ, sides)
    cm[0].proj_done = True
    run_spine(16 - NWQ, sides)
    drain(sides, lambda: cm[0].gla_end)
    drain(sides, lambda: cm[0].end and not cm[0].open)
    g_idle += cm[0].end + cm[0].gla_end
    run_early()
    after_c += cm[0].end + cm[0].gla_end
    run_spine(8, sides)

    now(cnorm.apply(lambda c: amod[:, 0, 1, 1, c:c + 1], hc, lambda c: modv(0, 1, 24 + c), at_once=True, needs=mod_ready[0]))
    run_pair(sides)
    run_spine(len(u_cffn) - 2, sides)
    mod_finish()
    now(cnorm.apply(lambda c: amod[:, 1, 1, 0, c:c + 1], hc, lambda c: modv(1, 1, c), at_once=True, needs=mod_ready[1]))
    gin[0].free = frontier()
    idle_c[1] += gin[0].free + [res_written[0]]
    cm[1].begin()
    sides.insert(0, Side(ctx_mixers(cm[1], sides), 2.0))
    run_pair(sides)
    run_spine(11, sides)
    drain(sides)
    end_w = frontier()
    gin[1].free = end_w + [res_written[1]]
    for n in range(2):
        for p in agc[n]:
            for x in p:
                x.free = gin[1].free if n else end_w
    for c in uact.cells:
        c.free = end_w
    load_gates(1)
    sides.append(Side(chosen_experts(end_w)))
    run_spine(GJ, sides)
    for g in range(NGR):
        if g + 2 < NGR:
            load_gates(g + 2)
        if g + 1 == NGR:
            drain(sides)
        run_spine(16 if g + 1 < NGR else 8, sides)
    for p, q in zip(hd, hl):
        for x, y in zip(p, q):
            y.free = x.free
    def finish_block1():
        rs = norm.rs()
        for c in range(KC):
            yield
            xr[c].ready = [stt(xr[c].ap, xr[c].ap, cv(G_FIN + c), norm.r[:], ALU.mult, ALU.mult,
                               [rs, xr[c].ready, chain_norm.used])]
        norm.used = xr[KC - 1].ready
    lat_in.ready.append(P.dma("sync", c2[:], io["consts2"][:, 0:NC2], "c2", chain_norm.summed))
    for l in range(2):
        sides = []
        if l == 0:
            g = tt(gboth[:], cv(G_FIN, 8), amod[:, 0, 0, 0], ALU.mult, [ld_c, mod_ready[0]])
            chain_norm.ready = chain_norm.rs(EPS * EPS) + [g]
            now(chain_norm.apply(lambda c: gboth[:, c:c + 1], hl, lambda c: modv(0, 0, c), at_once=True))
            sides.append(Side(finish_block1()))
        else:
            now(norm.apply(lambda c: amod[:, l, 0, 0, c:c + 1], hl, lambda c: modv(l, 0, c), at_once=True, needs=mod_ready[l]))
        idle_l[l] += frontier()
        lm[l].begin()
        run_pair(sides)
        mod_finish()
        drain(sides)
        mixers(lm[l])
        now(norm.apply(lambda c: amod[:, l, 0, 1, c:c + 1], hl, lambda c: modv(l, 0, 24 + c), at_once=True, needs=mod_ready[l]))
        after_l[l] += frontier()
        run_pair([])
        run_spine(len(u_lffn[l]) - 2, [])
    rs = norm.rs()
    for c in range(KC):
        w = stt(xr[c].ap, xr[c].ap, cv(N2FIN + c), norm.r[:], ALU.mult, ALU.mult, [rs, xr[c].ready])
        P.dma("sync", io["out"][:, c, :], xr[c].ap, f"x{c}", [w])
    P.emit(sem_of)


def constants(a):
    c = np.zeros((128, NCONST), np.float32)
    i = np.arange(128)
    c[:, IDENT:IDENT + 128] = np.eye(128)
    c[:, UF:UF + 128] = i[:, None] <= i[None, :]
    c[:, UB:UB + 128] = i[:, None] >= i[None, :]
    c[:, MASKF:MASKF + 128] = np.where(i[None, :] <= i[:, None], 0.0, NEG)
    c[:, MASKB:MASKB + 128] = np.where(i[None, :] >= i[:, None], 0.0, NEG)

    def cols(v):
        return v.reshape(-1, 128).T
    c[:, G_MIX:G_MIX + 8] = cols(a["norm_mix"][0])
    c[:, G_FFN:G_FFN + 8] = cols(a["norm_ffn"][0])
    c[:, G_FIN:G_FIN + 8] = cols(a["norm_final"])
    c[:, CONVW:CONVW + 48] = a["dn_conv"][0].reshape(4, 12, 128).transpose(2, 1, 0).reshape(128, 48)
    c[:, DTB:DTB + 8] = a["dn_dt_bias"][0].reshape(1, 8)
    c[:, ALOG:ALOG + 8] = a["dn_a_log"][0].reshape(1, 8)
    for l in range(2):
        c[:, BMOD + 48 * l:BMOD + 48 * l + 48] = cols(a["b_mod_2"][l])
        c[:, N2MIX + 8 * l:N2MIX + 8 * l + 8] = cols(a["norm_mix_2"][l])
        c[:, N2FFN + 8 * l:N2FFN + 8 * l + 8] = cols(a["norm_ffn_2"][l])
        c[:, GBA + 4 * l:GBA + 4 * l + 2] = cols(a["gla_ba_f_2"][l])
        c[:, GBA + 4 * l + 2:GBA + 4 * l + 4] = cols(a["gla_ba_b_2"][l])
        c[:, GNORM + 2 * l:GNORM + 2 * l + 2] = cols(a["gla_norm_2"][l])
        c[:, SINK + 6 * l:SINK + 6 * l + 6] = a["swa_sink_2"][l][None, :]
    c[:, N2FIN:N2FIN + 8] = cols(a["final_norm_2"])
    c[:, CVEC:CVEC + 8] = cols(a["c_2"][0])
    c[:, CVEC + 8:CVEC + 16] = cols(a["c_ctx_2"])
    c[:, IOTA:IOTA + 128] = i[None, :]
    c[:, ONORM:ONORM + 1] = a["dn_out_norm"][0][:, None]
    return c


def level_masks():
    i = np.arange(64)
    out = np.zeros((2, 64, 2, len(LEVELS), 64), np.float32)
    for n, b in enumerate(LEVELS):
        same = (i[:, None] // (2 * b)) == (i[None, :] // (2 * b))
        lower = same & ((i[:, None] // b) % 2 == 1) & ((i[None, :] // b) % 2 == 0)
        out[:, :, 0, n], out[:, :, 1, n] = lower, lower.T
    return out


def slabs(w):
    k, n = w.shape
    pad = -n % 128
    if pad:
        w = np.concatenate([w, np.zeros((k, pad), w.dtype)], axis=1)
    return np.ascontiguousarray(w.reshape(k // 128, 128, -1, 128).transpose(2, 1, 0, 3).reshape(-1, 128, k))


def feature_major(x):
    t, d = x.shape
    return np.ascontiguousarray(x.reshape(t, d // 128, 128).transpose(2, 1, 0))


def t5_bucket(rel):
    n = np.abs(rel)
    large = 8 + (np.log(np.maximum(n, 1) / 8) / np.log(1024 / 8) * 8).astype(np.int64)
    large = np.minimum(large, 15)
    return np.where(rel > 0, 16, 0) + np.where(n < 8, n, large)


def dilated_bias(rel_bias):
    l = np.arange(128)
    out = np.zeros((4, 4, 128, 768), np.float32)
    for r in range(4):
        q = (4 * l + r)[:, None]
        k0 = (4 * l[None, :] + np.arange(4)[:, None]).reshape(1, -1)
        k1 = (4 * l + r)[None, :]
        for g, (k, col) in enumerate(((k0, 0), (k1, 512), (k1, 640))):
            rel = k - q
            valid = (np.abs(rel) <= 64, np.abs(rel) <= 256, rel % 16 == 0)[g]
            b = t5_bucket(rel)
            for h in range(4):
                out[h, r, :, col:col + k.shape[1]] = np.where(valid, rel_bias[b, 4 * g + h], np.float32(NEG))
    return out


def constants2():
    c = np.zeros((128, NC2 + NC2C), np.float32)
    t = np.arange(T, dtype=np.int32)
    f32 = np.float32
    inv = (f32(10000.0) ** (-np.arange(16, dtype=f32) / f32(16))).astype(f32)
    ang = np.concatenate([(t // 64).astype(f32)[:, None] * inv, (t % 64).astype(f32)[:, None] * inv], axis=1)
    p = np.arange(128)
    c[:, COS:COS + T] = np.cos(ang).T[p % 32]
    c[:, SIN:SIN + T] = np.sin(ang).T[p % 32] * np.where(p % 64 < 32, -1.0, 1.0)[:, None]
    c[:, PERM:PERM + 128] = (p[:, None] ^ 32) == p[None, :]
    c[:, RSTF:RSTF + T] = t % 64 != 0
    c[:, RSTB:RSTB + T] = t % 64 != 63
    same = (p[:, None] // 64) == (p[None, :] // 64)
    c[:, ONESBD:ONESBD + 128] = same
    c[:, BMASK:BMASK + 128] = same
    c[:, NC2:NC2 + 256], c[:, NC2 + 256:NC2 + 512] = c[:, RSTF:RSTF + 256], c[:, RSTB:RSTB + 256]
    c[:, NC2 + 512:] = c[:, ONESBD:ONESBD + 256]
    return c


def tri_masks():
    p = np.arange(128)
    same = (p[:, None] // 64) == (p[None, :] // 64)
    out = np.zeros((128, 2, 128), np.float32)
    out[:, 0], out[:, 1] = same & (p[:, None] <= p[None, :]), same & (p[:, None] >= p[None, :])
    return out


def window_masks():
    q, k = np.arange(128)[:, None], np.arange(128)[None, :]
    left, right = np.where(k >= q, 0.0, NEG), np.where(k <= q, 0.0, NEG)
    z = np.zeros((128, 128))
    return np.concatenate([z, z, left, z, right, z, z], axis=1).astype(np.float32)


def grid_bias(rpb):
    out = np.zeros((2, 6, 4, 128, 256), np.float32)
    qr, qc = np.divmod(np.arange(128), 16)
    k = np.arange(256)
    kr, kc = 4 * (k // 128) + k % 4, (k % 128) // 4
    for b in range(4):
        col = kc + min(max(16 * b - 8, 0), 32)
        qcol = qc + 16 * b
        start = np.clip(qcol - 8, 0, 48)[:, None]
        valid = (col[None, :] >= start) & (col[None, :] < start + 16)
        dr = kr[None, :] - qr[:, None] + 7
        dc = np.clip(col[None, :] - qcol[:, None] + 15, 0, 30)
        out[:, :, b] = np.where(valid[None, None], rpb[:, :, dr, dc], np.float32(NEG))
    return out


def decay_weights(wf, wb):
    out = np.zeros((2, 128, 2, 256), np.float32)
    out[:, 0:16, 0], out[:, 16:32, 1] = wf, wb
    return out.reshape(2, 128, 512)


SWA_ORDER = np.concatenate([np.arange(64) + 64 * h for h in (0, 3, 1, 4, 2, 5)])


def in_slabs(w):
    w = np.concatenate([w[:, :1056], np.zeros((D, 96), w.dtype), w[:, 1056:2208], w[:, 2208 + SWA_ORDER], w[:, 2592:]],
                       axis=1)
    return slabs(w)


def out_slabs(w):
    w = w.reshape(2, 4, 128, 4, 2, 128).transpose(0, 3, 2, 4, 1, 5)
    return w.reshape(8, 128, 1024)


def down_slabs(w):
    w = w.reshape(2, HALF, 128, 8, 128).transpose(0, 3, 1, 2, 4).reshape(2, HALF, 8, 128, 128)
    return w.transpose(0, 1, 3, 2, 4).reshape(2 * HALF, 128, 1024)


def two(f, w):
    return np.ascontiguousarray(np.concatenate([f(w[0]), f(w[1])], axis=0))


def layout(a):
    w = a["w_in"][0]
    w = np.concatenate([w[:, :2048], w[:, 2048:2064], np.zeros((D, 112), w.dtype), w[:, 2064:]], axis=1)
    return {"consts": constants(a), "masks": np.concatenate([level_masks().reshape(128, -1), tri_masks().reshape(128, -1)], axis=1), "xT": feature_major(a["x"][0]), "w_in": slabs(w),
            "da_bias": dilated_bias(a["rel_bias"]),
            "w_br": np.concatenate([slabs(a["w_branch_dn"][0]), slabs(a["w_branch_da"][0])], axis=2),
            "w_out": slabs(a["w_out"][0]),
            "peer_wq": slabs(a["peer_wq"][0]),
            "peer_keys": np.ascontiguousarray(a["peer_sub_keys"][0].reshape(16, 128, 128).transpose(2, 0, 1)),
            "peer_u": np.ascontiguousarray(a["peer_u"][0].reshape(128, 128, 8, 128).transpose(1, 3, 2, 0)
                                           .reshape(128, 128, 1024)),
            "peer_v": np.ascontiguousarray(a["peer_v"][0].reshape(128, 16, 8, 8, 128).transpose(1, 3, 0, 2, 4)
                                           .reshape(128, 128, 1024)),
            "peer_u_rows": a["peer_u"][0],
            "peer_v_rows": a["peer_v"][0],
            "consts2": constants2(),
            "swa_mask": window_masks(),
            "na_bias": grid_bias(a["na_rpb_2"]),
            "wa2": decay_weights(a["gla_wa2_f_2"], a["gla_wa2_b_2"]),
            "ctxT": feature_major(a["ctx_2"][0]),
            "w_mod": np.ascontiguousarray(a["w_mod_2"].reshape(2, 8, 128, 3, 2, 1024).transpose(0, 3, 1, 4, 2, 5)
                                          .reshape(96, 128, 1024)),
            "w_in2": two(in_slabs, a["w_in_2"]),
            "w_out2": two(out_slabs, np.concatenate([a["w_out_2"][:, :640], a["w_out_2"][:, 640 + SWA_ORDER]], axis=1)),
            "w_gate2": two(slabs, a["w_gate_2"]),
            "w_up2": two(slabs, a["w_up_2"]),
            "w_down2": two(down_slabs, a["w_down_2"])}


def _build(nc, arrays):
    io = {n: nc.dram_tensor(n, v.shape, mybir.dt.from_np(v.dtype), kind="ExternalInput").ap() for n, v in arrays.items()}
    io["out"] = nc.dram_tensor("out_0_dram", (128, KC, T), F32, kind="ExternalOutput").ap()
    program(nc, io)


def kernel(**inputs):
    import concourse.bacc as _bacc
    from concourse.bass_utils import run_bass_kernel_spmd as _run

    arrays = layout({n: np.ascontiguousarray(v) for n, v in inputs.items()})
    nc = _bacc.Bacc("TRN2", target_bir_lowering=False, num_devices=1)
    _build(nc, arrays)
    r = _run(nc, [arrays], core_ids=[0])
    out = np.asarray(r.results[0]["out_0_dram"])
    return np.ascontiguousarray(out.transpose(2, 1, 0).reshape(1, T, D))
```
